# Optimizing a Trainium2 kernel written in Bass

```python
import math
import jax, jax.numpy as jnp
from jax import lax
import numpy as np

D_MODEL = 1024
BATCH = 1
SEQ = 1024
DEPTH = 1
DEC_BATCH = 8
DEC_SEQ = 4
PAST_LEN = 8192
PAGE_SIZE = 128

GLA_WIDTH = D_MODEL // 2
S5_WIDTH = D_MODEL - GLA_WIDTH
GLA_HEADS = 4
GLA_DV = GLA_WIDTH // GLA_HEADS
GLA_DK = GLA_DV // 2
GLA_RANK = 16
GLA_TAU = 16.0
GLA_CHUNK = 64
S5_GROUP_CH = 16
S5_GROUPS = S5_WIDTH // S5_GROUP_CH
S5_STATE = 64
PEER_KEYS = 128
PEER_EXPERTS = PEER_KEYS * PEER_KEYS
PEER_HEADS = 8
PEER_DQ = 256
PEER_TOPK = 16
PEER_BLOCK = 128
EPS = 1e-6

SPLIT_SIZES = (GLA_HEADS * GLA_DK, GLA_HEADS * GLA_DK, GLA_WIDTH, GLA_WIDTH, GLA_RANK, S5_WIDTH)
IN_COLS = sum(SPLIT_SIZES)
SPLIT_POINTS = tuple(int(v) for v in np.cumsum(SPLIT_SIZES)[:-1])

kernel_name = 'hymba_gla_s5_peer_step'

def rmsnorm(x, gain):
    xf = x.astype(jnp.float32)
    y = xf * lax.rsqrt(jnp.mean(xf * xf, axis=-1, keepdims=True) + EPS)
    return (y * gain.astype(jnp.float32)).astype(x.dtype)

def gla_mixer(q, k, v, log_a, s0):
    f32 = jnp.float32
    B, L, H, _ = q.shape
    C = math.gcd(L, GLA_CHUNK)
    n = L // C

    def to_chunks(t):
        return t.astype(f32).reshape(B, n, C, H, t.shape[-1]).transpose(1, 0, 3, 2, 4)

    qc, kc, vc, ac = map(to_chunks, (q * (GLA_DK ** -0.5), k, v, log_a))
    causal = jnp.tril(jnp.ones((C, C), dtype=bool))[:, :, None]

    def step(S, inp):
        qb, kb, vb, ab = inp
        b = jnp.cumsum(ab, axis=2)
        o_inter = jnp.einsum('bhcd,bhde->bhce', qb * jnp.exp(b), S)
        diff = b[:, :, :, None, :] - b[:, :, None, :, :]
        decay = jnp.exp(jnp.where(causal, diff, -jnp.inf))
        scores = jnp.einsum('bhid,bhijd,bhjd->bhij', qb, decay, kb)
        o = o_inter + jnp.einsum('bhij,bhje->bhie', scores, vb)
        b_last = b[:, :, -1:, :]
        S_new = jnp.exp(b_last[:, :, 0, :])[..., None] * S + jnp.einsum(
            'bhcd,bhce->bhde', kb * jnp.exp(b_last - b), vb)
        return S_new, o

    S_fin, o = lax.scan(step, s0.astype(f32), (qc, kc, vc, ac))
    o = o.transpose(1, 0, 3, 2, 4).reshape(B, L, H, vc.shape[-1])
    return o, S_fin

def s5_mixer(u, s_re, s_im, lam_re, lam_im, log_dt, b_re, b_im, c_re, c_im, d_skip):
    f32 = jnp.float32
    Bsz, L, _ = u.shape
    ug = u.astype(f32).reshape(Bsz, L, S5_GROUPS, S5_GROUP_CH)
    dt = jnp.exp(log_dt.astype(f32))[:, None]
    lr, li = lam_re.astype(f32), lam_im.astype(f32)
    mag = jnp.exp(lr * dt)
    ab_re, ab_im = mag * jnp.cos(li * dt), mag * jnp.sin(li * dt)
    den = lr * lr + li * li
    nr, ni = ab_re - 1.0, ab_im
    f_re = (nr * lr + ni * li) / den
    f_im = (ni * lr - nr * li) / den
    br, bi = b_re.astype(f32), b_im.astype(f32)
    bb_re = f_re[..., None] * br - f_im[..., None] * bi
    bb_im = f_re[..., None] * bi + f_im[..., None] * br
    bu_re = jnp.einsum('blgc,gpc->blgp', ug, bb_re)
    bu_im = jnp.einsum('blgc,gpc->blgp', ug, bb_im)
    sr, si = s_re.astype(f32), s_im.astype(f32)
    bu_re = bu_re.at[:, 0].add(ab_re * sr - ab_im * si)
    bu_im = bu_im.at[:, 0].add(ab_re * si + ab_im * sr)
    a_re = jnp.broadcast_to(ab_re, bu_re.shape)
    a_im = jnp.broadcast_to(ab_im, bu_im.shape)

    def combine(e1, e2):
        a1r, a1i, b1r, b1i = e1
        a2r, a2i, b2r, b2i = e2
        return (a1r * a2r - a1i * a2i,
                a1r * a2i + a1i * a2r,
                a2r * b1r - a2i * b1i + b2r,
                a2r * b1i + a2i * b1r + b2i)

    _, _, h_re, h_im = lax.associative_scan(combine, (a_re, a_im, bu_re, bu_im), axis=1)
    y = (jnp.einsum('blgp,gcp->blgc', h_re, c_re.astype(f32))
         - jnp.einsum('blgp,gcp->blgc', h_im, c_im.astype(f32)))
    y = y + d_skip.astype(f32).reshape(S5_GROUPS, S5_GROUP_CH) * ug
    return y.reshape(Bsz, L, S5_WIDTH), h_re[:, -1], h_im[:, -1]

def peer_ffn(h, w_query, sub_keys, expert_u, expert_v):
    f32 = jnp.float32
    Bsz, L, D = h.shape
    T = Bsz * L
    ht = h.reshape(T, D)
    q = (ht @ w_query).reshape(T, PEER_HEADS, 2, PEER_DQ // 2)
    s = jnp.einsum('thpd,hpnd->thpn', q, sub_keys).astype(f32)
    top_s, top_i = lax.top_k(s, PEER_TOPK)
    cand_s = top_s[:, :, 0, :, None] + top_s[:, :, 1, None, :]
    cand_i = top_i[:, :, 0, :, None] * PEER_KEYS + top_i[:, :, 1, None, :]
    cand_s = cand_s.reshape(T, PEER_HEADS, PEER_TOPK * PEER_TOPK)
    cand_i = cand_i.reshape(T, PEER_HEADS, PEER_TOPK * PEER_TOPK)
    fin_s, pos = lax.top_k(cand_s, PEER_TOPK)
    fin_i = jnp.take_along_axis(cand_i, pos, axis=-1)
    gate = jax.nn.softmax(fin_s, axis=-1)
    idx = fin_i.reshape(T, PEER_HEADS * PEER_TOPK)
    gate = gate.reshape(T, PEER_HEADS * PEER_TOPK).astype(h.dtype)
    pad = (-T) % PEER_BLOCK
    nb = (T + pad) // PEER_BLOCK
    xb = jnp.pad(ht, ((0, pad), (0, 0))).reshape(nb, PEER_BLOCK, D)
    ib = jnp.pad(idx, ((0, pad), (0, 0))).reshape(nb, PEER_BLOCK, -1)
    gb = jnp.pad(gate, ((0, pad), (0, 0))).reshape(nb, PEER_BLOCK, -1)

    def block(args):
        xk, ik, gk = args
        act = jax.nn.gelu(jnp.einsum('tkd,td->tk', expert_u[ik], xk))
        return jnp.einsum('tk,tkd->td', gk * act, expert_v[ik])

    out = lax.map(block, (xb, ib, gb))
    return out.reshape(nb * PEER_BLOCK, D)[:T].reshape(Bsz, L, D)

def decoder_layer(x, s_gla, s_re, s_im, norm1, w_in, w_a2, b_a2, gla_norm,
                  lam_re, lam_im, log_dt, b_re, b_im, c_re, c_im, d_skip,
                  w_glu, b_glu, w_out, norm2, peer_wq, peer_keys, peer_u, peer_v):
    Bsz, L, _ = x.shape
    h = rmsnorm(x, norm1)
    proj = h @ w_in
    q, k, v, g, a_lr, u = jnp.split(proj, SPLIT_POINTS, axis=-1)
    log_a = jax.nn.log_sigmoid((a_lr @ w_a2 + b_a2).astype(jnp.float32)) / GLA_TAU
    q = q.reshape(Bsz, L, GLA_HEADS, GLA_DK)
    k = k.reshape(Bsz, L, GLA_HEADS, GLA_DK)
    v = v.reshape(Bsz, L, GLA_HEADS, GLA_DV)
    log_a = log_a.reshape(Bsz, L, GLA_HEADS, GLA_DK)
    o_gla, s_gla_new = gla_mixer(q, k, v, log_a, s_gla)
    o_gla = rmsnorm(o_gla.astype(x.dtype), gla_norm).reshape(Bsz, L, GLA_WIDTH) * jax.nn.silu(g)
    y_s5, sre_new, sim_new = s5_mixer(u, s_re, s_im, lam_re, lam_im, log_dt,
                                      b_re, b_im, c_re, c_im, d_skip)
    z = jax.nn.gelu(y_s5.astype(x.dtype))
    o_s5 = z * jax.nn.sigmoid(z @ w_glu + b_glu)
    x = x + jnp.concatenate([o_gla, o_s5], axis=-1) @ w_out
    x = x + peer_ffn(rmsnorm(x, norm2), peer_wq, peer_keys, peer_u, peer_v)
    return (x, s_gla_new.astype(s_gla.dtype), sre_new.astype(s_re.dtype), sim_new.astype(s_im.dtype))

def setup_inputs(seed: int = 0) -> dict:
    key = jax.random.key(seed)
    ks = iter(jax.random.split(key, 40))
    f32 = jnp.float32

    def nrm(shape, scale):
        return scale * jax.random.normal(next(ks), shape, f32)

    Ld = DEPTH
    n_idx = jnp.arange(S5_STATE, dtype=f32)
    return {
        'x_prompt': nrm((BATCH, SEQ, D_MODEL), 1.0),
        'x_sample': nrm((DEC_BATCH, DEC_SEQ, D_MODEL), 1.0),
        'state_gla': nrm((Ld, DEC_BATCH, GLA_HEADS, GLA_DK, GLA_DV), 4.0),
        'state_s5_re': nrm((Ld, DEC_BATCH, S5_GROUPS, S5_STATE), 1.0),
        'state_s5_im': nrm((Ld, DEC_BATCH, S5_GROUPS, S5_STATE), 1.0),
        'norm1': 1.0 + nrm((Ld, D_MODEL), 0.02),
        'w_in': nrm((Ld, D_MODEL, IN_COLS), D_MODEL ** -0.5),
        'w_a2': nrm((Ld, GLA_RANK, GLA_HEADS * GLA_DK), GLA_RANK ** -0.5),
        'b_a2': 2.0 + nrm((Ld, GLA_HEADS * GLA_DK), 0.1),
        'gla_norm': 1.0 + nrm((Ld, GLA_HEADS, GLA_DV), 0.02),
        's5_lam_re': -0.5 + nrm((Ld, S5_GROUPS, S5_STATE), 0.01),
        's5_lam_im': math.pi * n_idx + nrm((Ld, S5_GROUPS, S5_STATE), 0.01),
        's5_log_dt': jax.random.uniform(next(ks), (Ld, S5_GROUPS), f32, math.log(1e-3), math.log(1e-1)),
        's5_b_re': nrm((Ld, S5_GROUPS, S5_STATE, S5_GROUP_CH), (2 * S5_GROUP_CH) ** -0.5),
        's5_b_im': nrm((Ld, S5_GROUPS, S5_STATE, S5_GROUP_CH), (2 * S5_GROUP_CH) ** -0.5),
        's5_c_re': nrm((Ld, S5_GROUPS, S5_GROUP_CH, S5_STATE), (2 * S5_STATE) ** -0.5),
        's5_c_im': nrm((Ld, S5_GROUPS, S5_GROUP_CH, S5_STATE), (2 * S5_STATE) ** -0.5),
        's5_d': nrm((Ld, S5_WIDTH), 1.0),
        'w_glu': nrm((Ld, S5_WIDTH, S5_WIDTH), S5_WIDTH ** -0.5),
        'b_glu': nrm((Ld, S5_WIDTH), 0.02),
        'w_out': nrm((Ld, D_MODEL, D_MODEL), D_MODEL ** -0.5),
        'norm2': 1.0 + nrm((Ld, D_MODEL), 0.02),
        'peer_wq': nrm((Ld, D_MODEL, PEER_HEADS * PEER_DQ), D_MODEL ** -0.5),
        'peer_keys': nrm((Ld, PEER_HEADS, 2, PEER_KEYS, PEER_DQ // 2), (PEER_DQ // 2) ** -0.5),
        'peer_u': nrm((Ld, PEER_EXPERTS, D_MODEL), D_MODEL ** -0.5),
        'peer_v': nrm((Ld, PEER_EXPERTS, D_MODEL), PEER_HEADS ** -0.5),
        'final_norm': 1.0 + nrm((D_MODEL,), 0.02),
    }

def reference(x_prompt, x_sample, state_gla, state_s5_re, state_s5_im, norm1, w_in, w_a2, b_a2,
              gla_norm, s5_lam_re, s5_lam_im, s5_log_dt, s5_b_re, s5_b_im, s5_c_re, s5_c_im, s5_d,
              w_glu, b_glu, w_out, norm2, peer_wq, peer_keys, peer_u, peer_v, final_norm):
    xp, xs = x_prompt, x_sample
    gp, rp, ip, gs, rs, is_ = [], [], [], [], [], []
    for l in range(DEPTH):
        params = (norm1[l], w_in[l], w_a2[l], b_a2[l], gla_norm[l], s5_lam_re[l], s5_lam_im[l],
                  s5_log_dt[l], s5_b_re[l], s5_b_im[l], s5_c_re[l], s5_c_im[l], s5_d[l],
                  w_glu[l], b_glu[l], w_out[l], norm2[l], peer_wq[l], peer_keys[l], peer_u[l], peer_v[l])
        zg = jnp.zeros((xp.shape[0], GLA_HEADS, GLA_DK, GLA_DV), xp.dtype)
        zs = jnp.zeros((xp.shape[0], S5_GROUPS, S5_STATE), xp.dtype)
        xp, g_new, r_new, i_new = decoder_layer(xp, zg, zs, zs, *params)
        gp.append(g_new); rp.append(r_new); ip.append(i_new)
        xs, g_new, r_new, i_new = decoder_layer(xs, state_gla[l], state_s5_re[l], state_s5_im[l], *params)
        gs.append(g_new); rs.append(r_new); is_.append(i_new)
    y_prompt = rmsnorm(xp, final_norm)
    y_sample = rmsnorm(xs, final_norm)
    return (y_prompt, y_sample, jnp.stack(gp), jnp.stack(rp), jnp.stack(ip),
            jnp.stack(gs), jnp.stack(rs), jnp.stack(is_))


_drawn_inputs = setup_inputs


def setup_inputs(seed=0):
    import zlib

    import numpy as np

    out = dict(_drawn_inputs(seed))
    spreads = {}
    factors = {'gla_norm': 9.349,
     's5_lam_re': 47.456,
     'b_glu': 73.714,
     'final_norm': 21.918,
     'norm2': 11.021}
    for name, (base, spread) in spreads.items():
        noise = np.random.default_rng([zlib.crc32(name.encode()), seed]).standard_normal(out[name].shape)
        drawn = base * np.exp(spread * noise) if base else spread * noise
        out[name] = __import__('jax').numpy.asarray(drawn.astype(out[name].dtype))
    for name, factor in factors.items():
        out[name] = (out[name] * factor).astype(out[name].dtype)
    return out
```

```python
from contextlib import ExitStack

import concourse.bass as bass
from concourse import mybir

ALU = mybir.AluOpType
ACT = mybir.ActivationFunctionType
AX = mybir.AxisListType
F32 = mybir.dt.float32
F32R = mybir.dt.float32r
I32 = mybir.dt.int32
U32 = mybir.dt.uint32

P = 128
D = 1024
KD = D // P
SEQ = 1024
NSEQ, SLEN = 8, 4
TS = NSEQ * SLEN
T = SEQ + TS
NTP = SEQ // P
NT = NTP + 1
NW = T // 3
H, DK, DV = 4, 64, 128
GC = 64
RANK = 16
TAU = 16.0
G, GCH, ST = 32, 16, 64
GP = G // 2
SC = 8
NM = SEQ // SC
NMS = NM + NSEQ
W4 = 512
EPS = 1e-6
NK = 128
PH = 8
TOPK = 16
NE = NK * NK
NSEL = PH * TOPK
QC, KC, VC, GTC, AC, UC = 0, 256, 512, 1024, 1536, 1552


def rows(t):
    return P if t < NTP else TS


LIVE_SEMS = []


def new_sem(nc, name):
    LIVE_SEMS.append(nc.alloc_semaphore(name))
    return LIVE_SEMS[-1]


def clear_sems(nc):
    nc.clear_and_free_semaphores(LIVE_SEMS)
    LIVE_SEMS.clear()
    nc.all_engine_barrier()


class Count:

    def __init__(self, sem):
        self.sem, self.n = sem, 0

    def up(self, k=1):
        self.n += k
        return self.n


def norm_transpose(nc, tag, tiles, gain, h_t):
    with ExitStack() as ctx:
        def sb(name, shape, dt=F32):
            return ctx.enter_context(nc.sbuf_tensor(tag + name, shape, dt))

        def sem(name):
            return new_sem(nc, tag + name)

        x_sb = [sb(f"x{b}", [P, D]) for b in range(2)]
        hn_sb = [sb(f"hn{b}", [P, D]) for b in range(2)]
        sq = sb("sq", [P, D])
        ss = sb("ss", [P, NT])
        rinv = sb("rinv", [P, NT])
        rstd = sb("rstd", [P, NT])
        gain_sb = sb("gain", [P, KD])
        grow = sb("grow", [KD, P])
        ident = sb("ident", [P, P])
        tp = [ctx.enter_context(nc.psum_tensor(f"{tag}tp{b}", [P, KD // 2, P], F32)) for b in range(4)]
        tg = ctx.enter_context(nc.psum_tensor(f"{tag}tg", [P, KD], F32))
        x_loaded = [sem(f"x_loaded{b}") for b in range(2)]
        gain_loaded = sem("gain_loaded")
        ident_zero, ident_ready = sem("ident_zero"), sem("ident_ready")
        gain_turned, gain_ready = sem("gain_turned"), sem("gain_ready")
        sums, means, stds, normed = sem("sums"), sem("means"), sem("stds"), sem("normed")
        minv = sem("minv")
        turned, stored = sem("turned"), sem("stored")
        block = ctx.enter_context(nc.Block())

        @block.sync
        def _(sp):
            sp.dma_start(grow[:], gain.rearrange("(k p) -> k p", p=P)).then_inc(gain_loaded, 16)
            for t in range(NT):
                if t >= 2:
                    sp.wait_ge(normed, t - 1)
                sp.dma_start(x_sb[t % 2][0:rows(t), :], tiles[t]).then_inc(x_loaded[t % 2], 16)

        @block.gpsimd
        def _(pool):
            nc.gpsimd.memset(ident[:], 0.0).then_inc(ident_zero, 1)
            pool.wait_ge(ident_zero, 1)
            nc.gpsimd.affine_select(out=ident[:], in_=ident[:], compare_op=ALU.not_equal, fill=1.0, base=0,
                                    pattern=[[-1, P]], channel_multiplier=1).then_inc(ident_ready, 1)

        @block.scalar
        def _(act):
            for t in range(NT):
                r = rows(t)
                act.wait_ge(x_loaded[t % 2], 16 * (t // 2 + 1))
                if t >= 1:
                    act.wait_ge(sums, t)
                nc.scalar.activation(sq[0:r], x_sb[t % 2][0:r], ACT.Square,
                                     accum_out=ss[0:r, t:t + 1]).then_inc(sums, 1)
                act.wait_ge(means, t + 1)
                nc.scalar.activation(rstd[0:r, t:t + 1], rinv[0:r, t:t + 1], ACT.Sqrt).then_inc(stds, 1)
                act.wait_ge(stds, t + 1)
                if t >= 2:
                    act.wait_ge(turned, 2 * (t - 1))
                nc.scalar.activation(hn_sb[t % 2][0:r], x_sb[t % 2][0:r], ACT.Copy,
                                     scale=rstd[0:r, t:t + 1]).then_inc(normed, 1)

        @block.tensor
        def _(pe):
            pe.wait_ge(ident_ready, 1)
            pe.wait_ge(gain_loaded, 16)
            nc.tensor.transpose(tg[:], grow[:], ident[0:KD, 0:KD]).then_inc(gain_turned, 1)
            for t in range(NT):
                r = rows(t)
                pe.wait_ge(normed, t + 1)
                for half in range(2):
                    if t >= 2:
                        pe.wait_ge(stored, 2 * (t - 2) + half + 1)
                    for k in range(KD // 2):
                        c = (half * (KD // 2) + k) * P
                        mm = nc.tensor.transpose(tp[2 * (t % 2) + half][:, k, 0:r],
                                                 hn_sb[t % 2][0:r, c:c + P], ident[0:r, 0:r])
                    mm.then_inc(turned, 1)

        @block.vector
        def _(dve):
            dve.wait_ge(gain_turned, 1)
            nc.vector.tensor_copy(gain_sb[:], tg[:]).then_inc(gain_ready, 1)

            def mean(t):
                r = rows(t)
                dve.wait_ge(sums, t + 1)
                nc.vector.tensor_scalar(ss[0:r, t:t + 1], ss[0:r, t:t + 1], 1.0 / D, EPS,
                                        ALU.mult, ALU.add).then_inc(minv, 1)
                dve.wait_ge(minv, t + 1)
                nc.vector.reciprocal(rinv[0:r, t:t + 1], ss[0:r, t:t + 1]).then_inc(means, 1)

            mean(0)
            dve.wait_ge(gain_ready, 1)
            for t in range(NT):
                r = rows(t)
                if t + 1 < NT:
                    mean(t + 1)
                for half in range(2):
                    dve.wait_ge(turned, 2 * t + half + 1)
                    k0 = half * (KD // 2)
                    nc.vector.tensor_tensor(
                        h_t[:, k0:k0 + KD // 2, t * P:t * P + r], tp[2 * (t % 2) + half][:, :, 0:r],
                        gain_sb[:, k0:k0 + KD // 2].unsqueeze(2).broadcast_to([P, KD // 2, r]),
                        ALU.mult).then_inc(stored, 1)


def project(nc, w_in, w_a2, b_a2, h_t, qk_t, la_t, v_sb, g_sb, u_sb, us_nat):
    with ExitStack() as ctx:
        def sem(name):
            return new_sem(nc, "pj_" + name)

        WB = RANK + W4
        wbuf = [ctx.enter_context(nc.sbuf_tensor(f"pj_w{b}", [P, KD, WB], F32)) for b in range(2)]
        alr_t = ctx.enter_context(nc.sbuf_tensor("pj_alr", [RANK, T], F32))
        wa2 = ctx.enter_context(nc.sbuf_tensor("pj_wa2", [RANK, H * DK], F32))
        ba2 = ctx.enter_context(nc.sbuf_tensor("pj_ba2", [P, 2], F32))
        pd = [ctx.enter_context(nc.psum_tensor(f"pj_pd{b}", [P, W4], F32)) for b in range(4)]
        pa = [ctx.enter_context(nc.psum_tensor(f"pj_pa{b}", [P, W4], F32)) for b in range(4)]
        w_loaded = [sem(f"w_loaded{b}") for b in range(2)]
        small_loaded = sem("small_loaded")
        d_done, a_done = sem("d_done"), sem("a_done")
        d_read, a_read = sem("d_read"), sem("a_read")
        block = ctx.enter_context(nc.Block())
        w_dram = w_in.rearrange("(k p) c -> p k c", p=P)
        cols = [(QC, W4), (VC, W4), (GTC, W4), (AC, RANK + W4)]

        @block.sync
        def _(sp):
            sp.dma_start(wa2[:], w_a2).then_inc(small_loaded, 16)
            sp.dma_start(ba2[:], b_a2.rearrange("(c p) -> p c", p=P)).then_inc(small_loaded, 16)
            for b, (c, n) in enumerate(cols):
                if b == 2:
                    sp.wait_ge(d_done, 4 * 3)
                if b == 3:
                    sp.wait_ge(d_done, 4 * 3 + NT)
                sp.dma_start(wbuf[b % 2][:, :, 0:n], w_dram[:, :, c:c + n]).then_inc(w_loaded[b % 2], 16)

        @block.tensor
        def _(pe):
            nd, na = 0, 0

            def transposed(out, w, c, m, n):
                for k in range(KD):
                    mm = nc.tensor.matmul(out, w[:, k, c:c + m], h_t[:, k, n * NW:(n + 1) * NW],
                                          start=(k == 0), stop=(k == KD - 1))
                return mm

            def natural(out, w, c, tok):
                for k in range(KD):
                    mm = nc.tensor.matmul(out, h_t[:, k, tok], w[:, k, c:c + W4],
                                          start=(k == 0), stop=(k == KD - 1))
                return mm

            pe.wait_ge(w_loaded[0], 16)
            for c in range(4):
                for n in range(3):
                    if nd >= 4:
                        pe.wait_ge(d_read, nd - 3)
                    mm = transposed(pd[nd % 4][:, 0:NW], wbuf[0], c * P, P, n)
                    mm.then_inc(d_done, 1)
                    nd += 1
            for b in (1, 2):
                pe.wait_ge(w_loaded[b % 2], 16 * (b // 2 + 1))
                for t in range(NT):
                    out = (pd[nd % 4] if b == 1 else pa[na % 4])
                    if b == 1 and nd >= 4:
                        pe.wait_ge(d_read, nd - 3)
                    if b == 2 and na >= 4:
                        pe.wait_ge(a_read, na - 3)
                    mm = natural(out[0:rows(t), :], wbuf[b % 2], 0, slice(t * P, t * P + rows(t)))
                    if b == 1:
                        mm.then_inc(d_done, 1)
                        nd += 1
                    else:
                        mm.then_inc(a_done, 1)
                        na += 1
            pe.wait_ge(w_loaded[1], 32)
            for n in range(3):
                pe.wait_ge(d_read, nd - 3)
                mm = transposed(pd[nd % 4][0:RANK, 0:NW], wbuf[1], 0, RANK, n)
                mm.then_inc(d_done, 1)
                nd += 1
            for r in range(SC):
                pe.wait_ge(a_read, na - 3)
                mm = natural(pa[na % 4][:, :], wbuf[1], RANK, slice(r, SEQ, SC))
                mm.then_inc(a_done, 1)
                na += 1
            pe.wait_ge(a_read, na - 3)
            mm = natural(pa[na % 4][0:TS, :], wbuf[1], RANK, slice(SEQ, T))
            mm.then_inc(a_done, 1)
            na += 1
            pe.wait_ge(small_loaded, 32)
            pe.wait_ge(d_read, nd)
            for c in range(2):
                for n in range(3):
                    if nd >= 4:
                        pe.wait_ge(d_read, nd - 3)
                    nc.tensor.matmul(pd[nd % 4][:, 0:NW], wa2[:, c * P:(c + 1) * P], alr_t[:, n * NW:(n + 1) * NW],
                                     start=True, stop=True).then_inc(d_done, 1)
                    nd += 1

        @block.vector
        def _(dve):
            nd = 0
            for c in range(4):
                for n in range(3):
                    dve.wait_ge(d_done, nd + 1)
                    nc.vector.tensor_copy(qk_t[:, c, n * NW:(n + 1) * NW], pd[nd % 4][:, 0:NW]).then_inc(d_read, 1)
                    nd += 1
            for t in range(NT):
                dve.wait_ge(d_done, nd + 1)
                nc.vector.tensor_copy(v_sb[0:rows(t), t, :], pd[nd % 4][0:rows(t), :]).then_inc(d_read, 1)
                nd += 1
            for n in range(3):
                dve.wait_ge(d_done, nd + 1)
                nc.vector.tensor_copy(alr_t[:, n * NW:(n + 1) * NW], pd[nd % 4][0:RANK, 0:NW]).then_inc(d_read, 1)
                nd += 1
            dve.wait_ge(small_loaded, 32)
            for c in range(2):
                for n in range(3):
                    dve.wait_ge(d_done, nd + 1)
                    nc.vector.tensor_scalar(la_t[:, c, n * NW:(n + 1) * NW], pd[nd % 4][:, 0:NW],
                                            ba2[:, c:c + 1], None, ALU.add).then_inc(d_read, 1)
                    nd += 1

        @block.scalar
        def _(act):
            na = 0
            for t in range(NT):
                act.wait_ge(a_done, na + 1)
                nc.scalar.activation(g_sb[0:rows(t), t, :], pa[na % 4][0:rows(t), :], ACT.Silu).then_inc(a_read, 1)
                na += 1
            for r in range(SC):
                act.wait_ge(a_done, na + 1)
                nc.scalar.activation(u_sb[:, :, r, :], pa[na % 4][:, :].rearrange("p (g c) -> p g c", g=G), ACT.Copy).then_inc(a_read, 1)
                na += 1
            act.wait_ge(a_done, na + 1)
            nc.scalar.activation(us_nat[:, :], pa[na % 4][0:TS, :], ACT.Copy).then_inc(a_read, 1)


def gla_decays(nc, qk_t, la_t, qz, fac, fac_s):
    with ExitStack() as ctx:
        def sb(name, shape, dt=F32):
            return ctx.enter_context(nc.sbuf_tensor("gd_" + name, shape, dt))

        def sem(name):
            return new_sem(nc, "gd_" + name)

        t1 = sb("t1", [P, 2, T])
        t2 = sb("t2", [P, 2, T])
        eq = sb("eq", [P, 2, T])
        ek = sb("ek", [P, 2, T])
        keep = sb("keep", [P, T])
        df = sb("df", [P, 2, 2, NTP * 2])
        step = sem("step")
        absd, exped, logged = sem("absd"), sem("exped"), sem("logged")
        diffed, factored = sem("diffed"), sem("factored")
        block = ctx.enter_context(nc.Block())
        NCH = SEQ // GC

        @block.vector
        def _(dve):
            s = Count(step)
            for h in range(H):
                other = slice(DK * (1 - h % 2), DK * (1 - h % 2) + DK)
                nc.vector.memset(qz[other, h, :], 0.0)
            nc.vector.memset(keep[:], 1.0).then_inc(step, 1)
            dve.wait_ge(step, s.up())
            nc.vector.memset(keep[:, 0:SEQ:GC], 0.0).then_inc(step, 1)
            nc.vector.memset(keep[:, SEQ:T:SLEN], 0.0).then_inc(step, 1)
            dve.wait_ge(absd, 1)
            nc.vector.tensor_scalar(la_t[:], la_t[:], 0.0, None, ALU.min).then_inc(step, 1)
            dve.wait_ge(logged, 1)
            dve.wait_ge(step, s.up(3))
            nc.vector.tensor_tensor(la_t[:], la_t[:], t2[:], ALU.subtract).then_inc(step, 1)
            dve.wait_ge(step, s.up())
            for c in range(2):
                nc.vector.tensor_tensor_scan(t1[:, c, :], keep[:], la_t[:, c, :], 0.0, ALU.mult, ALU.add).then_inc(step, 1)
            dve.wait_ge(step, s.up(2))
            for c in range(2):
                b = t1[:, c, 0:SEQ].rearrange("p (n s) -> p n s", s=GC)
                mid = b[:, :, GC // 2 - 1:GC // 2]
                end = b[:, :, GC - 1:GC]
                nc.vector.tensor_tensor(t2[:, c, 0:SEQ].rearrange("p (n s) -> p n s", s=GC), b,
                                        mid.broadcast_to([P, NCH, GC]), ALU.subtract).then_inc(diffed, 1)
                nc.vector.tensor_copy(t2[:, c, SEQ:T], t1[:, c, SEQ:T]).then_inc(diffed, 1)
                nc.vector.tensor_copy(df[:, 0, c, :].unsqueeze(2), mid).then_inc(diffed, 1)
                nc.vector.tensor_tensor(df[:, 1, c, :].unsqueeze(2), end, mid, ALU.subtract).then_inc(diffed, 1)
            dve.wait_ge(factored, 2)
            for h in range(H):
                own = slice(DK * (h % 2), DK * (h % 2) + DK)
                nc.vector.scalar_tensor_tensor(out=qz[own, h, :], in0=qk_t[own, h // 2, :], scalar=DK ** -0.5,
                                               in1=eq[own, h // 2, :], op0=ALU.mult, op1=ALU.mult)
            nc.vector.tensor_tensor(qk_t[:, 2:4, :], qk_t[:, 2:4, :], ek[:], ALU.mult)

        @block.scalar
        def _(act):
            nc.scalar.activation(t1[:], la_t[:], ACT.Abs).then_inc(absd, 1)
            act.wait_ge(absd, 1)
            nc.scalar.activation(t1[:], t1[:], ACT.Exp, scale=-1.0).then_inc(exped, 1)
            act.wait_ge(exped, 1)
            nc.scalar.activation(t2[:], t1[:], ACT.Ln, bias=1.0).then_inc(logged, 1)
            act.wait_ge(diffed, 8)
            nc.scalar.activation(eq[:], t2[:], ACT.Exp, scale=1.0 / TAU).then_inc(factored, 1)
            nc.scalar.activation(ek[:], t2[:], ACT.Exp, scale=-1.0 / TAU).then_inc(factored, 1)
            nc.scalar.activation(fac[:, 0:2], df[:], ACT.Exp, scale=1.0 / TAU)
            nc.scalar.activation(fac[:, 2], t1[:, :, GC - 1:SEQ:GC], ACT.Exp, scale=1.0 / TAU)
            nc.scalar.activation(fac_s[:], t1[:, :, SEQ + SLEN - 1:T:SLEN], ACT.Exp, scale=1.0 / TAU)


def gla(nc, qk_t, qz, v_sb, g_sb, fac, fac_s, gla_norm, state_in, state_prompt, state_sample, o_t):
    with ExitStack() as ctx:
        def sb(name, shape, dt=F32):
            return ctx.enter_context(nc.sbuf_tensor("gl_" + name, shape, dt))

        def ps(name, shape):
            return ctx.enter_context(nc.psum_tensor("gl_" + name, shape, F32))

        def sem(name):
            return new_sem(nc, "gl_" + name)

        ident = sb("ident", [P, P])
        mask = sb("mask", [P, P])
        mask_s = sb("mask_s", [TS, TS])
        seq_col = sb("seq_col", [P, NSEQ, TS])
        seq_row = sb("seq_row", [TS, NSEQ])
        gn = sb("gn", [H, P])
        gain = sb("gain", [P, H])
        k_nat = [sb(f"k_nat{b}", [P, 2, 2, P]) for b in range(2)]
        prob = [sb(f"prob{b}", [P, H, P]) for b in range(2)]
        S = sb("S", [P, 2, DV])
        Sm = [sb(f"Sm{b}", [P, 2, DV]) for b in range(2)]
        kvf = sb("kvf", [P, 2, DV])
        sq = sb("sq", [P, H, DV])
        ssum = sb("ssum", [P, H])
        rinv = sb("rinv", [P, H])
        rstd = sb("rstd", [P, H])
        on = [sb(f"on{b}", [P, H, DV]) for b in range(2)]
        Ss = sb("Ss", [P, 2, NSEQ, DV])
        qs = sb("qs", [P, H, NSEQ, TS])
        vs = sb("vs", [TS, NSEQ, H, DV])
        kp_bank = ps("kp", [P, 4, P])
        kp = kp_bank[:, 0:2, :]
        sp_ = [ps(f"sp{b}", [P, H, P]) for b in range(2)]
        kvp = ps("kvp", [P, 2, 2, DV])
        op = [ps(f"op{b}", [P, H, DV]) for b in range(2)]
        kvs = ps("kvs", [P, 2, W4])
        states_loaded, gn_loaded = sem("states_loaded"), sem("gn_loaded")
        zeroed, shaped = sem("zeroed"), sem("shaped")
        gain_turned = sem("gain_turned")
        k_turned, k_stored = sem("k_turned"), sem("k_stored")
        scored, masked = sem("scored"), sem("masked")
        kv_done, kv_read = sem("kv_done"), sem("kv_read")
        decayed, step, local = sem("decayed"), sem("step"), sem("local")
        o_done, squared, stded, o_normed = sem("o_done"), sem("squared"), sem("stded"), sem("o_normed")
        o_turned, o_stored = sem("o_turned"), sem("o_stored")
        s_ready, q_split, v_split, s_written = sem("s_ready"), sem("q_split"), sem("v_split"), sem("s_written")
        kvs_done, sample_ready = sem("kvs_done"), sem("sample_ready")
        block = ctx.enter_context(nc.Block())

        @block.sync
        def _(sp):
            sp.dma_start(gn[:], gla_norm).then_inc(gn_loaded, 16)
            for h in range(H):
                sp.dma_start(Ss[DK * (h % 2):DK * (h % 2) + DK, h // 2],
                             state_in[:, h].rearrange("s d e -> d s e")).then_inc(states_loaded, 16)
            sp.wait_ge(s_ready, SEQ // GC)
            for h in range(H):
                sp.dma_start(state_prompt[h], S[DK * (h % 2):DK * (h % 2) + DK, h // 2, :]).then_inc(s_written, 16)
            sp.wait_ge(sample_ready, 2)
            for h in range(H):
                sp.dma_start(state_sample[:, h].rearrange("s d e -> d s e"),
                             Ss[DK * (h % 2):DK * (h % 2) + DK, h // 2]).then_inc(s_written, 16)
            sp.wait_ge(s_written, 16 * 2 * H)

        @block.gpsimd
        def _(pool):
            nc.gpsimd.memset(ident[:], 0.0).then_inc(zeroed, 1)
            nc.gpsimd.memset(mask[:], 1.0).then_inc(zeroed, 1)
            nc.gpsimd.memset(mask_s[:], 1.0).then_inc(zeroed, 1)
            nc.gpsimd.memset(seq_col[:], 1.0).then_inc(zeroed, 1)
            nc.gpsimd.memset(seq_row[:], 1.0).then_inc(zeroed, 1)
            pool.wait_ge(zeroed, 5)
            s = 0

            def select(ap, op, fill, base, pattern, mul):
                return nc.gpsimd.affine_select(out=ap, in_=ap, compare_op=op, fill=fill, base=base,
                                               pattern=pattern, channel_multiplier=mul)

            select(ident[:], ALU.not_equal, 1.0, 0, [[-1, P]], 1).then_inc(shaped, 1)
            select(mask[:], ALU.is_ge, 0.0, 0, [[1, P]], -1).then_inc(shaped, 1)
            select(mask_s[:], ALU.is_ge, 0.0, 0, [[1, TS]], -1).then_inc(shaped, 1)
            sc = seq_col[:]
            select(sc, ALU.is_ge, 0.0, 0, [[-SLEN, NSEQ], [1, TS]], 0).then_inc(shaped, 1)
            select(seq_row[:], ALU.is_ge, 0.0, 0, [[-SLEN, NSEQ]], 1).then_inc(shaped, 1)
            pool.wait_ge(shaped, 5)
            select(mask[:, GC:P], ALU.is_ge, 0.0, -GC, [[0, GC]], 1).then_inc(shaped, 1)
            select(mask_s[:].rearrange("p (s j) -> p s j", j=SLEN), ALU.is_ge, 0.0, 0,
                   [[-SLEN, NSEQ], [0, SLEN]], 1).then_inc(shaped, 1)
            select(sc, ALU.is_ge, 0.0, SLEN - 1, [[SLEN, NSEQ], [-1, TS]], 0).then_inc(shaped, 1)
            select(seq_row[:], ALU.is_ge, 0.0, SLEN - 1, [[SLEN, NSEQ]], -1).then_inc(shaped, 1)

        def half(h):
            return slice(DK * (h % 2), DK * (h % 2) + DK)

        @block.tensor
        def _(pe):
            pe.wait_ge(shaped, 9)
            pe.wait_ge(gn_loaded, 16)
            nc.tensor.transpose(sp_[0][:, 0, 0:H], gn[:], ident[0:H, 0:H]).then_inc(gain_turned, 1)

            def turn_out(t):
                r = rows(t)
                pe.wait_ge(o_normed, t + 1)
                for h in range(H):
                    mm = nc.tensor.transpose(sp_[(t + 1) % 2][:, h, 0:r], on[t % 2][0:r, h, :], ident[0:r, 0:r])
                mm.then_inc(o_turned, 1)

            for t in range(NT):
                r = rows(t)
                tok = slice(t * P, t * P + r)
                if t >= 1:
                    pe.wait_ge(k_stored, t)
                for c in range(2):
                    mm = nc.tensor.transpose(kp[0:r, c, :], qk_t[:, 2 + c, tok], ident[:])
                mm.then_inc(k_turned, 1)
                if t == 0:
                    pe.wait_ge(masked, 1)
                if t >= 3:
                    pe.wait_ge(o_stored, t - 2)
                for h in range(H):
                    mm = nc.tensor.matmul(sp_[t % 2][0:r, h, 0:r], qk_t[:, 2 + h // 2, tok], qz[:, h, tok],
                                          start=True, stop=True)
                mm.then_inc(scored, 1)
                pe.wait_ge(k_stored, t + 1)
                if t < NTP:
                    if t >= 1:
                        pe.wait_ge(kv_read, 2 * t)
                    for c in range(2):
                        for h in range(H):
                            mm = nc.tensor.matmul(kvp[half(h), c, h // 2, :],
                                                  k_nat[t % 2][:, c, h // 2, half(h)],
                                                  v_sb[:, t, h * DV:(h + 1) * DV],
                                                  start=True, stop=True, skip_group_check=True)
                    mm.then_inc(kv_done, 1)
                pe.wait_ge(masked, t + 2)
                if t >= 2:
                    pe.wait_ge(o_normed, t - 1)
                if t < NTP:
                    pe.wait_ge(decayed, 2 * t + 2)
                    for h in range(H):
                        nc.tensor.matmul(op[t % 2][:, h, :], prob[t % 2][:, h, :], v_sb[:, t, h * DV:(h + 1) * DV],
                                         start=True, stop=False, skip_group_check=True)
                        for c in range(2):
                            mm = nc.tensor.matmul(op[t % 2][c * GC:(c + 1) * GC, h, :],
                                                  qz[:, h, t * P + c * GC:t * P + (c + 1) * GC],
                                                  Sm[c][:, h // 2, :], start=False, stop=True,
                                                  skip_group_check=True)
                    mm.then_inc(o_done, 1)
                else:
                    pe.wait_ge(q_split, 1)
                    pe.wait_ge(states_loaded, 16 * H)
                    for h in range(H):
                        nc.tensor.matmul(op[t % 2][0:r, h, :], prob[t % 2][0:r, h, 0:r],
                                         v_sb[0:r, t, h * DV:(h + 1) * DV], start=True, stop=False,
                                         skip_group_check=True)
                        for s in range(NSEQ):
                            mm = nc.tensor.matmul(op[t % 2][0:r, h, :], qs[:, h, s, :], Ss[:, h // 2, s, :], start=False, stop=(s == NSEQ - 1),
                                                  skip_group_check=True)
                    mm.then_inc(o_done, 1)
                if t >= 1:
                    turn_out(t - 1)
            pe.wait_ge(v_split, 1)
            pe.wait_ge(o_stored, NTP)
            for g in range(2):
                if g == 1:
                    pe.wait_ge(sample_ready, 1)
                for b in range(2):
                    for h in (2 * g, 2 * g + 1):
                        mm = nc.tensor.matmul(kvs[half(h), b, :], k_nat[NTP % 2][0:TS, 0, h // 2, half(h)],
                                              vs[:, 4 * b:4 * b + 4, h, :], start=True, stop=True,
                                              skip_group_check=True)
                mm.then_inc(kvs_done, 1)
            turn_out(NTP)

        @block.scalar
        def _(act):
            for t in range(NT):
                r = rows(t)
                act.wait_ge(o_done, t + 1)
                if t >= 1:
                    act.wait_ge(stded, t)
                nc.scalar.activation(sq[0:r], op[t % 2][0:r], ACT.Square).then_inc(squared, 1)
                act.wait_ge(step, 2 * (t + 1))
                nc.scalar.activation(rstd[0:r], rinv[0:r], ACT.Sqrt).then_inc(stded, 1)

        @block.vector
        def _(dve):
            ls = Count(local)
            dve.wait_ge(gain_turned, 1)
            nc.vector.tensor_copy(gain[:], sp_[0][:, 0, 0:H]).then_inc(masked, 1)
            for b in range(2):
                nc.vector.memset(k_nat[b][GC:P, 0], 0.0)
                nc.vector.memset(k_nat[b][0:GC, 1], 0.0)
            nc.vector.memset(S[:], 0.0).then_inc(local, 1)
            dve.wait_ge(local, ls.up())

            def state(t, c):
                n = 2 * t + c
                if t >= 1:
                    dve.wait_ge(o_done, t)
                for p in range(2):
                    ins = nc.vector.tensor_scalar(Sm[c][:, p, :], S[:, p, :], fac[:, 0, p, n:n + 1], None, ALU.mult)
                ins.then_inc(decayed, 1)
                if c == 0:
                    dve.wait_ge(kv_done, t + 1)
                for p in range(2):
                    ins = nc.vector.tensor_scalar(kvf[:, p, :], kvp[:, c, p, :], fac[:, 1, p, n:n + 1], None, ALU.mult)
                ins.then_inc(kv_read, 1)
                dve.wait_ge(kv_read, n + 1)
                dve.wait_ge(decayed, n + 1)
                for p in range(2):
                    ins = nc.vector.scalar_tensor_tensor(out=S[:, p, :], in0=S[:, p, :], scalar=fac[:, 2, p, n:n + 1],
                                                         in1=kvf[:, p, :], op0=ALU.mult, op1=ALU.add)
                ins.then_inc(s_ready, 1)
                dve.wait_ge(s_ready, n + 1)

            def store_out(t):
                r = rows(t)
                dve.wait_ge(o_turned, t + 1)
                nc.vector.tensor_tensor(o_t[:, 0:H, t * P:t * P + r], sp_[(t + 1) % 2][:, :, 0:r],
                                        gain[:].unsqueeze(2).broadcast_to([P, H, r]), ALU.mult).then_inc(o_stored, 1)

            for t in range(NT):
                r = rows(t)
                dve.wait_ge(k_turned, t + 1)
                if t < NTP:
                    for c in range(2):
                        own = slice(c * GC, (c + 1) * GC)
                        ins = nc.vector.tensor_copy(k_nat[t % 2][own, c], kp[own])
                    ins.then_inc(k_stored, 1)
                else:
                    nc.vector.tensor_copy(k_nat[t % 2][0:r, 0], kp[0:r]).then_inc(k_stored, 1)
                dve.wait_ge(scored, t + 1)
                if t == 0:
                    dve.wait_ge(shaped, 9)
                m = mask if t < NTP else mask_s
                nc.vector.tensor_tensor(prob[t % 2][0:r, :, 0:r], sp_[t % 2][0:r, :, 0:r],
                                        m[:].unsqueeze(1).broadcast_to([r, H, r]), ALU.mult).then_inc(masked, 1)
                if t < NTP:
                    state(t, 0)
                    state(t, 1)
                else:
                    for h in range(H):
                        ins = nc.vector.tensor_tensor(qs[:, h], seq_col[:],
                                                      qz[:, h, SEQ:T].unsqueeze(1).broadcast_to([P, NSEQ, TS]), ALU.mult)
                    ins.then_inc(q_split, 1)
                    for s in range(NSEQ):
                        ins = nc.vector.tensor_scalar(vs[:, s], v_sb[0:TS, NTP, :].rearrange("p (h e) -> p h e", h=H),
                                                      seq_row[:, s:s + 1], None, ALU.mult)
                    ins.then_inc(v_split, 1)
                dve.wait_ge(squared, t + 1)
                nc.vector.tensor_reduce(ssum[0:r], sq[0:r], AX.X, ALU.add).then_inc(local, 1)
                dve.wait_ge(local, ls.up())
                nc.vector.tensor_scalar(ssum[0:r], ssum[0:r], 1.0 / DV, EPS, ALU.mult, ALU.add).then_inc(step, 1)
                dve.wait_ge(step, 2 * t + 1)
                nc.vector.reciprocal(rinv[0:r], ssum[0:r]).then_inc(step, 1)
                dve.wait_ge(stded, t + 1)
                if t >= 2:
                    dve.wait_ge(o_turned, t - 1)
                nc.vector.tensor_tensor(on[t % 2][0:r], op[t % 2][0:r],
                                        rstd[0:r].unsqueeze(2).broadcast_to([r, H, DV]), ALU.mult).then_inc(local, 1)
                dve.wait_ge(local, ls.up())
                nc.vector.tensor_tensor(on[t % 2][0:r], on[t % 2][0:r],
                                        g_sb[0:r, t, :].rearrange("p (h e) -> p h e", h=H), ALU.mult).then_inc(o_normed, 1)
                if t >= 1:
                    store_out(t - 1)
            for g in range(2):
                dve.wait_ge(kvs_done, g + 1)
                nc.vector.tensor_tensor(Ss[:, g], Ss[:, g], kvs[:].rearrange("p b (s e) -> p (b s) e", e=DV),
                                        ALU.add).then_inc(local, 1)
                dve.wait_ge(local, ls.up())
                nc.vector.tensor_tensor(Ss[:, g], Ss[:, g], fac_s[:, g, :].unsqueeze(2).broadcast_to([P, NSEQ, DV]),
                                        ALU.mult).then_inc(sample_ready, 1)
            store_out(NTP)



TWO_PI = (6.28125, 0.0019350051879882812, 3.0199159819567e-07)
ROUND = 1.5 * 2 ** 23


def s5_tables(nc, A, tab):
    with ExitStack() as ctx:
        def sb(name, shape, dt=F32):
            return ctx.enter_context(nc.sbuf_tensor("st_" + name, shape, dt))

        def ps(name):
            return ctx.enter_context(nc.psum_tensor("st_" + name, [P, 4, P], F32))

        def sem(name):
            return new_sem(nc, "st_" + name)

        NA = 8
        lam = sb("lam", [P, 2, GP])
        ldt = sb("ldt", [P, GP])
        dt = sb("dt", [P, GP])
        lrdt = sb("lrdt", [P, GP])
        ang = sb("ang", [P, NA, GP])
        nrot = sb("nrot", [P, NA, GP])
        aab = sb("aab", [P, NA, GP])
        sn = sb("sn", [P, NA, GP])
        cs = sb("cs", [P, NA, GP])
        halfpi = sb("halfpi", [P, 1])
        mag = sb("mag", [P, GP])
        a1, a2 = sb("a1", [P, 2, GP]), sb("a2", [P, 2, GP])
        f = sb("f", [P, 2, GP])
        q = sb("q", [P, 6, GP])
        bin_ = sb("bin", [P, 2, GP, GCH])
        cin = sb("cin", [P, 2, 2, P])
        ba = sb("ba", [P, 2, GP, SC, GCH])
        ca = sb("ca", [P, 2, GP, SC + 1, GCH])
        bbz = sb("bbz", [P, 2, G, GCH])
        tmp = sb("tmp", [P, 2, GP, P])
        kk = tmp[0:GCH].rearrange("p i q s -> p (i q s)").rearrange("p (g k c) -> p g k c", g=G, c=GCH)
        dd = sb("dd", [GCH, G])
        dg = sb("dg", [GCH, G, GCH])
        ident = sb("ident", [P, P])
        pb = [ps(f"pb{b}") for b in range(8)]
        loaded, zeroed, shaped = sem("loaded"), sem("zeroed"), sem("shaped")
        step = sem("step")
        dted, angled, absd, trig = sem("dted"), sem("angled"), sem("absd"), sem("trig")
        c_turned, b_turned, b_ready = sem("c_turned"), sem("b_turned"), sem("b_ready")
        c_stored, b_stored = sem("c_stored"), sem("b_stored")
        k_done, k_ready, k_read, toep = sem("k_done"), sem("k_ready"), sem("k_read"), sem("toep")
        kk_ready = sem("kk_ready")
        block = ctx.enter_context(nc.Block())

        @block.sync
        def _(sp):
            for i, n in enumerate(("s5_lam_re", "s5_lam_im")):
                for h in range(2):
                    sp.dma_start(lam[ST * h:ST * h + ST, i, :],
                                 A[n][0].rearrange("(q h) p -> h p q", h=2)[h]).then_inc(loaded, 16)
            for h in range(2):
                sp.dma_start(ldt[ST * h:ST * h + ST, :],
                             A["s5_log_dt"][0].rearrange("(q h) -> h q", h=2)[h:h + 1, :].broadcast_to([ST, GP])
                             ).then_inc(loaded, 16)
                for i, n in enumerate(("s5_b_re", "s5_b_im")):
                    sp.dma_start(bin_[ST * h:ST * h + ST, i],
                                 A[n][0].rearrange("(q h) p c -> h p q c", h=2)[h]).then_inc(loaded, 16)
            for i, n in enumerate(("s5_c_re", "s5_c_im")):
                for half in range(2):
                    for j in range(SC):
                        g = 2 * (half * SC + j)
                        sp.dma_start(cin[j * GCH:(j + 1) * GCH, i, half, :].rearrange("c (h p) -> c h p", h=2),
                                     A[n][0, g:g + 2].rearrange("h c p -> c h p")).then_inc(loaded, 16)
            sp.dma_start(dd[:], A["s5_d"][0].rearrange("(g c) -> c g", c=GCH)).then_inc(loaded, 16)
            sp.wait_ge(kk_ready, 1)
            sp.wait_ge(shaped, 2)
            for r in range(SC):
                sp.dma_start(tab.tp[r * GCH:(r + 1) * GCH, :, r * GCH:],
                             kk[:, :, 0:SC - r, :].rearrange("c g k d -> c g (k d)")).then_inc(toep, 16)
            sp.wait_ge(toep, 16 * SC)

        @block.gpsimd
        def _(pool):
            nc.gpsimd.memset(ident[:], 0.0).then_inc(zeroed, 1)
            pool.wait_ge(zeroed, 1)
            nc.gpsimd.affine_select(out=ident[:], in_=ident[:], compare_op=ALU.not_equal, fill=1.0, base=0,
                                    pattern=[[-1, P]], channel_multiplier=1).then_inc(shaped, 1)
            nc.gpsimd.memset(tab.tp[:], 0.0).then_inc(shaped, 1)
            nc.gpsimd.memset(tab.cm[:], 0.0).then_inc(shaped, 1)
            nc.gpsimd.memset(bbz[:], 0.0).then_inc(shaped, 1)

        @block.scalar
        def _(act):
            act.wait_ge(loaded, 16 * NLOAD)
            nc.scalar.activation(dt[:], ldt[:], ACT.Exp).then_inc(dted, 1)
            act.wait_ge(angled, 1)
            nc.scalar.activation(mag[:], lrdt[:], ACT.Exp).then_inc(dted, 1)
            nc.scalar.activation(tab.r8[:], lrdt[:], ACT.Exp, scale=float(SC)).then_inc(dted, 1)
            act.wait_ge(angled, 2)
            nc.scalar.activation(aab[:], ang[:], ACT.Abs).then_inc(absd, 1)
            act.wait_ge(absd, 1)
            nc.scalar.activation(sn[:], ang[:], ACT.Sin).then_inc(trig, 1)
            nc.scalar.activation(cs[:], aab[:], ACT.Sin, bias=halfpi[:], scale=-1.0).then_inc(trig, 1)
            for n in range(8):
                act.wait_ge(b_turned, n + 1)
                nc.scalar.activation(tab.bm[:].rearrange("p q i s -> p (q i) s")[:, 4 * n:4 * n + 4], pb[4 + n % 4][:],
                                     ACT.Copy).then_inc(b_stored, 1)

        @block.tensor
        def _(pe):
            pe.wait_ge(loaded, 16 * NLOAD)
            pe.wait_ge(shaped, 1)
            for i in range(2):
                for half in range(2):
                    mm = nc.tensor.transpose(pb[0][:, 2 * i + half, :], cin[:, i, half, :], ident[:])
            mm.then_inc(c_turned, 1)
            pe.wait_ge(b_ready, 1)
            for n in range(8):
                if n >= 4:
                    pe.wait_ge(b_stored, n - 3)
                for j in range(4):
                    gp, i = (4 * n + j) // 2, (4 * n + j) % 2
                    mm = nc.tensor.transpose(pb[4 + n % 4][:, j, :], ba[:, i, gp, :, :].rearrange("p k c -> p (k c)"),
                                             ident[:])
                mm.then_inc(b_turned, 1)
            pe.wait_ge(k_ready, 1)
            for n in range(8):
                if n >= 4:
                    pe.wait_ge(k_read, n - 3)
                for j in range(4):
                    g = 4 * n + j
                    for i in range(2):
                        mm = nc.tensor.matmul(pb[n % 4][0:GCH, j, :], bbz[:, i, g, :],
                                              ca[:, i, g // 2, 0:SC, :].rearrange("p k c -> p (k c)"),
                                              start=(i == 0), stop=(i == 1))
                mm.then_inc(k_done, 1)

        @block.vector
        def _(dve):
            s = Count(step)

            def tt(out, a, b, op):
                nc.vector.tensor_tensor(out, a, b, op).then_inc(step, 1)
                s.up()

            def settle():
                dve.wait_ge(step, s.n)

            def cmul(out, x, a, shape):
                t = [tmp[:, i].rearrange("p q s -> p (q s)")[:, 0:shape[1] * shape[2]]
                     .rearrange("p (q s) -> p q s", q=shape[1]) for i in range(2)]
                tt(out[0], x[0], a[0], ALU.mult)
                tt(t[0], x[1], a[1], ALU.mult)
                tt(out[1], x[1], a[0], ALU.mult)
                tt(t[1], x[0], a[1], ALU.mult)
                settle()
                tt(out[0], out[0], t[0], ALU.subtract)
                tt(out[1], out[1], t[1], ALU.add)
                settle()

            def square(out, x):
                cmul([out[:, i, :].unsqueeze(2) for i in range(2)], [x[:, i, :].unsqueeze(2) for i in range(2)],
                     [x[:, i, :].unsqueeze(2) for i in range(2)], [P, GP, 1])

            nc.vector.memset(halfpi[:], 1.5707963267948966).then_inc(step, 1)
            s.up()
            dve.wait_ge(dted, 1)
            tt(lrdt[:], lam[:, 0, :], dt[:], ALU.mult)
            tt(ang[:, 0, :], lam[:, 1, :], dt[:], ALU.mult)
            settle()
            dve.sem_inc(angled, 1)
            for k in range(1, NA):
                nc.vector.tensor_scalar(ang[:, k, :], ang[:, 0, :], float(SC * 2 ** (k - 1)), None, ALU.mult).then_inc(step, 1)
                s.up()
            settle()
            nc.vector.tensor_scalar(nrot[:], ang[:], 0.15915494309189535, ROUND, ALU.mult, ALU.add).then_inc(step, 1)
            s.up()
            settle()
            nc.vector.tensor_scalar(nrot[:], nrot[:], ROUND, None, ALU.subtract).then_inc(step, 1)
            s.up()
            settle()
            for part in TWO_PI:
                nc.vector.scalar_tensor_tensor(out=ang[:], in0=nrot[:], scalar=-part, in1=ang[:],
                                               op0=ALU.mult, op1=ALU.add).then_inc(step, 1)
                s.up()
                settle()
            nc.vector.tensor_scalar(ang[:], ang[:], 3.1415925, -3.1415925, ALU.min, ALU.max).then_inc(angled, 1)
            dve.wait_ge(trig, 2)
            dve.wait_ge(dted, 3)
            tt(a1[:, 0, :], mag[:], cs[:, 0, :], ALU.mult)
            tt(a1[:, 1, :], mag[:], sn[:, 0, :], ALU.mult)
            lr, li = lam[:, 0, :], lam[:, 1, :]
            tt(q[:, 0, :], lr, lr, ALU.mult)
            tt(q[:, 1, :], li, li, ALU.mult)
            settle()
            tt(q[:, 0, :], q[:, 0, :], q[:, 1, :], ALU.add)
            nc.vector.tensor_scalar(q[:, 2, :], a1[:, 0, :], -1.0, None, ALU.add).then_inc(step, 1)
            s.up()
            settle()
            nc.vector.reciprocal(q[:, 1, :], q[:, 0, :]).then_inc(step, 1)
            s.up()
            tt(q[:, 3, :], q[:, 2, :], lr, ALU.mult)
            tt(q[:, 4, :], a1[:, 1, :], li, ALU.mult)
            tt(f[:, 1, :], a1[:, 1, :], lr, ALU.mult)
            tt(q[:, 5, :], q[:, 2, :], li, ALU.mult)
            settle()
            tt(f[:, 0, :], q[:, 3, :], q[:, 4, :], ALU.add)
            tt(f[:, 1, :], f[:, 1, :], q[:, 5, :], ALU.subtract)
            settle()
            tt(f[:, 0, :], f[:, 0, :], q[:, 1, :], ALU.mult)
            tt(f[:, 1, :], f[:, 1, :], q[:, 1, :], ALU.mult)
            square(a2, a1)
            square(tab.a4, a2)

            def over(v, n, i):
                return v[:, i, :].unsqueeze(2).broadcast_to([P, GP, n])

            def powers(arr, k0, k1, a, d0):
                n = (k1 - k0) * GCH

                def part(i, k):
                    return arr[:, i].rearrange("p q k c -> p q (k c)")[:, :, k * GCH:k * GCH + n]

                cmul([part(0, d0), part(1, d0)], [part(0, k0), part(1, k0)], [over(a, n, 0), over(a, n, 1)], [P, GP, n])

            cmul([ba[:, i, :, SC - 1, :] for i in range(2)], [bin_[:, i] for i in range(2)],
                 [over(f, GCH, 0), over(f, GCH, 1)], [P, GP, GCH])
            powers(ba, SC - 1, SC, a1, SC - 2)
            powers(ba, SC - 2, SC, a2, SC - 4)
            powers(ba, SC - 4, SC, tab.a4, SC - 8)
            dve.sem_inc(b_ready, 1)
            dve.wait_ge(c_turned, 1)
            for i in range(2):
                nc.vector.tensor_copy(ca[:, i, :, 0, :],
                                      pb[0][:, 2 * i:2 * i + 2, :].rearrange("p b (q c) -> p (b q) c", c=GCH)).then_inc(step, 1)
                s.up()
            settle()
            powers(ca, 0, 1, a1, 1)
            powers(ca, 0, 2, a2, 2)
            powers(ca, 0, 4, tab.a4, 4)
            powers(ca, 4, 5, tab.a4, 8)
            dve.wait_ge(shaped, 4)
            for h in range(2):
                own = slice(ST * h, ST * h + ST)
                nc.vector.tensor_copy(bbz[own, 0, h:G:2, :], ba[own, 0, :, SC - 1, :]).then_inc(step, 1)
                nc.vector.tensor_scalar(bbz[own, 1, h:G:2, :], ba[own, 1, :, SC - 1, :], -1.0, None, ALU.mult).then_inc(step, 1)
                nc.vector.tensor_copy(tab.cm[own, :, 0, h, :], ca[own, 0, :, 1:, :].rearrange("p q k c -> p q (k c)")).then_inc(step, 1)
                nc.vector.tensor_scalar(tab.cm[own, :, 1, h, :], ca[own, 1, :, 1:, :].rearrange("p q k c -> p q (k c)"),
                                        -1.0, None, ALU.mult).then_inc(step, 1)
                s.up(4)
            tt(dg[:], ident[0:GCH, 0:GCH].unsqueeze(1).broadcast_to([GCH, G, GCH]),
               dd[:].unsqueeze(2).broadcast_to([GCH, G, GCH]), ALU.mult)
            settle()
            dve.sem_inc(k_ready, 1)
            nc.vector.tensor_copy(tab.w[:, 0, :, 1], cs[:, 1, :]).then_inc(step, 1)
            nc.vector.tensor_copy(tab.w[:, 1, :, 1], sn[:, 1, :]).then_inc(step, 1)
            s.up(2)
            settle()
            for k in range(7):
                n = 2 ** k
                cmul([tab.w[:, i, :, n + 1:2 * n + 1] for i in range(2)], [tab.w[:, i, :, 1:n + 1] for i in range(2)],
                     [cs[:, k + 1, :].unsqueeze(2).broadcast_to([P, GP, n]),
                      sn[:, k + 1, :].unsqueeze(2).broadcast_to([P, GP, n])], [P, GP, n])
            for n in range(8):
                dve.wait_ge(k_done, n + 1)
                nc.vector.tensor_copy(kk[:, 4 * n:4 * n + 4], pb[n % 4][0:GCH].rearrange("p g (k c) -> p g k c", c=GCH)
                                      ).then_inc(k_read, 1)
            dve.wait_ge(k_read, 8)
            nc.vector.tensor_tensor(kk[:, :, 0, :], kk[:, :, 0, :], dg[:], ALU.add).then_inc(kk_ready, 1)


NLOAD = 2 * 2 + 2 * 3 + 2 * 2 * SC + 1


def s5_scan(nc, A, tab, u_sb, us_nat, x_g, s_all, s0, state_re, state_im, state_re_s, state_im_s):
    with ExitStack() as ctx:
        def sb(name, shape, dt=F32):
            return ctx.enter_context(nc.sbuf_tensor("ss_" + name, shape, dt))

        def sem(name):
            return new_sem(nc, "ss_" + name)

        v = sb("v", [P, 2, GP, NMS])
        tmp = sb("tmp", [P, 2, GP, NM])
        us8 = s_all[:].rearrange("p i q m -> p (i q m)")[0:NSEQ, 0:SC * W4].rearrange("p (g r c) -> p g r c", g=G, r=SC)
        s0_in = sb("s0_in", [P, 2, P])
        fin = sb("fin", [P, 2, NSEQ + 1, GP])
        fin_o = sb("fin_o", [P, 2, P])
        finp_o = sb("finp_o", [GP, 2, P])
        ident = sb("ident", [P, P])
        pb = [ctx.enter_context(nc.psum_tensor(f"ss_pb{b}", [P, W4], F32)) for b in range(8)]
        loaded, zeroed, shaped, us_loaded, us_zero = sem("loaded"), sem("zeroed"), sem("shaped"), sem("us_loaded"), sem("us_zero")
        u_turned, u_stored = sem("u_turned"), sem("u_stored")
        v_done, v_stored = sem("v_done"), sem("v_stored")
        step, rdata, fin_ready, fin_turned, fin_stored, written = (
            sem("step"), sem("rdata"), sem("fin_ready"), sem("fin_turned"), sem("fin_stored"), sem("written"))
        block = ctx.enter_context(nc.Block())

        @block.sync
        def _(sp):
            for i, n in enumerate(("state_s5_re", "state_s5_im")):
                sp.dma_start(s0_in[:, i, :], A[n][0].rearrange("s (q h) p -> (s q) (h p)", h=2)).then_inc(loaded, 16)
            sp.wait_ge(us_zero, 1)
            for j in range(SLEN):
                sp.dma_start(us8[:, :, SC - SLEN + j, :], us_nat[j:TS:SLEN, :].rearrange("s (g c) -> s g c", g=G)
                             ).then_inc(us_loaded, 16)
            sp.wait_ge(fin_stored, 2)
            for i, (ds, dp) in enumerate(((state_re_s, state_re), (state_im_s, state_im))):
                sp.dma_start(ds.rearrange("s (q h) p -> (s q) (h p)", h=2), fin_o[:, i, :]).then_inc(written, 16)
                sp.dma_start(dp.rearrange("(q h) p -> q (h p)", h=2), finp_o[:, i, :]).then_inc(written, 16)
            sp.wait_ge(written, 64)

        @block.gpsimd
        def _(pool):
            nc.gpsimd.memset(us8[:, :, 0:SC - SLEN, :], 0.0).then_inc(us_zero, 1)
            nc.gpsimd.memset(ident[:], 0.0).then_inc(zeroed, 1)
            pool.wait_ge(zeroed, 1)
            nc.gpsimd.affine_select(out=ident[:], in_=ident[:], compare_op=ALU.not_equal, fill=1.0, base=0,
                                    pattern=[[-1, P]], channel_multiplier=1).then_inc(shaped, 1)

        @block.tensor
        def _(pe):
            pe.wait_ge(shaped, 1)
            for n in range(8):
                if n >= 4:
                    pe.wait_ge(u_stored, n - 3)
                for j in range(4):
                    g = 4 * n + j
                    mm = nc.tensor.transpose(pb[n % 4][:, j * P:(j + 1) * P], u_sb[:, g].rearrange("p r c -> p (r c)"), ident[:])
                mm.then_inc(u_turned, 1)
            pe.wait_ge(us_loaded, 16 * SLEN)
            pe.wait_ge(u_stored, 5)
            for g in range(G):
                mm = nc.tensor.transpose(pb[0][:, g * NSEQ:(g + 1) * NSEQ], us8[:, g].rearrange("p r c -> p (r c)"),
                                         ident[0:NSEQ, 0:NSEQ])
            mm.then_inc(u_turned, 1)
            pe.wait_ge(loaded, 32)
            pe.wait_ge(u_stored, 6)
            for i in range(2):
                mm = nc.tensor.transpose(pb[1][:, i * P:(i + 1) * P], s0_in[:, i, :], ident[:])
            mm.then_inc(u_turned, 1)
            pe.wait_ge(u_stored, 9)
            for gp in range(GP):
                if gp >= 4:
                    pe.wait_ge(v_stored, gp - 3)
                for i in range(2):
                    for h in range(2):
                        mm = nc.tensor.matmul(pb[4 + gp % 4][ST * h:ST * h + ST, i * NMS:(i + 1) * NMS],
                                              tab.bm[:, gp, i, ST * h:ST * h + ST], x_g[:, 2 * gp + h, :],
                                              start=True, stop=True, skip_group_check=True)
                mm.then_inc(v_done, 1)
            pe.wait_ge(fin_ready, 1)
            for i in range(2):
                nc.tensor.transpose(pb[0][:, i * P:(i + 1) * P], fin[:, i, 0:NSEQ, :].rearrange("p s q -> p (s q)"), ident[:])
                mm = nc.tensor.transpose(pb[1][0:GP, i * P:(i + 1) * P], fin[:, i, NSEQ, :], ident[:])
            mm.then_inc(fin_turned, 1)

        @block.scalar
        def _(act):
            for gp in range(GP):
                act.wait_ge(v_done, gp + 1)
                nc.scalar.activation(v[:, :, gp, :], pb[4 + gp % 4][:, 0:2 * NMS].rearrange("p (i m) -> p i m", i=2),
                                     ACT.Copy).then_inc(v_stored, 1)

        @block.vector
        def _(dve):
            s = Count(step)

            def tt(out, a, b, op):
                nc.vector.tensor_tensor(out, a, b, op).then_inc(step, 1)
                s.up()

            def settle():
                dve.wait_ge(step, s.n)

            for n in range(8):
                dve.wait_ge(u_turned, n + 1)
                nc.vector.tensor_copy(x_g[:, 4 * n:4 * n + 4, 0:NM],
                                      pb[n % 4][:].rearrange("p (g m) -> p g m", m=P)).then_inc(u_stored, 1)
            dve.wait_ge(u_turned, 9)
            nc.vector.tensor_copy(x_g[:, :, NM:], pb[0][:, 0:G * NSEQ].rearrange("p (g m) -> p g m", m=NSEQ)
                                  ).then_inc(u_stored, 1)
            dve.wait_ge(u_turned, 10)
            nc.vector.tensor_copy(s0[:], pb[1][:, 0:2 * P].rearrange("p (i s q) -> p i s q", i=2, q=GP)).then_inc(u_stored, 1)
            w = [tab.w[:, i, :, 1:] for i in range(2)]
            after = [s_all[:, i, :, 1:] for i in range(2)]
            vp = [v[:, i, :, 0:NM] for i in range(2)]
            rot = [tmp[:, i] for i in range(2)]
            flat = [v[:].rearrange("p i q m -> p (i q m)")[:, i * GP * NM:(i + 1) * GP * NM] for i in range(2)]
            room = [x.rearrange("p (q m) -> p q m", m=NM) for x in flat]
            dve.wait_ge(v_stored, GP)
            for i in range(2):
                nc.vector.tensor_copy(fin[:, i, 0:NSEQ, :], v[:, i, :, NM:].rearrange("p q s -> p s q")).then_inc(step, 1)
            s.up(2)
            tt(rot[0], vp[0], w[0], ALU.mult)
            tt(after[0], vp[1], w[1], ALU.mult)
            tt(rot[1], vp[1], w[0], ALU.mult)
            tt(after[1], vp[0], w[1], ALU.mult)
            settle()
            tt(rot[0], rot[0], after[0], ALU.add)
            tt(rot[1], rot[1], after[1], ALU.subtract)
            nc.vector.tensor_copy(room[0], tab.r8[:].unsqueeze(2).broadcast_to([P, GP, NM])).then_inc(step, 1)
            s.up()
            settle()
            nc.vector.memset(room[0][:, :, 0], 0.0).then_inc(step, 1)
            nc.vector.memset(s_all[:, :, :, 0], 0.0).then_inc(step, 1)
            s.up(2)
            settle()
            for i in range(2):
                g = rot[i].rearrange("p q m -> p (q m)")
                nc.vector.tensor_tensor_scan(g, flat[0], g, 0.0, ALU.mult, ALU.add).then_inc(step, 1)
                s.up()
            settle()
            tt(after[0], rot[0], w[0], ALU.mult)
            tt(after[1], rot[1], w[0], ALU.mult)
            tt(room[0], rot[1], w[1], ALU.mult)
            tt(room[1], rot[0], w[1], ALU.mult)
            settle()
            tt(after[0], after[0], room[0], ALU.subtract)
            tt(after[1], after[1], room[1], ALU.add)
            settle()
            for i in range(2):
                nc.vector.tensor_copy(fin[:, i, NSEQ, :], s_all[:, i, :, NM]).then_inc(step, 1)
            s.up(2)
            a4 = [tab.a4[:, i, :].unsqueeze(1).broadcast_to([P, NSEQ, GP]) for i in range(2)]
            for i, j, k, op in ((0, 0, 0, ALU.add), (0, 1, 1, ALU.subtract), (1, 0, 1, ALU.add), (1, 1, 0, ALU.add)):
                tt(tmp[:, 0, 0:NSEQ, 0:GP], s0[:, j], a4[k], ALU.mult)
                settle()
                tt(fin[:, i, 0:NSEQ, :], fin[:, i, 0:NSEQ, :], tmp[:, 0, 0:NSEQ, 0:GP], op)
                settle()
            dve.sem_inc(fin_ready, 1)
            dve.wait_ge(fin_turned, 1)
            nc.vector.tensor_copy(fin_o[:], pb[0][:, 0:2 * P].rearrange("p (i s) -> p i s", i=2)).then_inc(fin_stored, 1)
            nc.vector.tensor_copy(finp_o[:], pb[1][0:GP, 0:2 * P].rearrange("p (i s) -> p i s", i=2)).then_inc(fin_stored, 1)


def s5_outputs(nc, A, tab, u_sb, x_g, s_all, s0, o_t):
    with ExitStack() as ctx:
        def sb(name, shape, dt=F32):
            return ctx.enter_context(nc.sbuf_tensor("so_" + name, shape, dt))

        def sem(name):
            return new_sem(nc, "so_" + name)

        z = u_sb[:].rearrange("p g r c -> p (g r c)").rearrange("p (r c) -> p r c", r=SC)
        zs = sb("zs", [NSEQ, SLEN, W4])
        z_t = sb("z_t", [P, 4, T])
        wg = sb("wg", [P, 4, W4])
        bg = sb("bg", [P, 4])
        sg = [sb(f"sg{b}", [P, NW]) for b in range(2)]
        ident = sb("ident", [P, P])
        pb = [ctx.enter_context(nc.psum_tensor(f"so_pb{b}", [P, W4], F32)) for b in range(8)]
        loaded, zeroed, shaped = sem("loaded"), sem("zeroed"), sem("shaped")
        y_done, z_ready, z_turned, z_stored = sem("y_done"), sem("z_ready"), sem("z_turned"), sem("z_stored")
        g_done, g_ready, o_ready = sem("g_done"), sem("g_ready"), sem("o_ready")
        block = ctx.enter_context(nc.Block())
        NY = GP // 2

        @block.sync
        def _(sp):
            sp.dma_start(wg[:], A["w_glu"][0].rearrange("(k p) c -> p k c", p=P)).then_inc(loaded, 16)
            sp.dma_start(bg[:], A["b_glu"][0].rearrange("(k p) -> p k", p=P)).then_inc(loaded, 16)

        @block.gpsimd
        def _(pool):
            nc.gpsimd.memset(ident[:], 0.0).then_inc(zeroed, 1)
            pool.wait_ge(zeroed, 1)
            nc.gpsimd.affine_select(out=ident[:], in_=ident[:], compare_op=ALU.not_equal, fill=1.0, base=0,
                                    pattern=[[-1, P]], channel_multiplier=1).then_inc(shaped, 1)

        @block.tensor
        def _(pe):
            def outputs(bank, gp, m, width, state, cols):
                q = (gp % 2) * 2 * P
                for h in range(2):
                    nc.tensor.matmul(bank[0:width, q + h * P:q + h * P + cols], x_g[:, 2 * gp + h, m],
                                     tab.tp[:, 2 * gp + h, P - cols:], start=True, stop=False, skip_group_check=True)
                    for i in range(2):
                        mm = nc.tensor.matmul(bank[0:width, q + h * P:q + h * P + cols], state(i, gp),
                                              tab.cm[:, gp, i, h, 0:cols], start=False, stop=(i == 1), skip_group_check=True)
                return mm

            for n in range(NY):
                if n >= 4:
                    pe.wait_ge(z_ready, n - 3)
                for gp in (2 * n, 2 * n + 1):
                    mm = outputs(pb[n % 4], gp, slice(0, NM), P, lambda i, gp: s_all[:, i, gp, 0:NM], P)
                mm.then_inc(y_done, 1)
            for n in range(NY):
                pe.wait_ge(z_ready, NY + n - 3)
                for gp in (2 * n, 2 * n + 1):
                    mm = outputs(pb[n % 4], gp, slice(NM, NMS), NSEQ, lambda i, gp: s0[:, i, :, gp], SLEN * GCH)
                mm.then_inc(y_done, 1)
            pe.wait_ge(shaped, 1)
            pe.wait_ge(z_ready, NY)
            for r in range(SC):
                if r >= 4:
                    pe.wait_ge(z_stored, r - 3)
                for c in range(4):
                    mm = nc.tensor.transpose(pb[4 + r % 4][:, c * P:(c + 1) * P], z[:, r, c * P:(c + 1) * P], ident[:])
                mm.then_inc(z_turned, 1)
            pe.wait_ge(z_ready, 2 * NY)
            pe.wait_ge(z_stored, SC - 3)
            for j in range(SLEN):
                for c in range(4):
                    q = (j * 4 + c) * NSEQ
                    mm = nc.tensor.transpose(pb[4][:, q:q + NSEQ], zs[:, j, c * P:(c + 1) * P], ident[0:NSEQ, 0:NSEQ])
            mm.then_inc(z_turned, 1)
            pe.wait_ge(loaded, 32)
            pe.wait_ge(z_stored, SC + 1)
            n = 0
            for c in range(4):
                for b in range(3):
                    if n >= 4:
                        pe.wait_ge(g_ready, n - 3)
                    for k in range(4):
                        mm = nc.tensor.matmul(pb[n % 4][:, 0:NW], wg[:, k, c * P:(c + 1) * P],
                                              z_t[:, k, b * NW:(b + 1) * NW], start=(k == 0), stop=(k == 3))
                    mm.then_inc(g_done, 1)
                    n += 1

        @block.scalar
        def _(act):
            for n in range(2 * NY):
                act.wait_ge(y_done, n + 1)
                c0 = (n % NY) * 4 * GCH
                if n < NY:
                    out = z[:, :, c0:c0 + 4 * GCH].rearrange("m r (q c) -> m q r c", c=GCH)
                    y = pb[n % 4][:].rearrange("m (q r c) -> m q r c", q=4, c=GCH)
                else:
                    out = zs[:, :, c0:c0 + 4 * GCH].rearrange("m r (q c) -> m q r c", c=GCH)
                    y = pb[n % 4][0:NSEQ].rearrange("m (q r c) -> m q r c", q=4, c=GCH)[:, :, 0:SLEN, :]
                nc.scalar.activation(out, y, ACT.Gelu_apprx_tanh).then_inc(z_ready, 1)
            act.wait_ge(loaded, 32)
            n = 0
            for c in range(4):
                for b in range(3):
                    act.wait_ge(g_done, n + 1)
                    if n >= 2:
                        act.wait_ge(o_ready, n - 1)
                    nc.scalar.activation(sg[n % 2][:], pb[n % 4][:, 0:NW], ACT.Sigmoid, bias=bg[:, c:c + 1]).then_inc(g_ready, 1)
                    n += 1

        @block.vector
        def _(dve):
            for r in range(SC):
                dve.wait_ge(z_turned, r + 1)
                nc.vector.tensor_copy(z_t[:, :, r:SEQ:SC], pb[4 + r % 4][:].rearrange("p (c m) -> p c m", c=4)
                                      ).then_inc(z_stored, 1)
            dve.wait_ge(z_turned, SC + 1)
            for j in range(SLEN):
                ins = nc.vector.tensor_copy(z_t[:, :, SEQ + j:T:SLEN], pb[4][:, j * 4 * NSEQ:(j + 1) * 4 * NSEQ]
                                            .rearrange("p (c m) -> p c m", c=4))
            ins.then_inc(z_stored, 1)
            dve.wait_ge(z_stored, SC + 1)
            n = 0
            for c in range(4):
                for b in range(3):
                    dve.wait_ge(g_ready, n + 1)
                    tok = slice(b * NW, (b + 1) * NW)
                    nc.vector.tensor_tensor(o_t[:, 4 + c, tok], z_t[:, c, tok], sg[n % 2][:], ALU.mult).then_inc(o_ready, 1)
                    n += 1



def mix_out(nc, w_out, o_t, x_tiles, x2_tiles):
    with ExitStack() as ctx:
        def sem(name):
            return new_sem(nc, "mo_" + name)

        w = ctx.enter_context(nc.sbuf_tensor("mo_w", [P, KD, D], F32))
        x = [ctx.enter_context(nc.sbuf_tensor(f"mo_x{b}", [P, D], F32)) for b in range(3)]
        pb = [ctx.enter_context(nc.psum_tensor(f"mo_pb{b}", [P, W4], F32)) for b in range(8)]
        w_loaded, done, added = sem("w_loaded"), sem("done"), sem("added")
        x_loaded = [sem(f"x_loaded{b}") for b in range(3)]
        stored = [sem(f"stored{b}") for b in range(3)]
        block = ctx.enter_context(nc.Block())

        @block.sync
        def _(sp):
            sp.dma_start(w[:], w_out.rearrange("(k p) c -> p k c", p=P)).then_inc(w_loaded, 16)
            for t in range(NT):
                if t >= 3:
                    sp.wait_ge(stored[t % 3], 16 * (t // 3))
                sp.dma_start(x[t % 3][0:rows(t)], x_tiles[t]).then_inc(x_loaded[t % 3], 16)

        @block.gpsimd
        def _(pool):
            for t in range(NT):
                pool.wait_ge(added, 2 * t + 2)
                pool.dma_start(x2_tiles[t], x[t % 3][0:rows(t)]).then_inc(stored[t % 3], 16)
            for b in range(3):
                pool.wait_ge(stored[b], 16 * (NT // 3))

        @block.tensor
        def _(pe):
            pe.wait_ge(w_loaded, 16)
            for t in range(NT):
                for half in range(2):
                    n = 2 * t + half
                    if n >= 8:
                        pe.wait_ge(added, n - 7)
                    for k in range(KD):
                        mm = nc.tensor.matmul(pb[n % 8][0:rows(t)], o_t[:, k, t * P:t * P + rows(t)],
                                              w[:, k, half * W4:(half + 1) * W4], start=(k == 0), stop=(k == KD - 1))
                    mm.then_inc(done, 1)

        @block.vector
        def _(dve):
            for t in range(NT):
                dve.wait_ge(x_loaded[t % 3], 16 * (t // 3 + 1))
                for half in range(2):
                    n = 2 * t + half
                    xs = x[t % 3][0:rows(t), half * W4:(half + 1) * W4]
                    dve.wait_ge(done, n + 1)
                    nc.vector.tensor_tensor(xs, pb[n % 8][0:rows(t)], xs, ALU.add).then_inc(added, 1)


PARTS = ((0, 0), (0, 1), (1, 0))
NU = 2 * PH


def peer_scores(nc, wq, keys, h_hi, h_lo, s_sb):
    with ExitStack() as ctx:
        def sb(name, shape, dt=F32):
            return ctx.enter_context(nc.sbuf_tensor("pq_" + name, shape, dt))

        def sem(name):
            return new_sem(nc, "pq_" + name)

        WQ = 2 * P
        NWB = NU // 2
        raw = sb("raw", [P, KD, WQ])
        w = [[sb(f"w{b}{x}", [P, KD, WQ], F32R) for x in "hl"] for b in range(2)]
        keys_sb = sb("keys", [P, NU, P])
        keys_t = sb("keys_t", [P, NU, P])
        q_t = [sb(f"q_t{b}", [P, T]) for b in range(2)]
        ident = sb("ident", [P, P])
        pq = [ctx.enter_context(nc.psum_tensor(f"pq_pq{b}", [P, W4], F32)) for b in range(3)]
        psc = [ctx.enter_context(nc.psum_tensor(f"pq_ps{b}", [P, W4], F32)) for b in range(3)]
        pk = ctx.enter_context(nc.psum_tensor("pq_pk", [P, 4, P], F32))
        w_loaded, w_hi, w_lo = sem("w_loaded"), sem("w_hi"), sem("w_lo")
        keys_loaded, zeroed, shaped = sem("keys_loaded"), sem("zeroed"), sem("shaped")
        k_turned, k_stored, cleared = sem("k_turned"), sem("k_stored"), sem("cleared")
        q_done, q_stored, s_done, s_stored = sem("q_done"), sem("q_stored"), sem("s_done"), sem("s_stored")
        block = ctx.enter_context(nc.Block())
        w_dram = wq.rearrange("(k p) c -> p k c", p=P)

        @block.sync
        def _(sp):
            sp.dma_start(keys_sb[:], keys.rearrange("h s n d -> n (h s) d")).then_inc(keys_loaded, 16)
            for b in range(NWB):
                if b >= 1:
                    sp.wait_ge(w_lo, b)
                sp.dma_start(raw[:], w_dram[:, :, b * WQ:(b + 1) * WQ]).then_inc(w_loaded, 16)

        @block.gpsimd
        def _(pool):
            nc.gpsimd.memset(ident[:], 0.0).then_inc(zeroed, 1)
            pool.wait_ge(zeroed, 1)
            nc.gpsimd.affine_select(out=ident[:], in_=ident[:], compare_op=ALU.not_equal, fill=1.0, base=0,
                                    pattern=[[-1, P]], channel_multiplier=1).then_inc(shaped, 1)

        @block.tensor
        def _(pe):
            pe.wait_ge(shaped, 1)
            pe.wait_ge(keys_loaded, 16)
            for n in range(4):
                if n >= 1:
                    pe.wait_ge(k_stored, n)
                for j in range(4):
                    mm = nc.tensor.transpose(pk[:, j, :], keys_sb[:, 4 * n + j, :], ident[:])
                mm.then_inc(k_turned, 1)

            def score(c):
                pe.wait_ge(q_stored, 3 * (c + 1))
                pe.wait_ge(k_stored, 4)
                for b in range(3):
                    if c >= 1:
                        pe.wait_ge(s_stored, 3 * (c - 1) + b + 1)
                    for t in range(3 * b, 3 * b + 3):
                        mm = nc.tensor.matmul(psc[b][0:rows(t), (t % 3) * P:(t % 3 + 1) * P],
                                              q_t[c % 2][:, t * P:t * P + rows(t)], keys_t[:, c, :],
                                              start=True, stop=True, skip_group_check=True)
                    mm.then_inc(s_done, 1)

            for c in range(NU):
                pe.wait_ge(w_lo, c // 2 + 1)
                for n in range(3):
                    if c >= 1:
                        pe.wait_ge(q_stored, 3 * (c - 1) + n + 1)
                    steps = [(x, y, k) for x, y in PARTS for k in range(KD)]
                    for s, (x, y, k) in enumerate(steps):
                        mm = nc.tensor.matmul(pq[n][:, 0:NW], w[(c // 2) % 2][x][:, k, (c % 2) * P:(c % 2 + 1) * P],
                                              (h_hi, h_lo)[y][:, k, n * NW:(n + 1) * NW],
                                              start=(s == 0), stop=(s == len(steps) - 1))
                    mm.then_inc(q_done, 1)
                if c >= 1:
                    score(c - 1)
            score(NU - 1)

        @block.scalar
        def _(act):
            def high(b):
                act.wait_ge(w_loaded, 16 * (b + 1))
                if b >= 2:
                    act.wait_ge(q_done, 3 * 2 * (b - 1))
                nc.scalar.activation(w[b % 2][0][:], raw[:], ACT.Copy).then_inc(w_hi, 1)

            high(0)
            for c in range(NU):
                if c % 2 == 0 and c // 2 + 1 < NWB:
                    high(c // 2 + 1)
                for n in range(3):
                    act.wait_ge(q_done, 3 * c + n + 1)
                    if c >= 2:
                        act.wait_ge(s_done, 3 * (c - 1))
                    nc.scalar.activation(q_t[c % 2][:, n * NW:(n + 1) * NW], pq[n][:, 0:NW], ACT.Copy).then_inc(q_stored, 1)

        @block.vector
        def _(dve):
            nc.vector.memset(s_sb[:, NTP], 0.0).then_inc(cleared, 1)
            for n in range(4):
                dve.wait_ge(k_turned, n + 1)
                nc.vector.tensor_copy(keys_t[:, 4 * n:4 * n + 4], pk[:]).then_inc(k_stored, 1)
            dve.wait_ge(cleared, 1)

            def low(b):
                dve.wait_ge(w_hi, b + 1)
                nc.vector.tensor_tensor(w[b % 2][1][:], raw[:], w[b % 2][0][:].bitcast(F32), ALU.subtract).then_inc(w_lo, 1)

            low(0)
            low(1)
            for c in range(NU):
                if c % 2 == 0 and c > 0 and c // 2 + 1 < NWB:
                    low(c // 2 + 1)
                for b in range(3):
                    dve.wait_ge(s_done, 3 * c + b + 1)
                    if b < 2:
                        nc.vector.tensor_copy(s_sb[:, 3 * b:3 * b + 3, c, :], psc[b][:, 0:3 * P].rearrange("p (t n) -> p t n", n=P)
                                              ).then_inc(s_stored, 1)
                    else:
                        nc.vector.tensor_copy(s_sb[:, 6:8, c, :], psc[b][:, 0:2 * P].rearrange("p (t n) -> p t n", n=P))
                        nc.vector.tensor_copy(s_sb[0:TS, NTP, c, :], psc[b][0:TS, 2 * P:3 * P]).then_inc(s_stored, 1)


NEG = -3.0e38
TPAD = NT * P


def peer_topk(nc, s_sb, sel_t):
    with ExitStack() as ctx:
        def sb(name, shape, dt=F32):
            return ctx.enter_context(nc.sbuf_tensor("tk_" + name, shape, dt))

        def sem(name):
            return new_sem(nc, "tk_" + name)

        K2 = TOPK * TOPK
        w1 = [sb("w1", [P, NU, NK])]
        w2 = sb("w2", [P, NU, NK])
        top = sb("top", [P, PH, 2, TOPK])
        idx = sb("idx", [P, PH, 2, TOPK], U32)
        idxf = sb("idxf", [P, PH, 2, TOPK])
        cand = sb("cand", [P, PH, K2])
        cand2 = w1[0][:].rearrange("p u k -> p (u k)").rearrange("p (h k) -> p h k", k=K2)
        fin = sb("fin", [P, PH, TOPK])
        pos = sb("pos", [P, PH, TOPK], U32)
        pos2 = sb("pos2", [P, 2, PH, TOPK], U32)
        posf = sb("posf", [P, 2, PH, TOPK])
        iota = sb("iota", [P, TOPK])
        oh = [x.rearrange("p (s m) -> p s m", m=TOPK) for x in (
            w2[:].rearrange("p u k -> p (u k)"), cand[:].rearrange("p h k -> p (h k)"))]
        res = sb("res", [P, 3, PH, TOPK])
        ex = sb("ex", [P, PH, TOPK])
        sums = sb("sums", [P, PH])
        ident = sb("ident", [P, P])
        pt = ctx.enter_context(nc.psum_tensor("tk_pt", [P, 4, P], F32))
        zeroed, shaped = sem("zeroed"), sem("shaped")
        step, passed, ex_in, ex_out = sem("step"), sem("passed"), sem("ex_in"), sem("ex_out")
        res_ready = sem("res_ready")
        turned, stored = sem("turned"), sem("stored")
        block = ctx.enter_context(nc.Block())

        @block.gpsimd
        def _(pool):
            nc.gpsimd.memset(ident[:], 0.0).then_inc(zeroed, 1)
            pool.wait_ge(zeroed, 1)
            nc.gpsimd.affine_select(out=ident[:], in_=ident[:], compare_op=ALU.not_equal, fill=1.0, base=0,
                                    pattern=[[-1, P]], channel_multiplier=1).then_inc(shaped, 1)
            nc.gpsimd.iota(iota[:], [[1, TOPK]], base=0, channel_multiplier=0,
                           allow_small_or_imprecise_dtypes=True).then_inc(shaped, 1)

        @block.scalar
        def _(act):
            act.sem_inc(stored, 1)
            with act.Fori(0, NT) as t:
                act.wait_ge(ex_in, t + 1)
                nc.scalar.activation(ex[:], ex[:], ACT.Exp).then_inc(ex_out, 1)
                act.wait_ge(turned, t + 2)
                nc.scalar.activation(sel_t[:, :, bass.ds(t * P, P)], pt[:, 0:3, :], ACT.Copy).then_inc(stored, 1)

        @block.tensor
        def _(pe):
            pe.sem_inc(turned, 1)
            pe.wait_ge(shaped, 1)
            with pe.Fori(0, NT) as t:
                pe.wait_ge(res_ready, t + 1)
                pe.wait_ge(stored, t + 1)
                for i in range(3):
                    mm = nc.tensor.transpose(pt[:, i, :], res[:, i].rearrange("p h k -> p (h k)"), ident[:])
                mm.then_inc(turned, 1)

        @block.vector
        def _(dve):
            dve.wait_ge(shaped, 2)
            with dve.Fori(0, NT) as t:
                n = [0]
                TOTAL = STEPS_TOPK

                def did(ins):
                    ins.then_inc(step, 1)
                    n[0] += 1

                def settle():
                    dve.wait_ge(step, t * TOTAL + n[0])
                    dve.sem_inc(passed, 1)

                v = nc.vector
                did(v.tensor_copy(w1[0][:], s_sb[:, bass.ds(t, 1)].rearrange("p o u k -> p (o u) k")))
                settle()
                units = [(h, i) for h in range(PH) for i in range(2)]

                def key(a, u):
                    return a[:, 2 * u[0] + u[1], :]

                for u in units:
                    did(v.max(top[:, u[0], u[1], 0:8], key(w1[0], u)))
                settle()
                for u in units:
                    did(v.max_index(idx[:, u[0], u[1], 0:8], top[:, u[0], u[1], 0:8], key(w1[0], u)))
                    did(v.match_replace(key(w2, u), top[:, u[0], u[1], 0:8], key(w1[0], u), NEG))
                settle()
                for u in units:
                    did(v.max(top[:, u[0], u[1], 8:16], key(w2, u)))
                settle()
                for u in units:
                    did(v.max_index(idx[:, u[0], u[1], 8:16], top[:, u[0], u[1], 8:16], key(w2, u)))
                did(v.tensor_tensor(cand[:].rearrange("p h (a b) -> p h a b", b=TOPK),
                                    top[:, :, 0, :].unsqueeze(3).broadcast_to([P, PH, TOPK, TOPK]),
                                    top[:, :, 1, :].unsqueeze(2).broadcast_to([P, PH, TOPK, TOPK]), ALU.add))
                settle()
                did(v.tensor_copy(idxf[:], idx[:]))
                for h in range(PH):
                    did(v.max(fin[:, h, 0:8], cand[:, h]))
                settle()
                for h in range(PH):
                    did(v.max_index(pos[:, h, 0:8], fin[:, h, 0:8], cand[:, h]))
                    did(v.match_replace(cand2[:, h], fin[:, h, 0:8], cand[:, h], NEG))
                settle()
                for h in range(PH):
                    did(v.max(fin[:, h, 8:16], cand2[:, h]))
                settle()
                for h in range(PH):
                    did(v.max_index(pos[:, h, 8:16], fin[:, h, 8:16], cand2[:, h]))
                did(v.tensor_tensor(ex[:], fin[:], fin[:, :, 0:1].broadcast_to([P, PH, TOPK]), ALU.subtract))
                settle()
                dve.sem_inc(ex_in, 1)
                did(v.tensor_scalar(pos2[:, 0], pos[:], 4, None, ALU.logical_shift_right))
                did(v.tensor_scalar(pos2[:, 1], pos[:], TOPK - 1, None, ALU.bitwise_and))
                settle()
                did(v.tensor_copy(posf[:], pos2[:]))
                settle()
                for i in range(2):
                    did(v.tensor_tensor(oh[i], iota[:].unsqueeze(1).broadcast_to([P, PH * TOPK, TOPK]),
                                        posf[:, i].rearrange("p h k -> p (h k)").unsqueeze(2)
                                        .broadcast_to([P, PH * TOPK, TOPK]), ALU.is_equal))
                settle()
                for i in range(2):
                    o4 = oh[i].rearrange("p (h k) m -> p h k m", k=TOPK)
                    did(v.tensor_tensor(o4, o4, idxf[:, :, i, :].unsqueeze(2).broadcast_to([P, PH, TOPK, TOPK]), ALU.mult))
                settle()
                dve.wait_ge(turned, t + 1)
                for i in range(2):
                    did(v.tensor_reduce(res[:, i].rearrange("p h k -> p (h k)"), oh[i], AX.X, ALU.add))
                dve.wait_ge(ex_out, t + 1)
                did(v.tensor_reduce(sums[:], ex[:], AX.X, ALU.add))
                settle()
                did(v.reciprocal(sums[:], sums[:]))
                settle()
                v.tensor_tensor(res[:, 2], ex[:], sums[:].unsqueeze(2).broadcast_to([P, PH, TOPK]), ALU.mult
                                ).then_inc(res_ready, 1)
                dve.wait_ge(res_ready, t + 1)
                assert n[0] == TOTAL, n[0]


STEPS_TOPK = 1 + 16 + 32 + 16 + 16 + 1 + 1 + 8 + 16 + 8 + 8 + 1 + 2 + 1 + 2 + 2 + 2 + 1 + 1


def peer_gates(nc, sel_t, w_d):
    with ExitStack() as ctx:
        def sb(name, shape, dt=F32):
            return ctx.enter_context(nc.sbuf_tensor("pg_" + name, shape, dt))

        def sem(name):
            return new_sem(nc, "pg_" + name)

        NBK = 2
        NB = 4 * NBK
        CH = WCH
        NI = CH // NB
        NO = T // (2 * CH)
        iota = sb("iota", [P, P])
        hot_i = sb("hot_i", [P, NB, P])
        hot_j = sb("hot_j", [P, NB, P])
        wb = sb("wb", [P, 2, NK, CH])
        pw = [ctx.enter_context(nc.psum_tensor(f"pg_pw{b}", [P, 4, P], F32)) for b in range(NBK)]
        shaped, hot = sem("shaped"), sem("hot")
        made, stored = sem("made"), sem("stored")
        wrote = [sem(f"wrote{b}") for b in range(2)]
        block = ctx.enter_context(nc.Block())

        @block.gpsimd
        def _(pool):
            nc.gpsimd.iota(iota[:], [[1, P]], base=0, channel_multiplier=0,
                           allow_small_or_imprecise_dtypes=True).then_inc(shaped, 1)

        @block.sync
        def _(sp):
            with sp.Fori(0, NO) as o:
                for b2 in range(2):
                    sp.wait_ge(stored, (o * 2 + b2 + 1) * (NI * NBK) + NBK)
                    sp.dma_start(w_d[:, :, bass.ds((o * 2 + b2) * CH, CH)].rearrange("i j t -> j i t"),
                                 wb[:, b2]).then_inc(wrote[b2], 16)
            for b2 in range(2):
                sp.wait_ge(wrote[b2], 16 * NO + 16)

        @block.vector
        def _(dve):
            dve.wait_ge(shaped, 1)
            with dve.Fori(0, T // NB) as i:
                for b in range(NBK):
                    dve.wait_ge(made, i * NBK + b + 1)
                    for j in range(4 * b, 4 * b + 4):
                        tok = bass.ds(i * NB + j, 1)
                        nc.vector.tensor_scalar(hot_i[:, j, :], iota[:], sel_t[:, 0, tok], sel_t[:, 2, tok],
                                                ALU.is_equal, ALU.mult)
                        ins = nc.vector.tensor_scalar(hot_j[:, j, :], iota[:], sel_t[:, 1, tok], None, ALU.is_equal)
                    ins.then_inc(hot, 1)

        @block.tensor
        def _(pe):
            pe.sem_inc(made, NBK)
            with pe.Fori(0, T // NB) as i:
                for b in range(NBK):
                    pe.wait_ge(hot, i * NBK + b + 1)
                    pe.wait_ge(stored, i * NBK + b + 1)
                    for j in range(4 * b, 4 * b + 4):
                        mm = nc.tensor.matmul(pw[b][:, j % 4, :], hot_j[:, j, :], hot_i[:, j, :], start=True, stop=True)
                    mm.then_inc(made, 1)

        @block.scalar
        def _(act):
            act.sem_inc(stored, NBK)
            for b2 in range(2):
                act.sem_inc(wrote[b2], 16)
            with act.Fori(0, NO) as o:
                for b2 in range(2):
                    act.wait_ge(wrote[b2], o * 16 + 16)
                    with act.Fori(0, NI) as i:
                        for b in range(NBK):
                            act.wait_ge(made, ((o * 2 + b2) * NI + i) * NBK + b + 1 + NBK)
                            nc.scalar.activation(wb[:, b2, :, bass.ds(i * NB + 4 * b, 4)].rearrange("p i t -> p t i"),
                                                 pw[b][:], ACT.Copy).then_inc(stored, 1)


WCH = T // 12


def split_h(nc, h_t, h_hi, h_lo):
    with ExitStack() as ctx:
        hi_done = new_sem(nc, "sh_hi")
        block = ctx.enter_context(nc.Block())

        @block.scalar
        def _(act):
            for k in range(KD):
                nc.scalar.activation(h_hi[:, k], h_t[:, k], ACT.Copy).then_inc(hi_done, 1)

        @block.vector
        def _(dve):
            for k in range(KD):
                dve.wait_ge(hi_done, k + 1)
                nc.vector.tensor_tensor(h_lo[:, k], h_t[:, k], h_hi[:, k].bitcast(F32), ALU.subtract)


def peer_experts(nc, u_d, v_d, w_d, h_hi, h_lo, acc_t):
    with ExitStack() as ctx:
        def sb(name, shape, dt=F32):
            return ctx.enter_context(nc.sbuf_tensor("pe_" + name, shape, dt))

        def sem(name):
            return new_sem(nc, "pe_" + name)

        NG = 2
        E2 = 2 * NG
        NIT = NK // E2
        OB = 3 * KD
        u_sb = [sb(f"u{b}", [P, D]) for b in range(2)]
        v_sb = [sb(f"v{b}", [P, D]) for b in range(2)]
        w_sb = [sb(f"w{b}", [P, T]) for b in range(2)]
        a_sb = [sb(f"a{b}", [P, NW]) for b in range(2)]
        ut = [[sb(f"ut{b}{x}", [P, KD, P], F32R) for x in "hl"] for b in range(2)]
        vx = [[sb(f"vx{b}{x}", [P, D], F32R) for x in "hl"] for b in range(E2)]
        wx = [[sb(f"wx{b}{x}", [P, T], F32R) for x in "hl"] for b in range(E2)]
        ident = sb("ident", [P, P])
        pa = [ctx.enter_context(nc.psum_tensor(f"pe_pa{b}", [P, W4], F32)) for b in range(3)]
        pt = [ctx.enter_context(nc.psum_tensor(f"pe_pt{b}", [P, W4], F32)) for b in range(2)]
        po = [ctx.enter_context(nc.psum_tensor(f"pe_po{b}", [P, W4], F32)) for b in range(3)]
        zeroed, shaped = sem("zeroed"), sem("shaped")
        u_in = [sem(f"u_in{b}") for b in range(2)]
        v_in = [sem(f"v_in{b}") for b in range(2)]
        w_in = [sem(f"w_in{b}") for b in range(2)]
        turned, TURNED0 = sem("turned"), 4
        ut_hi = sem("ut_hi")
        ut_lo, UT0 = sem("ut_lo"), 2
        v_hi = sem("v_hi")
        v_lo, V0 = sem("v_lo"), 2
        a_done, ADONE0 = sem("a_done"), 6
        a_act, AACT0 = sem("a_act"), 3
        a_mul, AMUL0 = sem("a_mul"), 2
        w_hi = sem("w_hi")
        w_lo, W0 = sem("w_lo"), 6
        o_done, ODONE0 = sem("o_done"), 2 * OB
        o_added, OADD0 = sem("o_added"), OB
        block = ctx.enter_context(nc.Block())

        def rounds(eng, first, ups, downs):
            first()
            ups(0, 0, False)
            with eng.Fori(0, NIT - 1) as i:
                ups(i, 1, False)
                downs(i, 0)
                ups(i + 1, 0, False)
                downs(i, 1)
            ups(NIT - 1, 1, True)
            downs(NIT - 1, 0)
            downs(NIT - 1, 1)

        @block.gpsimd
        def _(pool):
            nc.gpsimd.memset(ident[:], 0.0).then_inc(zeroed, 1)
            nc.gpsimd.memset(acc_t[:], 0.0).then_inc(shaped, 1)
            pool.wait_ge(zeroed, 1)
            nc.gpsimd.affine_select(out=ident[:], in_=ident[:], compare_op=ALU.not_equal, fill=1.0, base=0,
                                    pattern=[[-1, P]], channel_multiplier=1).then_inc(shaped, 1)
            with pool.Fori(0, NIT) as i:
                for e in range(E2):
                    n = i * E2 + e
                    pool.wait_ge(w_lo, (n - 1) * 3 + W0)
                    pool.dma_start(w_sb[e % 2][:], w_d[bass.ds(n, 1)].rearrange("o j t -> j (o t)")
                                   ).then_inc(w_in[e % 2], 16)

        @block.sync
        def _(sp):
            with sp.Fori(0, NIT) as i:
                for e in range(E2):
                    n = i * E2 + e
                    experts = bass.ds(n * NK, NK)
                    sp.wait_ge(turned, (n - 1) * 2 + TURNED0)
                    sp.dma_start(u_sb[e % 2][:], u_d[experts, :]).then_inc(u_in[e % 2], 16)
                    sp.wait_ge(v_lo, n - 1 + V0)
                    sp.dma_start(v_sb[e % 2][:], v_d[experts, :]).then_inc(v_in[e % 2], 16)

        @block.tensor
        def _(pe):
            pe.sem_inc(turned, TURNED0)
            pe.sem_inc(a_done, ADONE0)
            pe.sem_inc(o_done, ODONE0)
            pe.wait_ge(shaped, 2)

            def turn(i, e, half):
                n = i * E2 + e
                if half == 0:
                    pe.wait_ge(u_in[e % 2], (i * (E2 // 2) + e // 2 + 1) * 16)
                pe.wait_ge(ut_lo, (n - 1) * 2 + half + 1 + UT0)
                for k in range(4):
                    c = (4 * half + k) * P
                    mm = nc.tensor.transpose(pt[half][:, k * P:(k + 1) * P], u_sb[e % 2][:, c:c + P], ident[:])
                mm.then_inc(turned, 1)

            def ups(i, g, last):
                for e in range(g * NG, g * NG + NG):
                    n = i * E2 + e
                    for c in range(3):
                        if c >= 1 and not (last and e == E2 - 1):
                            turn(i + (e + 1) // E2, (e + 1) % E2, c - 1)
                        if c == 0:
                            pe.wait_ge(ut_lo, n * 2 + 2 + UT0)
                        pe.wait_ge(a_act, (n - 1) * 3 + c + 1 + AACT0)
                        steps = [(x, y, k) for x, y in PARTS for k in range(KD)]
                        for s, (x, y, k) in enumerate(steps):
                            mm = nc.tensor.matmul(pa[c][:, 0:NW], ut[e % 2][x][:, k, :],
                                                  (h_hi, h_lo)[y][:, k, c * NW:(c + 1) * NW],
                                                  start=(s == 0), stop=(s == len(steps) - 1))
                        mm.then_inc(a_done, 1)

            def downs(i, g):
                pe.wait_ge(v_lo, i * E2 + (g + 1) * NG + V0)
                pe.wait_ge(w_lo, (i * E2 + (g + 1) * NG) * 3 + W0)
                for o in range(OB):
                    k, c = o // 3, o % 3
                    pe.wait_ge(o_added, (i * 2 + g) * OB + o - 2 + OADD0)
                    steps = [(e, x, y) for e in range(g * NG, g * NG + NG) for x, y in PARTS]
                    for s, (e, x, y) in enumerate(steps):
                        mm = nc.tensor.matmul(po[o % 3][:, 0:NW], vx[e][x][:, k * P:(k + 1) * P],
                                              wx[e][y][:, c * NW:(c + 1) * NW],
                                              start=(s == 0), stop=(s == len(steps) - 1))
                    mm.then_inc(o_done, 1)

            def first():
                turn(0, 0, 0)
                turn(0, 0, 1)

            rounds(pe, first, ups, downs)

        @block.scalar
        def _(act):
            act.sem_inc(a_act, AACT0)

            def high_u(i, e, half):
                n = i * E2 + e
                act.wait_ge(a_done, (n - 1) * 3 + ADONE0)
                act.wait_ge(turned, n * 2 + half + 1 + TURNED0)
                nc.scalar.activation(ut[e % 2][0][:, 4 * half:4 * half + 4, :],
                                     pt[half][:].rearrange("p (k s) -> p k s", k=4), ACT.Copy).then_inc(ut_hi, 1)

            def ups(i, g, last):
                for e in range(g * NG, g * NG + NG):
                    n = i * E2 + e
                    for c in range(3):
                        m = n * 3 + c
                        act.wait_ge(a_done, m + 1 + ADONE0)
                        act.wait_ge(a_mul, m - 1 + AMUL0)
                        nc.scalar.activation(a_sb[(3 * e + c) % 2][:], pa[c][:, 0:NW], ACT.Gelu_apprx_tanh
                                             ).then_inc(a_act, 1)
                        if c >= 1 and not (last and e == E2 - 1):
                            high_u(i + (e + 1) // E2, (e + 1) % E2, c - 1)
                        if c == 0:
                            act.wait_ge(v_in[e % 2], (i * (E2 // 2) + e // 2 + 1) * 16)
                            act.wait_ge(o_done, (i * 2 - 2 + e // NG + 1) * OB + ODONE0)
                            nc.scalar.activation(vx[e][0][:], v_sb[e % 2][:], ACT.Copy).then_inc(v_hi, 1)
                        act.wait_ge(a_mul, m + 1 + AMUL0)
                        nc.scalar.activation(wx[e][0][:, c * NW:(c + 1) * NW], w_sb[e % 2][:, c * NW:(c + 1) * NW],
                                             ACT.Copy).then_inc(w_hi, 1)

            def first():
                high_u(0, 0, 0)
                high_u(0, 0, 1)

            rounds(act, first, ups, lambda i, g: None)

        @block.vector
        def _(dve):
            dve.sem_inc(ut_lo, UT0)
            dve.sem_inc(v_lo, V0)
            dve.sem_inc(a_mul, AMUL0)
            dve.sem_inc(w_lo, W0)
            dve.sem_inc(o_added, OADD0)
            dve.wait_ge(shaped, 2)

            def low_u(i, e, half):
                k = slice(4 * half, 4 * half + 4)
                dve.wait_ge(ut_hi, (i * E2 + e) * 2 + half + 1)
                nc.vector.tensor_tensor(ut[e % 2][1][:, k, :], pt[half][:].rearrange("p (k s) -> p k s", k=4),
                                        ut[e % 2][0][:, k, :].bitcast(F32), ALU.subtract).then_inc(ut_lo, 1)

            def ups(i, g, last):
                for e in range(g * NG, g * NG + NG):
                    n = i * E2 + e
                    for c in range(3):
                        tok = slice(c * NW, (c + 1) * NW)
                        w = w_sb[e % 2][:, tok]
                        if c == 0:
                            dve.wait_ge(w_in[e % 2], (i * (E2 // 2) + e // 2 + 1) * 16)
                        dve.wait_ge(a_act, n * 3 + c + 1 + AACT0)
                        nc.vector.tensor_tensor(w, w, a_sb[(3 * e + c) % 2][:], ALU.mult).then_inc(a_mul, 1)
                        if c >= 1 and not (last and e == E2 - 1):
                            low_u(i + (e + 1) // E2, (e + 1) % E2, c - 1)
                        if c == 0:
                            dve.wait_ge(v_hi, n + 1)
                            nc.vector.tensor_tensor(vx[e][1][:], v_sb[e % 2][:], vx[e][0][:].bitcast(F32),
                                                    ALU.subtract).then_inc(v_lo, 1)
                        dve.wait_ge(w_hi, n * 3 + c + 1)
                        nc.vector.tensor_tensor(wx[e][1][:, tok], w, wx[e][0][:, tok].bitcast(F32),
                                                ALU.subtract).then_inc(w_lo, 1)

            def downs(i, g):
                for o in range(OB):
                    m = (i * 2 + g) * OB + o
                    out = acc_t[:, o // 3, (o % 3) * NW:(o % 3 + 1) * NW]
                    dve.wait_ge(o_done, m + 1 + ODONE0)
                    dve.wait_ge(o_added, m - OB + 1 + OADD0)
                    nc.vector.tensor_tensor(out, po[o % 3][:, 0:NW], out, ALU.add).then_inc(o_added, 1)

            def first():
                low_u(0, 0, 0)
                low_u(0, 0, 1)

            rounds(dve, first, ups, downs)


def finish(nc, final_norm, x2_tiles, acc_t, y_tiles):
    with ExitStack() as ctx:
        def sb(name, shape, dt=F32):
            return ctx.enter_context(nc.sbuf_tensor("fn_" + name, shape, dt))

        def sem(name):
            return new_sem(nc, "fn_" + name)

        gain = sb("gain", [P, D])
        x = [sb(f"x{t}", [P, D]) for t in range(NT)]
        sq = sb("sq", [P, D])
        ident = sb("ident", [P, P])
        ss, rinv, rstd = sb("ss", [P, NT]), sb("rinv", [P, NT]), sb("rstd", [P, NT])
        pt = [ctx.enter_context(nc.psum_tensor(f"fn_pt{b}", [P, W4], F32)) for b in range(4)]
        gain_loaded = sem("gain_loaded")
        x_loaded = [sem(f"x_loaded{t}") for t in range(NT)]
        zeroed, shaped = sem("zeroed"), sem("shaped")
        turned, added, summed, meaned, inverted, rooted, scaled, ready, stored = (sem(n) for n in (
            "turned", "added", "summed", "meaned", "inverted", "rooted", "scaled", "ready", "stored"))
        block = ctx.enter_context(nc.Block())

        @block.sync
        def _(sp):
            sp.dma_start(gain[:], final_norm.rearrange("(o d) -> o d", o=1).broadcast_to([P, D])).then_inc(gain_loaded, 16)
            for t in range(NT):
                sp.dma_start(x[t][0:rows(t)], x2_tiles[t]).then_inc(x_loaded[t], 16)
            for t in range(NT):
                sp.wait_ge(ready, t + 1)
                sp.dma_start(y_tiles[t], x[t][0:rows(t)]).then_inc(stored, 16)
            sp.wait_ge(stored, 16 * NT)

        @block.gpsimd
        def _(pool):
            nc.gpsimd.memset(ident[:], 0.0).then_inc(zeroed, 1)
            pool.wait_ge(zeroed, 1)
            nc.gpsimd.affine_select(out=ident[:], in_=ident[:], compare_op=ALU.not_equal, fill=1.0, base=0,
                                    pattern=[[-1, P]], channel_multiplier=1).then_inc(shaped, 1)

        @block.tensor
        def _(pe):
            pe.wait_ge(shaped, 1)
            for t in range(NT):
                r = rows(t)
                for half in range(2):
                    if t >= 2:
                        pe.wait_ge(added, 2 * (t - 2) + half + 1)
                    for k in range(4):
                        mm = nc.tensor.transpose(pt[2 * (t % 2) + half][0:r, k * P:(k + 1) * P],
                                                 acc_t[:, 4 * half + k, t * P:t * P + r], ident[:])
                    mm.then_inc(turned, 1)

        @block.scalar
        def _(act):
            def scale(t):
                r = rows(t)
                act.wait_ge(inverted, t + 1)
                nc.scalar.activation(rstd[0:r, t:t + 1], rinv[0:r, t:t + 1], ACT.Sqrt).then_inc(rooted, 1)
                act.wait_ge(rooted, t + 1)
                nc.scalar.activation(x[t][0:r], x[t][0:r], ACT.Copy, scale=rstd[0:r, t:t + 1]).then_inc(scaled, 1)

            for t in range(NT):
                r = rows(t)
                act.wait_ge(added, 2 * t + 2)
                if t >= 1:
                    act.wait_ge(summed, t)
                nc.scalar.activation(sq[0:r], x[t][0:r], ACT.Square, accum_out=ss[0:r, t:t + 1]).then_inc(summed, 1)
                if t >= 1:
                    scale(t - 1)
            scale(NT - 1)

        @block.vector
        def _(dve):
            dve.wait_ge(gain_loaded, 16)
            for t in range(NT + 2):
                if t < NT:
                    r = rows(t)
                    dve.wait_ge(x_loaded[t], 16)
                    for half in range(2):
                        dve.wait_ge(turned, 2 * t + half + 1)
                        xs = x[t][0:r, half * W4:(half + 1) * W4]
                        nc.vector.tensor_tensor(xs, xs, pt[2 * (t % 2) + half][0:r, :], ALU.add).then_inc(added, 1)
                if 1 <= t <= NT:
                    r = rows(t - 1)
                    dve.wait_ge(summed, t)
                    nc.vector.tensor_scalar(ss[0:r, t - 1:t], ss[0:r, t - 1:t], 1.0 / D, EPS, ALU.mult, ALU.add
                                            ).then_inc(meaned, 1)
                    dve.wait_ge(meaned, t)
                    nc.vector.reciprocal(rinv[0:r, t - 1:t], ss[0:r, t - 1:t]).then_inc(inverted, 1)
                if t >= 2:
                    r = rows(t - 2)
                    xs = x[t - 2][0:r]
                    dve.wait_ge(scaled, t - 1)
                    nc.vector.tensor_tensor(xs, xs, gain[0:r], ALU.mult).then_inc(ready, 1)


class Tables:

    def __init__(self, ctx, nc):
        def sb(name, shape):
            return ctx.enter_context(nc.sbuf_tensor("tab_" + name, shape, F32))

        self.cm = sb("cm", [P, GP, 2, 2, P])
        self.tp = sb("tp", [P, G, P])
        self.bm = sb("bm", [P, GP, 2, P])
        self.w = sb("w", [P, 2, GP, NM + 1])
        self.r8 = sb("r8", [P, GP])
        self.a4 = sb("a4", [P, 2, GP])


def mixers(nc, A, O, x_tiles, x2_tiles, stop):
    with ExitStack() as ctx:
        o_t = ctx.enter_context(nc.sbuf_tensor("o_t", [P, KD, T], F32))
        u_sb = ctx.enter_context(nc.sbuf_tensor("u_sb", [P, G, SC, GCH], F32))
        us_nat = ctx.enter_context(nc.sbuf_tensor("us_nat", [TS, W4], F32))
        with ExitStack() as c2:
            def sb(name, shape):
                return c2.enter_context(nc.sbuf_tensor(name, shape, F32))

            qk_t = sb("qk_t", [P, 4, T])
            la_t = sb("la_t", [P, 2, T])
            v_sb = sb("v_sb", [P, NT, W4])
            g_sb = sb("g_sb", [P, NT, W4])
            fac = sb("fac", [P, 3, 2, SEQ // GC])
            fac_s = sb("fac_s", [P, 2, NSEQ])
            with nc.sbuf_tensor("h_t", [P, KD, T], F32) as h_t:
                norm_transpose(nc, "n1_", x_tiles, A["norm1"][0], h_t)
                project(nc, A["w_in"][0], A["w_a2"][0], A["b_a2"][0], h_t, qk_t, la_t, v_sb, g_sb, u_sb, us_nat)
            qz = sb("qz", [P, H, T])
            gla_decays(nc, qk_t, la_t, qz, fac, fac_s)
            gla(nc, qk_t, qz, v_sb, g_sb, fac, fac_s, A["gla_norm"][0], A["state_gla"][0], O[2][0, 0], O[5][0], o_t)
        with ExitStack() as c2:
            tab = Tables(c2, nc)
            s5_tables(nc, A, tab)
            x_g = c2.enter_context(nc.sbuf_tensor("x_g", [P, G, NMS], F32))
            s_all = c2.enter_context(nc.sbuf_tensor("s_all", [P, 2, GP, NM + 1], F32))
            s0 = c2.enter_context(nc.sbuf_tensor("s0", [P, 2, NSEQ, GP], F32))
            s5_scan(nc, A, tab, u_sb, us_nat, x_g, s_all, s0, O[3][0, 0], O[4][0, 0], O[6][0], O[7][0])
            s5_outputs(nc, A, tab, u_sb, x_g, s_all, s0, o_t)
        mix_out(nc, A["w_out"][0], o_t, x_tiles, x2_tiles)


def build(nc, A, O, stop=99):
    def tiles(prompt, sample):
        return [prompt[0, t * P:(t + 1) * P, :] for t in range(NTP)] + [sample.rearrange("s j d -> (s j) d")]

    LIVE_SEMS.clear()
    x2_d = nc.dram_tensor("x2_d", [NT * P, D], F32).ap()
    w_d = nc.dram_tensor("w_d", [NK, NK, T], F32).ap()
    x2_tiles = [x2_d[t * P:t * P + rows(t), :] for t in range(NT)]
    with nc.allow_non_contiguous_dma(reason="biases and S5 parameters, a few kilobytes"):
        mixers(nc, A, O, tiles(A["x_prompt"], A["x_sample"]), x2_tiles, stop)
        clear_sems(nc)
        if stop <= 4:
            return
        with ExitStack() as ctx:
            h_hi = ctx.enter_context(nc.sbuf_tensor("h_hi", [P, KD, T], F32R))
            h_lo = ctx.enter_context(nc.sbuf_tensor("h_lo", [P, KD, T], F32R))
            with nc.sbuf_tensor("h2_t", [P, KD, T], F32) as h_t:
                norm_transpose(nc, "n2_", x2_tiles, A["norm2"][0], h_t)
                split_h(nc, h_t, h_hi, h_lo)
            with ExitStack() as c2:
                s_sb = c2.enter_context(nc.sbuf_tensor("s_sb", [P, NT, NU, NK], F32))
                peer_scores(nc, A["peer_wq"][0], A["peer_keys"][0], h_hi, h_lo, s_sb)
                c_sel = ctx.enter_context(ExitStack())
                sel_t = c_sel.enter_context(nc.sbuf_tensor("sel_t", [P, 3, TPAD], F32, side="right"))
                peer_topk(nc, s_sb, sel_t)
            peer_gates(nc, sel_t, w_d)
            c_sel.close()
            if stop <= 5:
                return
            acc_t = ctx.enter_context(nc.sbuf_tensor("acc_t", [P, KD, T], F32))
            peer_experts(nc, A["peer_u"][0], A["peer_v"][0], w_d, h_hi, h_lo, acc_t)
            finish(nc, A["final_norm"], x2_tiles, acc_t, tiles(O[0], O[1]))


_INS = ['x_prompt', 'x_sample', 'state_gla', 'state_s5_re', 'state_s5_im', 'norm1', 'w_in', 'w_a2', 'b_a2', 'gla_norm',
        's5_lam_re', 's5_lam_im', 's5_log_dt', 's5_b_re', 's5_b_im', 's5_c_re', 's5_c_im', 's5_d', 'w_glu', 'b_glu',
        'w_out', 'norm2', 'peer_wq', 'peer_keys', 'peer_u', 'peer_v', 'final_norm']
_OUTS = [(1, SEQ, D), (NSEQ, SLEN, D), (1, 1, H, DK, DV), (1, 1, G, ST), (1, 1, G, ST),
         (1, NSEQ, H, DK, DV), (1, NSEQ, G, ST), (1, NSEQ, G, ST)]


def kernel(**inputs):
    import numpy as _np
    import concourse.bacc as _bacc
    from concourse.bass_utils import run_bass_kernel_spmd as _run

    nc = _bacc.Bacc("TRN2", target_bir_lowering=False, num_devices=1)
    arrays, args = {}, {}
    for name in _INS:
        a = _np.ascontiguousarray(inputs[name])
        arrays[f"in_{name}_dram"] = a
        args[name] = nc.dram_tensor(f"in_{name}_dram", a.shape, F32, kind="ExternalInput").ap()
    outs = [nc.dram_tensor(f"out_{i}_dram", shape, F32, kind="ExternalOutput").ap() for i, shape in enumerate(_OUTS)]
    build(nc, args, outs)
    r = _run(nc, [arrays], core_ids=[0])
    return tuple(r.results[0][f"out_{i}_dram"] for i in range(len(_OUTS)))
```

```python
from contextlib import ExitStack

import concourse.bass as bass
from concourse import mybir

ALU = mybir.AluOpType
ACT = mybir.ActivationFunctionType
AX = mybir.AxisListType
F32 = mybir.dt.float32
F32R = mybir.dt.float32r
U32 = mybir.dt.uint32

P = 128
D = 1024
KD = D // P
SEQ = 1024
NSEQ, SLEN = 8, 4
TS = NSEQ * SLEN
T = SEQ + TS
NTP = SEQ // P
NT = NTP + 1
NW = T // 3
H, DK, DV = 4, 64, 128
GC = 64
RANK = 16
TAU = 16.0
G, GCH, ST = 32, 16, 64
GP = G // 2
SC = 8
NM = SEQ // SC
NMS = NM + NSEQ
W4 = 512
EPS = 1e-6
NK = 128
PH = 8
TOPK = 16
NE = NK * NK
QC, KC, VC, GTC, AC, UC = 0, 256, 512, 1024, 1536, 1552


def rows(t):
    return P if t < NTP else TS


LIVE_SEMS = []


def new_sem(nc, name):
    LIVE_SEMS.append(nc.alloc_semaphore(name))
    return LIVE_SEMS[-1]


def clear_sems(nc):
    nc.clear_and_free_semaphores(LIVE_SEMS)
    LIVE_SEMS.clear()
    nc.all_engine_barrier()


class Count:

    def __init__(self, sem):
        self.sem, self.n = sem, 0

    def up(self, k=1):
        self.n += k
        return self.n


def norm_transpose(nc, tag, tiles, gain, h_t, preload=None):
    with ExitStack() as ctx:
        def sb(name, shape, dt=F32):
            return ctx.enter_context(nc.sbuf_tensor(tag + name, shape, dt))

        def sem(name):
            return new_sem(nc, tag + name)

        x_sb = [sb(f"x{b}", [P, D]) for b in range(3)]
        hn_sb = [sb(f"hn{b}", [P, D]) for b in range(2)]
        sq = sb("sq", [P, D])
        ss = sb("ss", [P, NT])
        rinv = sb("rinv", [P, NT])
        rstd = sb("rstd", [P, NT])
        gain_sb = sb("gain", [P, KD])
        grow = sb("grow", [KD, P])
        ident = sb("ident", [P, P])
        tp = [ctx.enter_context(nc.psum_tensor(f"{tag}tp{b}", [P, KD // 2, P], F32)) for b in range(4)]
        tg = ctx.enter_context(nc.psum_tensor(f"{tag}tg", [P, KD], F32))
        x_loaded = [sem(f"x_loaded{b}") for b in range(3)]
        gain_loaded = sem("gain_loaded")
        ident_zero, ident_ready = sem("ident_zero"), sem("ident_ready")
        gain_turned, gain_ready = sem("gain_turned"), sem("gain_ready")
        sums, means, stds, normed = sem("sums"), sem("means"), sem("stds"), sem("normed")
        minv = sem("minv")
        turned, stored = sem("turned"), sem("stored")
        block = ctx.enter_context(nc.Block())

        @block.sync
        def _(sp):
            for t in range(NT):
                if t >= 3:
                    sp.wait_ge(normed, t - 2)
                sp.dma_start(x_sb[t % 3][0:rows(t), :], tiles[t]).then_inc(x_loaded[t % 3], 16)
                if t == 0:
                    sp.dma_start(grow[:], gain.rearrange("(k p) -> k p", p=P)).then_inc(gain_loaded, 16)
            if preload is not None:
                sp.dma_start(preload[0], preload[1]).then_inc(preload[2], 16)

        @block.gpsimd
        def _(pool):
            nc.gpsimd.memset(ident[:], 0.0).then_inc(ident_zero, 1)
            pool.wait_ge(ident_zero, 1)
            nc.gpsimd.affine_select(out=ident[:], in_=ident[:], compare_op=ALU.not_equal, fill=1.0, base=0,
                                    pattern=[[-1, P]], channel_multiplier=1).then_inc(ident_ready, 1)

        @block.scalar
        def _(act):
            def square(t):
                r = rows(t)
                act.wait_ge(x_loaded[t % 3], 16 * (t // 3 + 1))
                if t >= 1:
                    act.wait_ge(sums, t)
                nc.scalar.activation(sq[0:r], x_sb[t % 3][0:r], ACT.Square,
                                     accum_out=ss[0:r, t:t + 1]).then_inc(sums, 1)

            square(0)
            for t in range(NT):
                r = rows(t)
                if t + 1 < NT:
                    square(t + 1)
                act.wait_ge(means, t + 1)
                nc.scalar.activation(rstd[0:r, t:t + 1], rinv[0:r, t:t + 1], ACT.Sqrt).then_inc(stds, 1)
                act.wait_ge(stds, t + 1)
                if t >= 2:
                    act.wait_ge(turned, 2 * (t - 1))
                nc.scalar.activation(hn_sb[t % 2][0:r], x_sb[t % 3][0:r], ACT.Copy,
                                     scale=rstd[0:r, t:t + 1]).then_inc(normed, 1)

        @block.tensor
        def _(pe):
            pe.wait_ge(ident_ready, 1)
            pe.wait_ge(gain_loaded, 16)
            nc.tensor.transpose(tg[:], grow[:], ident[0:KD, 0:KD]).then_inc(gain_turned, 1)
            for t in range(NT):
                r = rows(t)
                pe.wait_ge(normed, t + 1)
                for half in range(2):
                    if t >= 2:
                        pe.wait_ge(stored, 2 * (t - 2) + half + 1)
                    for k in range(KD // 2):
                        c = (half * (KD // 2) + k) * P
                        mm = nc.tensor.transpose(tp[2 * (t % 2) + half][:, k, 0:r],
                                                 hn_sb[t % 2][0:r, c:c + P], ident[0:r, 0:r])
                    mm.then_inc(turned, 1)

        @block.vector
        def _(dve):
            dve.wait_ge(gain_turned, 1)
            nc.vector.tensor_copy(gain_sb[:], tg[:]).then_inc(gain_ready, 1)

            def mean(t):
                r = rows(t)
                dve.wait_ge(sums, t + 1)
                nc.vector.tensor_scalar(ss[0:r, t:t + 1], ss[0:r, t:t + 1], 1.0 / D, EPS,
                                        ALU.mult, ALU.add).then_inc(minv, 1)
                dve.wait_ge(minv, t + 1)
                nc.vector.reciprocal(rinv[0:r, t:t + 1], ss[0:r, t:t + 1]).then_inc(means, 1)

            mean(0)
            dve.wait_ge(gain_ready, 1)
            for t in range(NT):
                r = rows(t)
                if t + 1 < NT:
                    mean(t + 1)
                for half in range(2):
                    dve.wait_ge(turned, 2 * t + half + 1)
                    k0 = half * (KD // 2)
                    nc.vector.tensor_tensor(
                        h_t[:, k0:k0 + KD // 2, t * P:t * P + r], tp[2 * (t % 2) + half][:, :, 0:r],
                        gain_sb[:, k0:k0 + KD // 2].unsqueeze(2).broadcast_to([P, KD // 2, r]),
                        ALU.mult).then_inc(stored, 1)


def project(nc, w_in, w_a2, b_a2, h_t, qk_t, la_t, v_sb, g_sb, u_sb, us_nat):
    with ExitStack() as ctx:
        def sem(name):
            return new_sem(nc, "pj_" + name)

        WB = RANK + W4
        wbuf = [ctx.enter_context(nc.sbuf_tensor(f"pj_w{b}", [P, KD, WB], F32)) for b in range(2)]
        alr_t = ctx.enter_context(nc.sbuf_tensor("pj_alr", [RANK, T], F32))
        wa2 = ctx.enter_context(nc.sbuf_tensor("pj_wa2", [RANK, H * DK], F32))
        ba2 = ctx.enter_context(nc.sbuf_tensor("pj_ba2", [P, 2], F32))
        pd = [ctx.enter_context(nc.psum_tensor(f"pj_pd{b}", [P, W4], F32)) for b in range(4)]
        pa = [ctx.enter_context(nc.psum_tensor(f"pj_pa{b}", [P, W4], F32)) for b in range(4)]
        w_loaded = [sem(f"w_loaded{b}") for b in range(2)]
        first_loaded = [sem(f"first_loaded{k}") for k in range(KD)]
        small_loaded = sem("small_loaded")
        d_done, a_done = sem("d_done"), sem("a_done")
        d_read, a_read = sem("d_read"), sem("a_read")
        block = ctx.enter_context(nc.Block())
        w_dram = w_in.rearrange("(k p) c -> p k c", p=P)
        cols = [(QC, W4), (VC, W4), (GTC, W4), (AC, RANK + W4)]

        @block.sync
        def _(sp):
            for k in range(KD):
                sp.dma_start(wbuf[0][:, k, 0:W4], w_dram[:, k, QC:QC + W4]).then_inc(first_loaded[k], 16)
            sp.dma_start(wa2[:], w_a2).then_inc(small_loaded, 16)
            sp.dma_start(ba2[:], b_a2.rearrange("(c p) -> p c", p=P)).then_inc(small_loaded, 16)
            for b, (c, n) in list(enumerate(cols))[1:]:
                if b == 2:
                    sp.wait_ge(d_done, 4 * 3)
                if b == 3:
                    sp.wait_ge(d_done, 4 * 3 + NT)
                sp.dma_start(wbuf[b % 2][:, :, 0:n], w_dram[:, :, c:c + n]).then_inc(w_loaded[b % 2], 16)

        @block.tensor
        def _(pe):
            nd, na = 0, 0

            def transposed(out, w, c, m, n):
                for k in range(KD):
                    mm = nc.tensor.matmul(out, w[:, k, c:c + m], h_t[:, k, n * NW:(n + 1) * NW],
                                          start=(k == 0), stop=(k == KD - 1))
                return mm

            def natural(out, w, c, tok):
                for k in range(KD):
                    mm = nc.tensor.matmul(out, h_t[:, k, tok], w[:, k, c:c + W4],
                                          start=(k == 0), stop=(k == KD - 1))
                return mm

            for k in range(KD):
                pe.wait_ge(first_loaded[k], 16)
                for nd in range(4):
                    mm = nc.tensor.matmul(pd[nd][:, 0:NW], wbuf[0][:, k, nd // 3 * P:(nd // 3 + 1) * P],
                                          h_t[:, k, nd % 3 * NW:(nd % 3 + 1) * NW], start=(k == 0), stop=(k == KD - 1))
                    if k == KD - 1:
                        mm.then_inc(d_done, 1)
            nd = 4
            for c in range(4):
                for n in range(3):
                    if c * 3 + n < 4:
                        continue
                    pe.wait_ge(d_read, nd - 3)
                    mm = transposed(pd[nd % 4][:, 0:NW], wbuf[0], c * P, P, n)
                    mm.then_inc(d_done, 1)
                    nd += 1
            for b in (1, 2):
                pe.wait_ge(w_loaded[b % 2], 16)
                for t in range(NT):
                    out = (pd[nd % 4] if b == 1 else pa[na % 4])
                    if b == 1 and nd >= 4:
                        pe.wait_ge(d_read, nd - 3)
                    if b == 2 and na >= 4:
                        pe.wait_ge(a_read, na - 3)
                    mm = natural(out[0:rows(t), :], wbuf[b % 2], 0, slice(t * P, t * P + rows(t)))
                    if b == 1:
                        mm.then_inc(d_done, 1)
                        nd += 1
                    else:
                        mm.then_inc(a_done, 1)
                        na += 1
            pe.wait_ge(w_loaded[1], 32)
            for n in range(3):
                pe.wait_ge(d_read, nd - 3)
                mm = transposed(pd[nd % 4][0:RANK, 0:NW], wbuf[1], 0, RANK, n)
                mm.then_inc(d_done, 1)
                nd += 1
            for r in range(SC):
                pe.wait_ge(a_read, na - 3)
                mm = natural(pa[na % 4][:, :], wbuf[1], RANK, slice(r, SEQ, SC))
                mm.then_inc(a_done, 1)
                na += 1
            pe.wait_ge(a_read, na - 3)
            mm = natural(pa[na % 4][0:TS, :], wbuf[1], RANK, slice(SEQ, T))
            mm.then_inc(a_done, 1)
            na += 1
            pe.wait_ge(small_loaded, 32)
            pe.wait_ge(d_read, nd)
            for c in range(2):
                for n in range(3):
                    if nd >= 4:
                        pe.wait_ge(d_read, nd - 3)
                    nc.tensor.matmul(pd[nd % 4][:, 0:NW], wa2[:, c * P:(c + 1) * P], alr_t[:, n * NW:(n + 1) * NW],
                                     start=True, stop=True).then_inc(d_done, 1)
                    nd += 1

        @block.vector
        def _(dve):
            nd = 0
            for c in range(4):
                for n in range(3):
                    dve.wait_ge(d_done, nd + 1)
                    nc.vector.tensor_copy(qk_t[:, c, n * NW:(n + 1) * NW], pd[nd % 4][:, 0:NW]).then_inc(d_read, 1)
                    nd += 1
            for t in range(NT):
                dve.wait_ge(d_done, nd + 1)
                nc.vector.tensor_copy(v_sb[0:rows(t), t, :], pd[nd % 4][0:rows(t), :]).then_inc(d_read, 1)
                nd += 1
            for n in range(3):
                dve.wait_ge(d_done, nd + 1)
                nc.vector.tensor_copy(alr_t[:, n * NW:(n + 1) * NW], pd[nd % 4][0:RANK, 0:NW]).then_inc(d_read, 1)
                nd += 1
            dve.wait_ge(small_loaded, 32)
            for c in range(2):
                for n in range(3):
                    dve.wait_ge(d_done, nd + 1)
                    nc.vector.tensor_scalar(la_t[:, c, n * NW:(n + 1) * NW], pd[nd % 4][:, 0:NW],
                                            ba2[:, c:c + 1], None, ALU.add).then_inc(d_read, 1)
                    nd += 1

        @block.scalar
        def _(act):
            na = 0
            for t in range(NT):
                act.wait_ge(a_done, na + 1)
                nc.scalar.activation(g_sb[0:rows(t), t, :], pa[na % 4][0:rows(t), :], ACT.Silu).then_inc(a_read, 1)
                na += 1
            for r in range(SC):
                act.wait_ge(a_done, na + 1)
                nc.scalar.activation(u_sb[:, :, r, :], pa[na % 4][:, :].rearrange("p (g c) -> p g c", g=G), ACT.Copy).then_inc(a_read, 1)
                na += 1
            act.wait_ge(a_done, na + 1)
            nc.scalar.activation(us_nat[:, :], pa[na % 4][0:TS, :], ACT.Copy).then_inc(a_read, 1)


def gla_decays(nc, qk_t, la_t, qz, fac, fac_s):
    with ExitStack() as ctx:
        def sb(name, shape, dt=F32):
            return ctx.enter_context(nc.sbuf_tensor("gd_" + name, shape, dt))

        def sem(name):
            return new_sem(nc, "gd_" + name)

        t1 = sb("t1", [P, 2, T])
        t2 = sb("t2", [P, 2, T])
        eq = sb("eq", [P, 2, T])
        ek = sb("ek", [P, 2, T])
        keep = sb("keep", [P, T])
        df = sb("df", [P, 2, 2, NTP * 2])
        step = sem("step")
        absd, exped, logged = sem("absd"), sem("exped"), sem("logged")
        diffed, factored = sem("diffed"), sem("factored")
        block = ctx.enter_context(nc.Block())
        NCH = SEQ // GC

        @block.vector
        def _(dve):
            s = Count(step)
            for h in range(H):
                other = slice(DK * (1 - h % 2), DK * (1 - h % 2) + DK)
                nc.vector.memset(qz[other, h, :], 0.0)
            nc.vector.memset(keep[:], 1.0).then_inc(step, 1)
            dve.wait_ge(step, s.up())
            nc.vector.memset(keep[:, 0:SEQ:GC], 0.0).then_inc(step, 1)
            nc.vector.memset(keep[:, SEQ:T:SLEN], 0.0).then_inc(step, 1)
            dve.wait_ge(absd, 1)
            nc.vector.tensor_scalar(la_t[:], la_t[:], 0.0, None, ALU.min).then_inc(step, 1)
            dve.wait_ge(logged, 1)
            dve.wait_ge(step, s.up(3))
            nc.vector.tensor_tensor(la_t[:], la_t[:], t2[:], ALU.subtract).then_inc(step, 1)
            dve.wait_ge(step, s.up())
            for c in range(2):
                nc.vector.tensor_tensor_scan(t1[:, c, :], keep[:], la_t[:, c, :], 0.0, ALU.mult, ALU.add).then_inc(step, 1)
            dve.wait_ge(step, s.up(2))
            for c in range(2):
                b = t1[:, c, 0:SEQ].rearrange("p (n s) -> p n s", s=GC)
                mid = b[:, :, GC // 2 - 1:GC // 2]
                end = b[:, :, GC - 1:GC]
                nc.vector.tensor_tensor(t2[:, c, 0:SEQ].rearrange("p (n s) -> p n s", s=GC), b,
                                        mid.broadcast_to([P, NCH, GC]), ALU.subtract).then_inc(diffed, 1)
                nc.vector.tensor_copy(t2[:, c, SEQ:T], t1[:, c, SEQ:T]).then_inc(diffed, 1)
                nc.vector.tensor_copy(df[:, 0, c, :].unsqueeze(2), mid).then_inc(diffed, 1)
                nc.vector.tensor_tensor(df[:, 1, c, :].unsqueeze(2), end, mid, ALU.subtract).then_inc(diffed, 1)
            dve.wait_ge(factored, 2)
            for h in range(H):
                own = slice(DK * (h % 2), DK * (h % 2) + DK)
                nc.vector.scalar_tensor_tensor(out=qz[own, h, :], in0=qk_t[own, h // 2, :], scalar=DK ** -0.5,
                                               in1=eq[own, h // 2, :], op0=ALU.mult, op1=ALU.mult)
            nc.vector.tensor_tensor(qk_t[:, 2:4, :], qk_t[:, 2:4, :], ek[:], ALU.mult)

        @block.scalar
        def _(act):
            nc.scalar.activation(t1[:], la_t[:], ACT.Abs).then_inc(absd, 1)
            act.wait_ge(absd, 1)
            nc.scalar.activation(t1[:], t1[:], ACT.Exp, scale=-1.0).then_inc(exped, 1)
            act.wait_ge(exped, 1)
            nc.scalar.activation(t2[:], t1[:], ACT.Ln, bias=1.0).then_inc(logged, 1)
            act.wait_ge(diffed, 8)
            nc.scalar.activation(eq[:], t2[:], ACT.Exp, scale=1.0 / TAU).then_inc(factored, 1)
            nc.scalar.activation(ek[:], t2[:], ACT.Exp, scale=-1.0 / TAU).then_inc(factored, 1)
            nc.scalar.activation(fac[:, 0:2], df[:], ACT.Exp, scale=1.0 / TAU)
            nc.scalar.activation(fac[:, 2], t1[:, :, GC - 1:SEQ:GC], ACT.Exp, scale=1.0 / TAU)
            nc.scalar.activation(fac_s[:], t1[:, :, SEQ + SLEN - 1:T:SLEN], ACT.Exp, scale=1.0 / TAU)


def gla(nc, qk_t, qz, v_sb, g_sb, fac, fac_s, gla_norm, state_in, state_prompt, state_sample, o_t):
    with ExitStack() as ctx:
        def sb(name, shape, dt=F32):
            return ctx.enter_context(nc.sbuf_tensor("gl_" + name, shape, dt))

        def ps(name, shape):
            return ctx.enter_context(nc.psum_tensor("gl_" + name, shape, F32))

        def sem(name):
            return new_sem(nc, "gl_" + name)

        ident = sb("ident", [P, P])
        mask = sb("mask", [P, P])
        mask_s = sb("mask_s", [TS, TS])
        seq_col = sb("seq_col", [P, NSEQ, TS])
        seq_row = sb("seq_row", [TS, NSEQ])
        gn = sb("gn", [H, P])
        gain = sb("gain", [P, H])
        k_nat = [sb(f"k_nat{b}", [P, 2, 2, P]) for b in range(2)]
        prob = [sb(f"prob{b}", [P, H, P]) for b in range(2)]
        S = sb("S", [P, 2, DV])
        Sm = [sb(f"Sm{b}", [P, 2, DV]) for b in range(2)]
        kvf = sb("kvf", [P, 2, DV])
        sq = sb("sq", [P, H, DV])
        ssum = sb("ssum", [P, H])
        rinv = sb("rinv", [P, H])
        rstd = sb("rstd", [P, H])
        on = [sb(f"on{b}", [P, H, DV]) for b in range(2)]
        Ss = sb("Ss", [P, 2, NSEQ, DV])
        qs = sb("qs", [P, H, NSEQ, TS])
        vs = sb("vs", [TS, NSEQ, H, DV])
        kp_bank = ps("kp", [P, 4, P])
        kp = kp_bank[:, 0:2, :]
        sp_ = [ps(f"sp{b}", [P, H, P]) for b in range(2)]
        kvp = ps("kvp", [P, 2, 2, DV])
        op = [ps(f"op{b}", [P, H, DV]) for b in range(2)]
        kvs = ps("kvs", [P, 2, W4])
        states_loaded, gn_loaded = sem("states_loaded"), sem("gn_loaded")
        zeroed, shaped = sem("zeroed"), sem("shaped")
        gain_turned = sem("gain_turned")
        k_turned, k_stored = sem("k_turned"), sem("k_stored")
        scored, masked = sem("scored"), sem("masked")
        kv_done, kv_read = sem("kv_done"), sem("kv_read")
        decayed, step, local = sem("decayed"), sem("step"), sem("local")
        o_done, squared, stded, o_normed = sem("o_done"), sem("squared"), sem("stded"), sem("o_normed")
        o_turned, o_stored = sem("o_turned"), sem("o_stored")
        s_ready, q_split, v_split, s_written = sem("s_ready"), sem("q_split"), sem("v_split"), sem("s_written")
        kvs_done, sample_ready = sem("kvs_done"), sem("sample_ready")
        block = ctx.enter_context(nc.Block())

        @block.sync
        def _(sp):
            sp.dma_start(gn[:], gla_norm).then_inc(gn_loaded, 16)
            for h in range(H):
                sp.dma_start(Ss[DK * (h % 2):DK * (h % 2) + DK, h // 2],
                             state_in[:, h].rearrange("s d e -> d s e")).then_inc(states_loaded, 16)
            sp.wait_ge(s_ready, SEQ // GC)
            for h in range(H):
                sp.dma_start(state_prompt[h], S[DK * (h % 2):DK * (h % 2) + DK, h // 2, :]).then_inc(s_written, 16)
            sp.wait_ge(sample_ready, 2)
            for h in range(H):
                sp.dma_start(state_sample[:, h].rearrange("s d e -> d s e"),
                             Ss[DK * (h % 2):DK * (h % 2) + DK, h // 2]).then_inc(s_written, 16)
            sp.wait_ge(s_written, 16 * 2 * H)

        @block.gpsimd
        def _(pool):
            nc.gpsimd.memset(ident[:], 0.0).then_inc(zeroed, 1)
            nc.gpsimd.memset(mask[:], 1.0).then_inc(zeroed, 1)
            nc.gpsimd.memset(mask_s[:], 1.0).then_inc(zeroed, 1)
            nc.gpsimd.memset(seq_col[:], 1.0).then_inc(zeroed, 1)
            nc.gpsimd.memset(seq_row[:], 1.0).then_inc(zeroed, 1)
            pool.wait_ge(zeroed, 5)
            s = 0

            def select(ap, op, fill, base, pattern, mul):
                return nc.gpsimd.affine_select(out=ap, in_=ap, compare_op=op, fill=fill, base=base,
                                               pattern=pattern, channel_multiplier=mul)

            select(ident[:], ALU.not_equal, 1.0, 0, [[-1, P]], 1).then_inc(shaped, 1)
            select(mask[:], ALU.is_ge, 0.0, 0, [[1, P]], -1).then_inc(shaped, 1)
            select(mask_s[:], ALU.is_ge, 0.0, 0, [[1, TS]], -1).then_inc(shaped, 1)
            sc = seq_col[:]
            select(sc, ALU.is_ge, 0.0, 0, [[-SLEN, NSEQ], [1, TS]], 0).then_inc(shaped, 1)
            select(seq_row[:], ALU.is_ge, 0.0, 0, [[-SLEN, NSEQ]], 1).then_inc(shaped, 1)
            pool.wait_ge(shaped, 5)
            select(mask[:, GC:P], ALU.is_ge, 0.0, -GC, [[0, GC]], 1).then_inc(shaped, 1)
            select(mask_s[:].rearrange("p (s j) -> p s j", j=SLEN), ALU.is_ge, 0.0, 0,
                   [[-SLEN, NSEQ], [0, SLEN]], 1).then_inc(shaped, 1)
            select(sc, ALU.is_ge, 0.0, SLEN - 1, [[SLEN, NSEQ], [-1, TS]], 0).then_inc(shaped, 1)
            select(seq_row[:], ALU.is_ge, 0.0, SLEN - 1, [[SLEN, NSEQ]], -1).then_inc(shaped, 1)

        def half(h):
            return slice(DK * (h % 2), DK * (h % 2) + DK)

        @block.tensor
        def _(pe):
            pe.wait_ge(shaped, 9)
            pe.wait_ge(gn_loaded, 16)
            nc.tensor.transpose(sp_[0][:, 0, 0:H], gn[:], ident[0:H, 0:H]).then_inc(gain_turned, 1)

            def turn_out(t):
                r = rows(t)
                pe.wait_ge(o_normed, t + 1)
                for h in range(H):
                    mm = nc.tensor.transpose(sp_[(t + 1) % 2][:, h, 0:r], on[t % 2][0:r, h, :], ident[0:r, 0:r])
                mm.then_inc(o_turned, 1)

            for t in range(NT):
                r = rows(t)
                tok = slice(t * P, t * P + r)
                if t >= 1:
                    pe.wait_ge(k_stored, t)
                for c in range(2):
                    mm = nc.tensor.transpose(kp[0:r, c, :], qk_t[:, 2 + c, tok], ident[:])
                mm.then_inc(k_turned, 1)
                if t == 0:
                    pe.wait_ge(masked, 1)
                if t >= 3:
                    pe.wait_ge(o_stored, t - 2)
                for h in range(H):
                    mm = nc.tensor.matmul(sp_[t % 2][0:r, h, 0:r], qk_t[:, 2 + h // 2, tok], qz[:, h, tok],
                                          start=True, stop=True)
                mm.then_inc(scored, 1)
                pe.wait_ge(k_stored, t + 1)
                if t < NTP:
                    if t >= 1:
                        pe.wait_ge(kv_read, 2 * t)
                    for c in range(2):
                        for h in range(H):
                            mm = nc.tensor.matmul(kvp[half(h), c, h // 2, :],
                                                  k_nat[t % 2][:, c, h // 2, half(h)],
                                                  v_sb[:, t, h * DV:(h + 1) * DV],
                                                  start=True, stop=True, skip_group_check=True)
                    mm.then_inc(kv_done, 1)
                pe.wait_ge(masked, t + 2)
                if t >= 2:
                    pe.wait_ge(o_normed, t - 1)
                if t < NTP:
                    pe.wait_ge(decayed, 2 * t + 2)
                    for h in range(H):
                        nc.tensor.matmul(op[t % 2][:, h, :], prob[t % 2][:, h, :], v_sb[:, t, h * DV:(h + 1) * DV],
                                         start=True, stop=False, skip_group_check=True)
                        for c in range(2):
                            mm = nc.tensor.matmul(op[t % 2][c * GC:(c + 1) * GC, h, :],
                                                  qz[:, h, t * P + c * GC:t * P + (c + 1) * GC],
                                                  Sm[c][:, h // 2, :], start=False, stop=True,
                                                  skip_group_check=True)
                    mm.then_inc(o_done, 1)
                else:
                    pe.wait_ge(q_split, 1)
                    pe.wait_ge(states_loaded, 16 * H)
                    for h in range(H):
                        nc.tensor.matmul(op[t % 2][0:r, h, :], prob[t % 2][0:r, h, 0:r],
                                         v_sb[0:r, t, h * DV:(h + 1) * DV], start=True, stop=False,
                                         skip_group_check=True)
                        for s in range(NSEQ):
                            mm = nc.tensor.matmul(op[t % 2][0:r, h, :], qs[:, h, s, :], Ss[:, h // 2, s, :], start=False, stop=(s == NSEQ - 1),
                                                  skip_group_check=True)
                    mm.then_inc(o_done, 1)
                if t >= 1:
                    turn_out(t - 1)
            pe.wait_ge(v_split, 1)
            pe.wait_ge(o_stored, NTP)
            for g in range(2):
                if g == 1:
                    pe.wait_ge(sample_ready, 1)
                for b in range(2):
                    for h in (2 * g, 2 * g + 1):
                        mm = nc.tensor.matmul(kvs[half(h), b, :], k_nat[NTP % 2][0:TS, 0, h // 2, half(h)],
                                              vs[:, 4 * b:4 * b + 4, h, :], start=True, stop=True,
                                              skip_group_check=True)
                mm.then_inc(kvs_done, 1)
            turn_out(NTP)

        @block.scalar
        def _(act):
            for t in range(NT):
                r = rows(t)
                act.wait_ge(o_done, t + 1)
                if t >= 1:
                    act.wait_ge(stded, t)
                nc.scalar.activation(sq[0:r], op[t % 2][0:r], ACT.Square).then_inc(squared, 1)
                act.wait_ge(step, 2 * (t + 1))
                nc.scalar.activation(rstd[0:r], rinv[0:r], ACT.Sqrt).then_inc(stded, 1)

        @block.vector
        def _(dve):
            ls = Count(local)
            dve.wait_ge(gain_turned, 1)
            nc.vector.tensor_copy(gain[:], sp_[0][:, 0, 0:H]).then_inc(masked, 1)
            for b in range(2):
                nc.vector.memset(k_nat[b][GC:P, 0], 0.0)
                nc.vector.memset(k_nat[b][0:GC, 1], 0.0)
            nc.vector.memset(S[:], 0.0).then_inc(local, 1)
            dve.wait_ge(local, ls.up())

            def state(t, c):
                n = 2 * t + c
                if t >= 1:
                    dve.wait_ge(o_done, t)
                for p in range(2):
                    ins = nc.vector.tensor_scalar(Sm[c][:, p, :], S[:, p, :], fac[:, 0, p, n:n + 1], None, ALU.mult)
                ins.then_inc(decayed, 1)
                if c == 0:
                    dve.wait_ge(kv_done, t + 1)
                for p in range(2):
                    ins = nc.vector.tensor_scalar(kvf[:, p, :], kvp[:, c, p, :], fac[:, 1, p, n:n + 1], None, ALU.mult)
                ins.then_inc(kv_read, 1)
                dve.wait_ge(kv_read, n + 1)
                dve.wait_ge(decayed, n + 1)
                for p in range(2):
                    ins = nc.vector.scalar_tensor_tensor(out=S[:, p, :], in0=S[:, p, :], scalar=fac[:, 2, p, n:n + 1],
                                                         in1=kvf[:, p, :], op0=ALU.mult, op1=ALU.add)
                ins.then_inc(s_ready, 1)
                dve.wait_ge(s_ready, n + 1)

            def store_out(t):
                r = rows(t)
                dve.wait_ge(o_turned, t + 1)
                nc.vector.tensor_tensor(o_t[:, 0:H, t * P:t * P + r], sp_[(t + 1) % 2][:, :, 0:r],
                                        gain[:].unsqueeze(2).broadcast_to([P, H, r]), ALU.mult).then_inc(o_stored, 1)

            for t in range(NT):
                r = rows(t)
                dve.wait_ge(k_turned, t + 1)
                if t < NTP:
                    for c in range(2):
                        own = slice(c * GC, (c + 1) * GC)
                        ins = nc.vector.tensor_copy(k_nat[t % 2][own, c], kp[own])
                    ins.then_inc(k_stored, 1)
                else:
                    nc.vector.tensor_copy(k_nat[t % 2][0:r, 0], kp[0:r]).then_inc(k_stored, 1)
                dve.wait_ge(scored, t + 1)
                if t == 0:
                    dve.wait_ge(shaped, 9)
                m = mask if t < NTP else mask_s
                nc.vector.tensor_tensor(prob[t % 2][0:r, :, 0:r], sp_[t % 2][0:r, :, 0:r],
                                        m[:].unsqueeze(1).broadcast_to([r, H, r]), ALU.mult).then_inc(masked, 1)
                if t < NTP:
                    state(t, 0)
                    state(t, 1)
                else:
                    for h in range(H):
                        ins = nc.vector.tensor_tensor(qs[:, h], seq_col[:],
                                                      qz[:, h, SEQ:T].unsqueeze(1).broadcast_to([P, NSEQ, TS]), ALU.mult)
                    ins.then_inc(q_split, 1)
                    for s in range(NSEQ):
                        ins = nc.vector.tensor_scalar(vs[:, s], v_sb[0:TS, NTP, :].rearrange("p (h e) -> p h e", h=H),
                                                      seq_row[:, s:s + 1], None, ALU.mult)
                    ins.then_inc(v_split, 1)
                dve.wait_ge(squared, t + 1)
                nc.vector.tensor_reduce(ssum[0:r], sq[0:r], AX.X, ALU.add).then_inc(local, 1)
                dve.wait_ge(local, ls.up())
                nc.vector.tensor_scalar(ssum[0:r], ssum[0:r], 1.0 / DV, EPS, ALU.mult, ALU.add).then_inc(step, 1)
                dve.wait_ge(step, 2 * t + 1)
                nc.vector.reciprocal(rinv[0:r], ssum[0:r]).then_inc(step, 1)
                dve.wait_ge(stded, t + 1)
                if t >= 2:
                    dve.wait_ge(o_turned, t - 1)
                nc.vector.tensor_tensor(on[t % 2][0:r], op[t % 2][0:r],
                                        rstd[0:r].unsqueeze(2).broadcast_to([r, H, DV]), ALU.mult).then_inc(local, 1)
                dve.wait_ge(local, ls.up())
                nc.vector.tensor_tensor(on[t % 2][0:r], on[t % 2][0:r],
                                        g_sb[0:r, t, :].rearrange("p (h e) -> p h e", h=H), ALU.mult).then_inc(o_normed, 1)
                if t >= 1:
                    store_out(t - 1)
            for g in range(2):
                dve.wait_ge(kvs_done, g + 1)
                nc.vector.tensor_tensor(Ss[:, g], Ss[:, g], kvs[:].rearrange("p b (s e) -> p (b s) e", e=DV),
                                        ALU.add).then_inc(local, 1)
                dve.wait_ge(local, ls.up())
                nc.vector.tensor_tensor(Ss[:, g], Ss[:, g], fac_s[:, g, :].unsqueeze(2).broadcast_to([P, NSEQ, DV]),
                                        ALU.mult).then_inc(sample_ready, 1)
            store_out(NTP)



TWO_PI = (6.28125, 0.0019350051879882812, 3.0199159819567e-07)
ROUND = 1.5 * 2 ** 23


def s5_tables(nc, A, tab):
    with ExitStack() as ctx:
        def sb(name, shape, dt=F32):
            return ctx.enter_context(nc.sbuf_tensor("st_" + name, shape, dt))

        def ps(name):
            return ctx.enter_context(nc.psum_tensor("st_" + name, [P, 4, P], F32))

        def sem(name):
            return new_sem(nc, "st_" + name)

        NA = 8
        lam = sb("lam", [P, 2, GP])
        ldt = sb("ldt", [P, GP])
        dt = sb("dt", [P, GP])
        lrdt = sb("lrdt", [P, GP])
        ang = sb("ang", [P, NA, GP])
        nrot = sb("nrot", [P, NA, GP])
        aab = sb("aab", [P, NA, GP])
        sn = sb("sn", [P, NA, GP])
        cs = sb("cs", [P, NA, GP])
        halfpi = sb("halfpi", [P, 1])
        mag = sb("mag", [P, GP])
        a1, a2 = sb("a1", [P, 2, GP]), sb("a2", [P, 2, GP])
        f = sb("f", [P, 2, GP])
        q = sb("q", [P, 6, GP])
        bin_ = sb("bin", [P, 2, GP, GCH])
        cin = sb("cin", [P, 2, 2, P])
        ba = sb("ba", [P, 2, GP, SC, GCH])
        ca = sb("ca", [P, 2, GP, SC + 1, GCH])
        bbz = sb("bbz", [P, 2, G, GCH])
        tmp = sb("tmp", [P, 2, GP, P])
        kk = tmp[0:GCH].rearrange("p i q s -> p (i q s)").rearrange("p (g k c) -> p g k c", g=G, c=GCH)
        dd = sb("dd", [GCH, G])
        dg = sb("dg", [GCH, G, GCH])
        ident = sb("ident", [P, P])
        pb = [ps(f"pb{b}") for b in range(8)]
        loaded, zeroed, shaped = sem("loaded"), sem("zeroed"), sem("shaped")
        step = sem("step")
        dted, angled, absd, trig = sem("dted"), sem("angled"), sem("absd"), sem("trig")
        c_turned, b_turned, b_ready = sem("c_turned"), sem("b_turned"), sem("b_ready")
        c_stored, b_stored = sem("c_stored"), sem("b_stored")
        k_done, k_ready, k_read, toep = sem("k_done"), sem("k_ready"), sem("k_read"), sem("toep")
        kk_ready = sem("kk_ready")
        block = ctx.enter_context(nc.Block())

        @block.sync
        def _(sp):
            for i, n in enumerate(("s5_lam_re", "s5_lam_im")):
                for h in range(2):
                    sp.dma_start(lam[ST * h:ST * h + ST, i, :],
                                 A[n][0].rearrange("(q h) p -> h p q", h=2)[h]).then_inc(loaded, 16)
            for h in range(2):
                sp.dma_start(ldt[ST * h:ST * h + ST, :],
                             A["s5_log_dt"][0].rearrange("(q h) -> h q", h=2)[h:h + 1, :].broadcast_to([ST, GP])
                             ).then_inc(loaded, 16)
                for i, n in enumerate(("s5_b_re", "s5_b_im")):
                    sp.dma_start(bin_[ST * h:ST * h + ST, i],
                                 A[n][0].rearrange("(q h) p c -> h p q c", h=2)[h]).then_inc(loaded, 16)
            for i, n in enumerate(("s5_c_re", "s5_c_im")):
                for half in range(2):
                    for j in range(SC):
                        g = 2 * (half * SC + j)
                        sp.dma_start(cin[j * GCH:(j + 1) * GCH, i, half, :].rearrange("c (h p) -> c h p", h=2),
                                     A[n][0, g:g + 2].rearrange("h c p -> c h p")).then_inc(loaded, 16)
            sp.dma_start(dd[:], A["s5_d"][0].rearrange("(g c) -> c g", c=GCH)).then_inc(loaded, 16)
            sp.wait_ge(kk_ready, 1)
            sp.wait_ge(shaped, 2)
            for r in range(SC):
                sp.dma_start(tab.tp[r * GCH:(r + 1) * GCH, :, r * GCH:],
                             kk[:, :, 0:SC - r, :].rearrange("c g k d -> c g (k d)")).then_inc(toep, 16)
            sp.wait_ge(toep, 16 * SC)

        @block.gpsimd
        def _(pool):
            nc.gpsimd.memset(ident[:], 0.0).then_inc(zeroed, 1)
            pool.wait_ge(zeroed, 1)
            nc.gpsimd.affine_select(out=ident[:], in_=ident[:], compare_op=ALU.not_equal, fill=1.0, base=0,
                                    pattern=[[-1, P]], channel_multiplier=1).then_inc(shaped, 1)
            nc.gpsimd.memset(tab.tp[:], 0.0).then_inc(shaped, 1)
            nc.gpsimd.memset(tab.cm[:], 0.0).then_inc(shaped, 1)
            nc.gpsimd.memset(bbz[:], 0.0).then_inc(shaped, 1)

        @block.scalar
        def _(act):
            act.wait_ge(loaded, 16 * NLOAD)
            nc.scalar.activation(dt[:], ldt[:], ACT.Exp).then_inc(dted, 1)
            act.wait_ge(angled, 1)
            nc.scalar.activation(mag[:], lrdt[:], ACT.Exp).then_inc(dted, 1)
            nc.scalar.activation(tab.r8[:], lrdt[:], ACT.Exp, scale=float(SC)).then_inc(dted, 1)
            act.wait_ge(angled, 2)
            nc.scalar.activation(aab[:], ang[:], ACT.Abs).then_inc(absd, 1)
            act.wait_ge(absd, 1)
            nc.scalar.activation(sn[:], ang[:], ACT.Sin).then_inc(trig, 1)
            nc.scalar.activation(cs[:], aab[:], ACT.Sin, bias=halfpi[:], scale=-1.0).then_inc(trig, 1)
            for n in range(8):
                act.wait_ge(b_turned, n + 1)
                nc.scalar.activation(tab.bm[:].rearrange("p q i s -> p (q i) s")[:, 4 * n:4 * n + 4], pb[4 + n % 4][:],
                                     ACT.Copy).then_inc(b_stored, 1)

        @block.tensor
        def _(pe):
            pe.wait_ge(loaded, 16 * NLOAD)
            pe.wait_ge(shaped, 1)
            for i in range(2):
                for half in range(2):
                    mm = nc.tensor.transpose(pb[0][:, 2 * i + half, :], cin[:, i, half, :], ident[:])
            mm.then_inc(c_turned, 1)
            pe.wait_ge(b_ready, 1)
            for n in range(8):
                if n >= 4:
                    pe.wait_ge(b_stored, n - 3)
                for j in range(4):
                    gp, i = (4 * n + j) // 2, (4 * n + j) % 2
                    mm = nc.tensor.transpose(pb[4 + n % 4][:, j, :], ba[:, i, gp, :, :].rearrange("p k c -> p (k c)"),
                                             ident[:])
                mm.then_inc(b_turned, 1)
            pe.wait_ge(k_ready, 1)
            for n in range(8):
                if n >= 4:
                    pe.wait_ge(k_read, n - 3)
                for j in range(4):
                    g = 4 * n + j
                    for i in range(2):
                        mm = nc.tensor.matmul(pb[n % 4][0:GCH, j, :], bbz[:, i, g, :],
                                              ca[:, i, g // 2, 0:SC, :].rearrange("p k c -> p (k c)"),
                                              start=(i == 0), stop=(i == 1))
                mm.then_inc(k_done, 1)

        @block.vector
        def _(dve):
            s = Count(step)

            def tt(out, a, b, op):
                nc.vector.tensor_tensor(out, a, b, op).then_inc(step, 1)
                s.up()

            def settle():
                dve.wait_ge(step, s.n)

            def cmul(out, x, a, shape):
                t = [tmp[:, i].rearrange("p q s -> p (q s)")[:, 0:shape[1] * shape[2]]
                     .rearrange("p (q s) -> p q s", q=shape[1]) for i in range(2)]
                tt(out[0], x[0], a[0], ALU.mult)
                tt(t[0], x[1], a[1], ALU.mult)
                tt(out[1], x[1], a[0], ALU.mult)
                tt(t[1], x[0], a[1], ALU.mult)
                settle()
                tt(out[0], out[0], t[0], ALU.subtract)
                tt(out[1], out[1], t[1], ALU.add)
                settle()

            def square(out, x):
                cmul([out[:, i, :].unsqueeze(2) for i in range(2)], [x[:, i, :].unsqueeze(2) for i in range(2)],
                     [x[:, i, :].unsqueeze(2) for i in range(2)], [P, GP, 1])

            nc.vector.memset(halfpi[:], 1.5707963267948966).then_inc(step, 1)
            s.up()
            dve.wait_ge(dted, 1)
            tt(lrdt[:], lam[:, 0, :], dt[:], ALU.mult)
            tt(ang[:, 0, :], lam[:, 1, :], dt[:], ALU.mult)
            settle()
            dve.sem_inc(angled, 1)
            for k in range(1, NA):
                nc.vector.tensor_scalar(ang[:, k, :], ang[:, 0, :], float(SC * 2 ** (k - 1)), None, ALU.mult).then_inc(step, 1)
                s.up()
            settle()
            nc.vector.tensor_scalar(nrot[:], ang[:], 0.15915494309189535, ROUND, ALU.mult, ALU.add).then_inc(step, 1)
            s.up()
            settle()
            nc.vector.tensor_scalar(nrot[:], nrot[:], ROUND, None, ALU.subtract).then_inc(step, 1)
            s.up()
            settle()
            for part in TWO_PI:
                nc.vector.scalar_tensor_tensor(out=ang[:], in0=nrot[:], scalar=-part, in1=ang[:],
                                               op0=ALU.mult, op1=ALU.add).then_inc(step, 1)
                s.up()
                settle()
            nc.vector.tensor_scalar(ang[:], ang[:], 3.1415925, -3.1415925, ALU.min, ALU.max).then_inc(angled, 1)
            dve.wait_ge(trig, 2)
            dve.wait_ge(dted, 3)
            tt(a1[:, 0, :], mag[:], cs[:, 0, :], ALU.mult)
            tt(a1[:, 1, :], mag[:], sn[:, 0, :], ALU.mult)
            lr, li = lam[:, 0, :], lam[:, 1, :]
            tt(q[:, 0, :], lr, lr, ALU.mult)
            tt(q[:, 1, :], li, li, ALU.mult)
            settle()
            tt(q[:, 0, :], q[:, 0, :], q[:, 1, :], ALU.add)
            nc.vector.tensor_scalar(q[:, 2, :], a1[:, 0, :], -1.0, None, ALU.add).then_inc(step, 1)
            s.up()
            settle()
            nc.vector.reciprocal(q[:, 1, :], q[:, 0, :]).then_inc(step, 1)
            s.up()
            tt(q[:, 3, :], q[:, 2, :], lr, ALU.mult)
            tt(q[:, 4, :], a1[:, 1, :], li, ALU.mult)
            tt(f[:, 1, :], a1[:, 1, :], lr, ALU.mult)
            tt(q[:, 5, :], q[:, 2, :], li, ALU.mult)
            settle()
            tt(f[:, 0, :], q[:, 3, :], q[:, 4, :], ALU.add)
            tt(f[:, 1, :], f[:, 1, :], q[:, 5, :], ALU.subtract)
            settle()
            tt(f[:, 0, :], f[:, 0, :], q[:, 1, :], ALU.mult)
            tt(f[:, 1, :], f[:, 1, :], q[:, 1, :], ALU.mult)
            square(a2, a1)
            square(tab.a4, a2)

            def over(v, n, i):
                return v[:, i, :].unsqueeze(2).broadcast_to([P, GP, n])

            def powers(arr, k0, k1, a, d0):
                n = (k1 - k0) * GCH

                def part(i, k):
                    return arr[:, i].rearrange("p q k c -> p q (k c)")[:, :, k * GCH:k * GCH + n]

                cmul([part(0, d0), part(1, d0)], [part(0, k0), part(1, k0)], [over(a, n, 0), over(a, n, 1)], [P, GP, n])

            cmul([ba[:, i, :, SC - 1, :] for i in range(2)], [bin_[:, i] for i in range(2)],
                 [over(f, GCH, 0), over(f, GCH, 1)], [P, GP, GCH])
            powers(ba, SC - 1, SC, a1, SC - 2)
            powers(ba, SC - 2, SC, a2, SC - 4)
            powers(ba, SC - 4, SC, tab.a4, SC - 8)
            dve.sem_inc(b_ready, 1)
            dve.wait_ge(c_turned, 1)
            for i in range(2):
                nc.vector.tensor_copy(ca[:, i, :, 0, :],
                                      pb[0][:, 2 * i:2 * i + 2, :].rearrange("p b (q c) -> p (b q) c", c=GCH)).then_inc(step, 1)
                s.up()
            settle()
            powers(ca, 0, 1, a1, 1)
            powers(ca, 0, 2, a2, 2)
            powers(ca, 0, 4, tab.a4, 4)
            powers(ca, 4, 5, tab.a4, 8)
            dve.wait_ge(shaped, 4)
            for h in range(2):
                own = slice(ST * h, ST * h + ST)
                nc.vector.tensor_copy(bbz[own, 0, h:G:2, :], ba[own, 0, :, SC - 1, :]).then_inc(step, 1)
                nc.vector.tensor_scalar(bbz[own, 1, h:G:2, :], ba[own, 1, :, SC - 1, :], -1.0, None, ALU.mult).then_inc(step, 1)
                nc.vector.tensor_copy(tab.cm[own, :, 0, h, :], ca[own, 0, :, 1:, :].rearrange("p q k c -> p q (k c)")).then_inc(step, 1)
                nc.vector.tensor_scalar(tab.cm[own, :, 1, h, :], ca[own, 1, :, 1:, :].rearrange("p q k c -> p q (k c)"),
                                        -1.0, None, ALU.mult).then_inc(step, 1)
                s.up(4)
            tt(dg[:], ident[0:GCH, 0:GCH].unsqueeze(1).broadcast_to([GCH, G, GCH]),
               dd[:].unsqueeze(2).broadcast_to([GCH, G, GCH]), ALU.mult)
            settle()
            dve.sem_inc(k_ready, 1)
            nc.vector.tensor_copy(tab.w[:, 0, :, 1], cs[:, 1, :]).then_inc(step, 1)
            nc.vector.tensor_copy(tab.w[:, 1, :, 1], sn[:, 1, :]).then_inc(step, 1)
            s.up(2)
            settle()
            for k in range(7):
                n = 2 ** k
                cmul([tab.w[:, i, :, n + 1:2 * n + 1] for i in range(2)], [tab.w[:, i, :, 1:n + 1] for i in range(2)],
                     [cs[:, k + 1, :].unsqueeze(2).broadcast_to([P, GP, n]),
                      sn[:, k + 1, :].unsqueeze(2).broadcast_to([P, GP, n])], [P, GP, n])
            for n in range(8):
                dve.wait_ge(k_done, n + 1)
                nc.vector.tensor_copy(kk[:, 4 * n:4 * n + 4], pb[n % 4][0:GCH].rearrange("p g (k c) -> p g k c", c=GCH)
                                      ).then_inc(k_read, 1)
            dve.wait_ge(k_read, 8)
            nc.vector.tensor_tensor(kk[:, :, 0, :], kk[:, :, 0, :], dg[:], ALU.add).then_inc(kk_ready, 1)


NLOAD = 2 * 2 + 2 * 3 + 2 * 2 * SC + 1


def s5_scan(nc, A, tab, u_sb, us_nat, x_g, s_all, s0, state_re, state_im, state_re_s, state_im_s):
    with ExitStack() as ctx:
        def sb(name, shape, dt=F32):
            return ctx.enter_context(nc.sbuf_tensor("ss_" + name, shape, dt))

        def sem(name):
            return new_sem(nc, "ss_" + name)

        v = sb("v", [P, 2, GP, NMS])
        tmp = sb("tmp", [P, 2, GP, NM])
        us8 = s_all[:].rearrange("p i q m -> p (i q m)")[0:NSEQ, 0:SC * W4].rearrange("p (g r c) -> p g r c", g=G, r=SC)
        s0_in = sb("s0_in", [P, 2, P])
        fin = sb("fin", [P, 2, NSEQ + 1, GP])
        fin_o = sb("fin_o", [P, 2, P])
        finp_o = sb("finp_o", [GP, 2, P])
        ident = sb("ident", [P, P])
        pb = [ctx.enter_context(nc.psum_tensor(f"ss_pb{b}", [P, W4], F32)) for b in range(8)]
        loaded, zeroed, shaped, us_loaded, us_zero = sem("loaded"), sem("zeroed"), sem("shaped"), sem("us_loaded"), sem("us_zero")
        u_turned, u_stored = sem("u_turned"), sem("u_stored")
        v_done, v_stored = sem("v_done"), sem("v_stored")
        step, rdata, fin_ready, fin_turned, fin_stored, written = (
            sem("step"), sem("rdata"), sem("fin_ready"), sem("fin_turned"), sem("fin_stored"), sem("written"))
        block = ctx.enter_context(nc.Block())

        @block.sync
        def _(sp):
            for i, n in enumerate(("state_s5_re", "state_s5_im")):
                sp.dma_start(s0_in[:, i, :], A[n][0].rearrange("s (q h) p -> (s q) (h p)", h=2)).then_inc(loaded, 16)
            sp.wait_ge(us_zero, 1)
            for j in range(SLEN):
                sp.dma_start(us8[:, :, SC - SLEN + j, :], us_nat[j:TS:SLEN, :].rearrange("s (g c) -> s g c", g=G)
                             ).then_inc(us_loaded, 16)
            sp.wait_ge(fin_stored, 2)
            for i, (ds, dp) in enumerate(((state_re_s, state_re), (state_im_s, state_im))):
                sp.dma_start(ds.rearrange("s (q h) p -> (s q) (h p)", h=2), fin_o[:, i, :]).then_inc(written, 16)
                sp.dma_start(dp.rearrange("(q h) p -> q (h p)", h=2), finp_o[:, i, :]).then_inc(written, 16)
            sp.wait_ge(written, 64)

        @block.gpsimd
        def _(pool):
            nc.gpsimd.memset(us8[:, :, 0:SC - SLEN, :], 0.0).then_inc(us_zero, 1)
            nc.gpsimd.memset(ident[:], 0.0).then_inc(zeroed, 1)
            pool.wait_ge(zeroed, 1)
            nc.gpsimd.affine_select(out=ident[:], in_=ident[:], compare_op=ALU.not_equal, fill=1.0, base=0,
                                    pattern=[[-1, P]], channel_multiplier=1).then_inc(shaped, 1)

        @block.tensor
        def _(pe):
            pe.wait_ge(shaped, 1)
            for n in range(8):
                if n >= 4:
                    pe.wait_ge(u_stored, n - 3)
                for j in range(4):
                    g = 4 * n + j
                    mm = nc.tensor.transpose(pb[n % 4][:, j * P:(j + 1) * P], u_sb[:, g].rearrange("p r c -> p (r c)"), ident[:])
                mm.then_inc(u_turned, 1)
            pe.wait_ge(us_loaded, 16 * SLEN)
            pe.wait_ge(u_stored, 5)
            for g in range(G):
                mm = nc.tensor.transpose(pb[0][:, g * NSEQ:(g + 1) * NSEQ], us8[:, g].rearrange("p r c -> p (r c)"),
                                         ident[0:NSEQ, 0:NSEQ])
            mm.then_inc(u_turned, 1)
            pe.wait_ge(loaded, 32)
            pe.wait_ge(u_stored, 6)
            for i in range(2):
                mm = nc.tensor.transpose(pb[1][:, i * P:(i + 1) * P], s0_in[:, i, :], ident[:])
            mm.then_inc(u_turned, 1)
            pe.wait_ge(u_stored, 9)
            for gp in range(GP):
                if gp >= 4:
                    pe.wait_ge(v_stored, gp - 3)
                for i in range(2):
                    for h in range(2):
                        mm = nc.tensor.matmul(pb[4 + gp % 4][ST * h:ST * h + ST, i * NMS:(i + 1) * NMS],
                                              tab.bm[:, gp, i, ST * h:ST * h + ST], x_g[:, 2 * gp + h, :],
                                              start=True, stop=True, skip_group_check=True)
                mm.then_inc(v_done, 1)
            pe.wait_ge(fin_ready, 1)
            for i in range(2):
                nc.tensor.transpose(pb[0][:, i * P:(i + 1) * P], fin[:, i, 0:NSEQ, :].rearrange("p s q -> p (s q)"), ident[:])
                mm = nc.tensor.transpose(pb[1][0:GP, i * P:(i + 1) * P], fin[:, i, NSEQ, :], ident[:])
            mm.then_inc(fin_turned, 1)

        @block.scalar
        def _(act):
            for gp in range(GP):
                act.wait_ge(v_done, gp + 1)
                nc.scalar.activation(v[:, :, gp, :], pb[4 + gp % 4][:, 0:2 * NMS].rearrange("p (i m) -> p i m", i=2),
                                     ACT.Copy).then_inc(v_stored, 1)

        @block.vector
        def _(dve):
            s = Count(step)

            def tt(out, a, b, op):
                nc.vector.tensor_tensor(out, a, b, op).then_inc(step, 1)
                s.up()

            def settle():
                dve.wait_ge(step, s.n)

            for n in range(8):
                dve.wait_ge(u_turned, n + 1)
                nc.vector.tensor_copy(x_g[:, 4 * n:4 * n + 4, 0:NM],
                                      pb[n % 4][:].rearrange("p (g m) -> p g m", m=P)).then_inc(u_stored, 1)
            dve.wait_ge(u_turned, 9)
            nc.vector.tensor_copy(x_g[:, :, NM:], pb[0][:, 0:G * NSEQ].rearrange("p (g m) -> p g m", m=NSEQ)
                                  ).then_inc(u_stored, 1)
            dve.wait_ge(u_turned, 10)
            nc.vector.tensor_copy(s0[:], pb[1][:, 0:2 * P].rearrange("p (i s q) -> p i s q", i=2, q=GP)).then_inc(u_stored, 1)
            w = [tab.w[:, i, :, 1:] for i in range(2)]
            after = [s_all[:, i, :, 1:] for i in range(2)]
            vp = [v[:, i, :, 0:NM] for i in range(2)]
            rot = [tmp[:, i] for i in range(2)]
            flat = [v[:].rearrange("p i q m -> p (i q m)")[:, i * GP * NM:(i + 1) * GP * NM] for i in range(2)]
            room = [x.rearrange("p (q m) -> p q m", m=NM) for x in flat]
            dve.wait_ge(v_stored, GP)
            for i in range(2):
                nc.vector.tensor_copy(fin[:, i, 0:NSEQ, :], v[:, i, :, NM:].rearrange("p q s -> p s q")).then_inc(step, 1)
            s.up(2)
            tt(rot[0], vp[0], w[0], ALU.mult)
            tt(after[0], vp[1], w[1], ALU.mult)
            tt(rot[1], vp[1], w[0], ALU.mult)
            tt(after[1], vp[0], w[1], ALU.mult)
            settle()
            tt(rot[0], rot[0], after[0], ALU.add)
            tt(rot[1], rot[1], after[1], ALU.subtract)
            nc.vector.tensor_copy(room[0], tab.r8[:].unsqueeze(2).broadcast_to([P, GP, NM])).then_inc(step, 1)
            s.up()
            settle()
            nc.vector.memset(room[0][:, :, 0], 0.0).then_inc(step, 1)
            nc.vector.memset(s_all[:, :, :, 0], 0.0).then_inc(step, 1)
            s.up(2)
            settle()
            for i in range(2):
                g = rot[i].rearrange("p q m -> p (q m)")
                nc.vector.tensor_tensor_scan(g, flat[0], g, 0.0, ALU.mult, ALU.add).then_inc(step, 1)
                s.up()
            settle()
            tt(after[0], rot[0], w[0], ALU.mult)
            tt(after[1], rot[1], w[0], ALU.mult)
            tt(room[0], rot[1], w[1], ALU.mult)
            tt(room[1], rot[0], w[1], ALU.mult)
            settle()
            tt(after[0], after[0], room[0], ALU.subtract)
            tt(after[1], after[1], room[1], ALU.add)
            settle()
            for i in range(2):
                nc.vector.tensor_copy(fin[:, i, NSEQ, :], s_all[:, i, :, NM]).then_inc(step, 1)
            s.up(2)
            a4 = [tab.a4[:, i, :].unsqueeze(1).broadcast_to([P, NSEQ, GP]) for i in range(2)]
            for i, j, k, op in ((0, 0, 0, ALU.add), (0, 1, 1, ALU.subtract), (1, 0, 1, ALU.add), (1, 1, 0, ALU.add)):
                tt(tmp[:, 0, 0:NSEQ, 0:GP], s0[:, j], a4[k], ALU.mult)
                settle()
                tt(fin[:, i, 0:NSEQ, :], fin[:, i, 0:NSEQ, :], tmp[:, 0, 0:NSEQ, 0:GP], op)
                settle()
            dve.sem_inc(fin_ready, 1)
            dve.wait_ge(fin_turned, 1)
            nc.vector.tensor_copy(fin_o[:], pb[0][:, 0:2 * P].rearrange("p (i s) -> p i s", i=2)).then_inc(fin_stored, 1)
            nc.vector.tensor_copy(finp_o[:], pb[1][0:GP, 0:2 * P].rearrange("p (i s) -> p i s", i=2)).then_inc(fin_stored, 1)


def s5_outputs(nc, A, tab, u_sb, x_g, s_all, s0, o_t):
    with ExitStack() as ctx:
        def sb(name, shape, dt=F32):
            return ctx.enter_context(nc.sbuf_tensor("so_" + name, shape, dt))

        def sem(name):
            return new_sem(nc, "so_" + name)

        z = u_sb[:].rearrange("p g r c -> p (g r c)").rearrange("p (r c) -> p r c", r=SC)
        zs = sb("zs", [NSEQ, SLEN, W4])
        z_t = sb("z_t", [P, 4, T])
        wg = sb("wg", [P, 4, W4])
        bg = sb("bg", [P, 4])
        sg = [sb(f"sg{b}", [P, NW]) for b in range(2)]
        ident = sb("ident", [P, P])
        pb = [ctx.enter_context(nc.psum_tensor(f"so_pb{b}", [P, W4], F32)) for b in range(8)]
        loaded, zeroed, shaped = sem("loaded"), sem("zeroed"), sem("shaped")
        y_done, z_ready, z_turned, z_stored = sem("y_done"), sem("z_ready"), sem("z_turned"), sem("z_stored")
        g_done, g_ready, o_ready = sem("g_done"), sem("g_ready"), sem("o_ready")
        block = ctx.enter_context(nc.Block())
        NY = GP // 2

        @block.sync
        def _(sp):
            sp.dma_start(wg[:], A["w_glu"][0].rearrange("(k p) c -> p k c", p=P)).then_inc(loaded, 16)
            sp.dma_start(bg[:], A["b_glu"][0].rearrange("(k p) -> p k", p=P)).then_inc(loaded, 16)

        @block.gpsimd
        def _(pool):
            nc.gpsimd.memset(ident[:], 0.0).then_inc(zeroed, 1)
            pool.wait_ge(zeroed, 1)
            nc.gpsimd.affine_select(out=ident[:], in_=ident[:], compare_op=ALU.not_equal, fill=1.0, base=0,
                                    pattern=[[-1, P]], channel_multiplier=1).then_inc(shaped, 1)

        @block.tensor
        def _(pe):
            def outputs(bank, gp, m, width, state, cols):
                q = (gp % 2) * 2 * P
                for h in range(2):
                    nc.tensor.matmul(bank[0:width, q + h * P:q + h * P + cols], x_g[:, 2 * gp + h, m],
                                     tab.tp[:, 2 * gp + h, P - cols:], start=True, stop=False, skip_group_check=True)
                    for i in range(2):
                        mm = nc.tensor.matmul(bank[0:width, q + h * P:q + h * P + cols], state(i, gp),
                                              tab.cm[:, gp, i, h, 0:cols], start=False, stop=(i == 1), skip_group_check=True)
                return mm

            for n in range(NY):
                if n >= 4:
                    pe.wait_ge(z_ready, n - 3)
                for gp in (2 * n, 2 * n + 1):
                    mm = outputs(pb[n % 4], gp, slice(0, NM), P, lambda i, gp: s_all[:, i, gp, 0:NM], P)
                mm.then_inc(y_done, 1)
            for n in range(NY):
                pe.wait_ge(z_ready, NY + n - 3)
                for gp in (2 * n, 2 * n + 1):
                    mm = outputs(pb[n % 4], gp, slice(NM, NMS), NSEQ, lambda i, gp: s0[:, i, :, gp], SLEN * GCH)
                mm.then_inc(y_done, 1)
            pe.wait_ge(shaped, 1)
            pe.wait_ge(z_ready, NY)
            for r in range(SC):
                if r >= 4:
                    pe.wait_ge(z_stored, r - 3)
                for c in range(4):
                    mm = nc.tensor.transpose(pb[4 + r % 4][:, c * P:(c + 1) * P], z[:, r, c * P:(c + 1) * P], ident[:])
                mm.then_inc(z_turned, 1)
            pe.wait_ge(z_ready, 2 * NY)
            pe.wait_ge(z_stored, SC - 3)
            for j in range(SLEN):
                for c in range(4):
                    q = (j * 4 + c) * NSEQ
                    mm = nc.tensor.transpose(pb[4][:, q:q + NSEQ], zs[:, j, c * P:(c + 1) * P], ident[0:NSEQ, 0:NSEQ])
            mm.then_inc(z_turned, 1)
            pe.wait_ge(loaded, 32)
            pe.wait_ge(z_stored, SC + 1)
            n = 0
            for c in range(4):
                for b in range(3):
                    if n >= 4:
                        pe.wait_ge(g_ready, n - 3)
                    for k in range(4):
                        mm = nc.tensor.matmul(pb[n % 4][:, 0:NW], wg[:, k, c * P:(c + 1) * P],
                                              z_t[:, k, b * NW:(b + 1) * NW], start=(k == 0), stop=(k == 3))
                    mm.then_inc(g_done, 1)
                    n += 1

        @block.scalar
        def _(act):
            for n in range(2 * NY):
                act.wait_ge(y_done, n + 1)
                c0 = (n % NY) * 4 * GCH
                if n < NY:
                    out = z[:, :, c0:c0 + 4 * GCH].rearrange("m r (q c) -> m q r c", c=GCH)
                    y = pb[n % 4][:].rearrange("m (q r c) -> m q r c", q=4, c=GCH)
                else:
                    out = zs[:, :, c0:c0 + 4 * GCH].rearrange("m r (q c) -> m q r c", c=GCH)
                    y = pb[n % 4][0:NSEQ].rearrange("m (q r c) -> m q r c", q=4, c=GCH)[:, :, 0:SLEN, :]
                nc.scalar.activation(out, y, ACT.Gelu_apprx_tanh).then_inc(z_ready, 1)
            act.wait_ge(loaded, 32)
            n = 0
            for c in range(4):
                for b in range(3):
                    act.wait_ge(g_done, n + 1)
                    if n >= 2:
                        act.wait_ge(o_ready, n - 1)
                    nc.scalar.activation(sg[n % 2][:], pb[n % 4][:, 0:NW], ACT.Sigmoid, bias=bg[:, c:c + 1]).then_inc(g_ready, 1)
                    n += 1

        @block.vector
        def _(dve):
            for r in range(SC):
                dve.wait_ge(z_turned, r + 1)
                nc.vector.tensor_copy(z_t[:, :, r:SEQ:SC], pb[4 + r % 4][:].rearrange("p (c m) -> p c m", c=4)
                                      ).then_inc(z_stored, 1)
            dve.wait_ge(z_turned, SC + 1)
            for j in range(SLEN):
                ins = nc.vector.tensor_copy(z_t[:, :, SEQ + j:T:SLEN], pb[4][:, j * 4 * NSEQ:(j + 1) * 4 * NSEQ]
                                            .rearrange("p (c m) -> p c m", c=4))
            ins.then_inc(z_stored, 1)
            dve.wait_ge(z_stored, SC + 1)
            n = 0
            for c in range(4):
                for b in range(3):
                    dve.wait_ge(g_ready, n + 1)
                    tok = slice(b * NW, (b + 1) * NW)
                    nc.vector.tensor_tensor(o_t[:, 4 + c, tok], z_t[:, c, tok], sg[n % 2][:], ALU.mult).then_inc(o_ready, 1)
                    n += 1



def mix_out(nc, w_out, o_t, x_tiles, x2_tiles):
    with ExitStack() as ctx:
        def sem(name):
            return new_sem(nc, "mo_" + name)

        w = ctx.enter_context(nc.sbuf_tensor("mo_w", [P, KD, D], F32))
        x = [ctx.enter_context(nc.sbuf_tensor(f"mo_x{b}", [P, D], F32)) for b in range(3)]
        pb = [ctx.enter_context(nc.psum_tensor(f"mo_pb{b}", [P, W4], F32)) for b in range(8)]
        w_loaded = [sem(f"w_loaded{k}") for k in range(KD)]
        done, added = sem("done"), sem("added")
        x_loaded = [sem(f"x_loaded{b}") for b in range(3)]
        stored = [sem(f"stored{b}") for b in range(3)]
        block = ctx.enter_context(nc.Block())

        @block.sync
        def _(sp):
            for k in range(KD):
                sp.dma_start(w[:, k], w_out[k * P:(k + 1) * P, :]).then_inc(w_loaded[k], 16)
            for t in range(NT):
                if t >= 3:
                    sp.wait_ge(stored[t % 3], 16 * (t // 3))
                sp.dma_start(x[t % 3][0:rows(t)], x_tiles[t]).then_inc(x_loaded[t % 3], 16)

        @block.gpsimd
        def _(pool):
            for t in range(NT):
                pool.wait_ge(added, 2 * t + 2)
                pool.dma_start(x2_tiles[t], x[t % 3][0:rows(t)]).then_inc(stored[t % 3], 16)
            for b in range(3):
                pool.wait_ge(stored[b], 16 * (NT // 3))

        @block.tensor
        def _(pe):
            def product(n, k):
                t, half = n // 2, n % 2
                return nc.tensor.matmul(pb[n % 8][0:rows(t)], o_t[:, k, t * P:t * P + rows(t)],
                                        w[:, k, half * W4:(half + 1) * W4], start=(k == 0), stop=(k == KD - 1))

            for k in range(KD):
                pe.wait_ge(w_loaded[k], 16)
                for n in range(8):
                    mm = product(n, k)
                    if k == KD - 1:
                        mm.then_inc(done, 1)
            for n in range(8, 2 * NT):
                pe.wait_ge(added, n - 7)
                for k in range(KD):
                    mm = product(n, k)
                mm.then_inc(done, 1)

        @block.vector
        def _(dve):
            for t in range(NT):
                dve.wait_ge(x_loaded[t % 3], 16 * (t // 3 + 1))
                for half in range(2):
                    n = 2 * t + half
                    xs = x[t % 3][0:rows(t), half * W4:(half + 1) * W4]
                    dve.wait_ge(done, n + 1)
                    nc.vector.tensor_tensor(xs, pb[n % 8][0:rows(t)], xs, ALU.add).then_inc(added, 1)


PARTS = ((0, 0), (0, 1), (1, 0))
NU = 2 * PH


def wq_block(wq, b):
    return wq.rearrange("(k p) c -> p k c", p=P)[:, :, b * 2 * P:(b + 1) * 2 * P]


def peer_scores(nc, wq, keys, h_hi, h_lo, s_sb, raw, w_loaded):
    with ExitStack() as ctx:
        def sb(name, shape, dt=F32):
            return ctx.enter_context(nc.sbuf_tensor("pq_" + name, shape, dt))

        def sem(name):
            return new_sem(nc, "pq_" + name)

        WQ = 2 * P
        NWB = NU // 2
        w = [[sb(f"w{b}{x}", [P, KD, WQ], F32R) for x in "hl"] for b in range(2)]
        keys_sb = sb("keys", [P, NU, P])
        keys_t = sb("keys_t", [P, NU, P])
        q_t = [sb(f"q_t{b}", [P, T]) for b in range(2)]
        ident = sb("ident", [P, P])
        pq = [ctx.enter_context(nc.psum_tensor(f"pq_pq{b}", [P, W4], F32)) for b in range(3)]
        psc = [ctx.enter_context(nc.psum_tensor(f"pq_ps{b}", [P, W4], F32)) for b in range(3)]
        pk = ctx.enter_context(nc.psum_tensor("pq_pk", [P, 4, P], F32))
        w_hi, w_lo = sem("w_hi"), sem("w_lo")
        keys_loaded, zeroed, shaped = sem("keys_loaded"), sem("zeroed"), sem("shaped")
        k_turned, k_stored, cleared = sem("k_turned"), sem("k_stored"), sem("cleared")
        q_done, q_stored, s_done, s_stored = sem("q_done"), sem("q_stored"), sem("s_done"), sem("s_stored")
        block = ctx.enter_context(nc.Block())

        @block.sync
        def _(sp):
            sp.dma_start(keys_sb[:], keys.rearrange("h s n d -> n (h s) d")).then_inc(keys_loaded, 16)
            for b in range(1, NWB):
                sp.wait_ge(w_lo, b)
                sp.dma_start(raw[:], wq_block(wq, b)).then_inc(w_loaded, 16)

        @block.gpsimd
        def _(pool):
            nc.gpsimd.memset(ident[:], 0.0).then_inc(zeroed, 1)
            pool.wait_ge(zeroed, 1)
            nc.gpsimd.affine_select(out=ident[:], in_=ident[:], compare_op=ALU.not_equal, fill=1.0, base=0,
                                    pattern=[[-1, P]], channel_multiplier=1).then_inc(shaped, 1)

        @block.tensor
        def _(pe):
            pe.wait_ge(shaped, 1)

            def turn_keys(n):
                pe.wait_ge(keys_loaded, 16)
                for q in (n, 3) if n == 2 else (n,):
                    if q >= 1:
                        pe.wait_ge(k_stored, q)
                    for j in range(4):
                        mm = nc.tensor.transpose(pk[:, j, :], keys_sb[:, 4 * q + j, :], ident[:])
                    mm.then_inc(k_turned, 1)

            def score(c):
                pe.wait_ge(q_stored, 3 * (c + 1))
                pe.wait_ge(k_stored, 4)
                for b in range(3):
                    if c >= 1:
                        pe.wait_ge(s_stored, 3 * (c - 1) + b + 1)
                    for t in range(3 * b, 3 * b + 3):
                        mm = nc.tensor.matmul(psc[b][0:rows(t), (t % 3) * P:(t % 3 + 1) * P],
                                              q_t[c % 2][:, t * P:t * P + rows(t)], keys_t[:, c, :],
                                              start=True, stop=True, skip_group_check=True)
                    mm.then_inc(s_done, 1)

            for c in range(NU):
                pe.wait_ge(w_lo, c // 2 + 1)
                for n in range(3):
                    if c >= 1:
                        pe.wait_ge(q_stored, 3 * (c - 1) + n + 1)
                    steps = [(x, y, k) for x, y in PARTS for k in range(KD)]
                    for s, (x, y, k) in enumerate(steps):
                        mm = nc.tensor.matmul(pq[n][:, 0:NW], w[(c // 2) % 2][x][:, k, (c % 2) * P:(c % 2 + 1) * P],
                                              (h_hi, h_lo)[y][:, k, n * NW:(n + 1) * NW],
                                              start=(s == 0), stop=(s == len(steps) - 1))
                    mm.then_inc(q_done, 1)
                    if c == 0:
                        turn_keys(n)
                if c >= 1:
                    score(c - 1)
            score(NU - 1)

        @block.scalar
        def _(act):
            def high(b):
                act.wait_ge(w_loaded, 16 * (b + 1))
                if b >= 2:
                    act.wait_ge(q_done, 3 * 2 * (b - 1))
                nc.scalar.activation(w[b % 2][0][:], raw[:], ACT.Copy).then_inc(w_hi, 1)

            high(0)
            for c in range(NU):
                if c % 2 == 0 and c // 2 + 1 < NWB:
                    high(c // 2 + 1)
                for n in range(3):
                    act.wait_ge(q_done, 3 * c + n + 1)
                    if c >= 2:
                        act.wait_ge(s_done, 3 * (c - 1))
                    nc.scalar.activation(q_t[c % 2][:, n * NW:(n + 1) * NW], pq[n][:, 0:NW], ACT.Copy).then_inc(q_stored, 1)

        @block.vector
        def _(dve):
            def low(b):
                dve.wait_ge(w_hi, b + 1)
                nc.vector.tensor_tensor(w[b % 2][1][:], raw[:], w[b % 2][0][:].bitcast(F32), ALU.subtract).then_inc(w_lo, 1)

            low(0)
            for n in range(4):
                dve.wait_ge(k_turned, n + 1)
                nc.vector.tensor_copy(keys_t[:, 4 * n:4 * n + 4], pk[:]).then_inc(k_stored, 1)
            nc.vector.memset(s_sb[:, NTP], 0.0).then_inc(cleared, 1)
            low(1)
            for c in range(NU):
                if c % 2 == 0 and c > 0 and c // 2 + 1 < NWB:
                    low(c // 2 + 1)
                for b in range(3):
                    dve.wait_ge(s_done, 3 * c + b + 1)
                    if b < 2:
                        nc.vector.tensor_copy(s_sb[:, 3 * b:3 * b + 3, c, :], psc[b][:, 0:3 * P].rearrange("p (t n) -> p t n", n=P)
                                              ).then_inc(s_stored, 1)
                    else:
                        if c == 0:
                            dve.wait_ge(cleared, 1)
                        nc.vector.tensor_copy(s_sb[:, 6:8, c, :], psc[b][:, 0:2 * P].rearrange("p (t n) -> p t n", n=P))
                        nc.vector.tensor_copy(s_sb[0:TS, NTP, c, :], psc[b][0:TS, 2 * P:3 * P]).then_inc(s_stored, 1)


NEG = -3.0e38
TPAD = NT * P


class Ahead:

    def __init__(self, ctx, nc, tag, base, u_d, act_d, h):
        def sb(name, shape, dt=F32):
            return ctx.enter_context(nc.sbuf_tensor(f"{tag}_{name}", shape, dt))

        def sem(name):
            return new_sem(nc, f"{tag}_{name}")

        self.base, self.u_d, self.act_d, self.h = base, u_d, act_d, h
        self.u_sb = sb("u", [P, D])
        self.ut = [[sb(f"ut{b}{x}", [P, KD, P], F32R) for x in "hl"] for b in range(2)]
        self.a_sb = [sb(f"a{b}", [P, NW]) for b in range(2)]
        self.ident = sb("ident", [P, P])
        self.pa = [ctx.enter_context(nc.psum_tensor(f"{tag}_pa{b}", [P, W4], F32)) for b in range(3)]
        self.pt = [ctx.enter_context(nc.psum_tensor(f"{tag}_pt{b}", [P, W4], F32)) for b in range(2)]
        self.zeroed, self.shaped = sem("zeroed"), sem("shaped")
        self.u_in = sem("u_in")
        self.ut_hi = sem("ut_hi")
        self.turned = sem("turned")
        self.ut_lo = sem("ut_lo")
        self.a_done = sem("a_done")
        self.a_act = sem("a_act")
        self.kept = [sem(f"kept{b}") for b in range(2)]


def ahead_ident(nc, pool, ah):
    nc.gpsimd.memset(ah.ident[:], 0.0).then_inc(ah.zeroed, 1)
    pool.wait_ge(ah.zeroed, 1)
    nc.gpsimd.affine_select(out=ah.ident[:], in_=ah.ident[:], compare_op=ALU.not_equal, fill=1.0, base=0,
                            pattern=[[-1, P]], channel_multiplier=1).then_inc(ah.shaped, 1)


def ahead_load(sp, ah, r, e):
    m = r * 2 + e
    sp.wait_ge(ah.turned, m * 2 + 2)
    sp.dma_start(ah.u_sb[:], ah.u_d[bass.ds((m + ah.base) * NK, NK), :]).then_inc(ah.u_in, 16)


def ahead_keep(sp, ah, r, e, c):
    m = r * 2 + e
    sp.wait_ge(ah.a_act, m * 3 + c + 1 + 3)
    sp.dma_start(ah.act_d[bass.ds(m + ah.base, 1), :, c * NW:(c + 1) * NW].rearrange("o j t -> j (o t)"),
                 ah.a_sb[(3 * e + c) % 2][:]).then_inc(ah.kept[(3 * e + c) % 2], 16)


def ahead_tile_io(sp, ah, r, e, between=lambda c: None):
    for c in range(3):
        if c == 2:
            ahead_load(sp, ah, r + 1, e)
        ahead_keep(sp, ah, r, e, c)
        between(c)


def ahead_turn(nc, pe, ah, r, e, half):
    m = r * 2 + e
    if half == 0:
        pe.wait_ge(ah.u_in, (m + 1) * 16)
    pe.wait_ge(ah.ut_lo, (m - 1) * 2 + half + 1 + 2)
    for k in range(4):
        c = (4 * half + k) * P
        mm = nc.tensor.transpose(ah.pt[half][:, k * P:(k + 1) * P], ah.u_sb[:, c:c + P], ah.ident[:])
    mm.then_inc(ah.turned, 1)


def ahead_up(nc, pe, ah, r, e, c):
    m = r * 2 + e
    if c == 0:
        pe.wait_ge(ah.ut_lo, m * 2 + 2 + 2)
    else:
        ahead_turn(nc, pe, ah, r + e, 1 - e, c - 1)
    pe.wait_ge(ah.a_act, (m - 1) * 3 + c + 1 + 3)
    steps = [(x, y, k) for x, y in PARTS for k in range(KD)]
    for s, (x, y, k) in enumerate(steps):
        mm = nc.tensor.matmul(ah.pa[c][:, 0:NW], ah.ut[e][x][:, k, :], ah.h[y][:, k, c * NW:(c + 1) * NW],
                              start=(s == 0), stop=(s == len(steps) - 1))
    mm.then_inc(ah.a_done, 1)


def ahead_high(nc, act, ah, r, e, half):
    m = r * 2 + e
    act.wait_ge(ah.a_done, (m - 1) * 3 + 6)
    act.wait_ge(ah.turned, m * 2 + half + 1 + 2)
    nc.scalar.activation(ah.ut[e][0][:, 4 * half:4 * half + 4, :],
                         ah.pt[half][:].rearrange("p (k s) -> p k s", k=4), ACT.Copy).then_inc(ah.ut_hi, 1)


def ahead_gelu(nc, act, ah, r, e, c):
    m = r * 2 + e
    if c >= 1:
        ahead_high(nc, act, ah, r + e, 1 - e, c - 1)
    act.wait_ge(ah.a_done, m * 3 + c + 1 + 6)
    b = (3 * e + c) % 2
    act.wait_ge(ah.kept[b], (r * 3 + (3 * e + c) // 2 + 1) * 16)
    nc.scalar.activation(ah.a_sb[b][:], ah.pa[c][:, 0:NW], ACT.Gelu_apprx_tanh).then_inc(ah.a_act, 1)


def ahead_low(nc, dve, ah, r, e, half):
    k = slice(4 * half, 4 * half + 4)
    dve.wait_ge(ah.ut_hi, (r * 2 + e) * 2 + half + 1)
    nc.vector.tensor_tensor(ah.ut[e][1][:, k, :], ah.pt[half][:].rearrange("p (k s) -> p k s", k=4),
                            ah.ut[e][0][:, k, :].bitcast(F32), ALU.subtract).then_inc(ah.ut_lo, 1)


def peer_topk(nc, s_sb, sel_t, u_d, act_d, h):
    with ExitStack() as ctx:
        def sb(name, shape, dt=F32):
            return ctx.enter_context(nc.sbuf_tensor("tk_" + name, shape, dt))

        def sem(name):
            return new_sem(nc, "tk_" + name)

        K2 = TOPK * TOPK
        w1 = sb("w1", [P, NU, NK])
        w2 = sb("w2", [P, NU, NK])
        top = sb("top", [P, PH, 2, TOPK])
        idx = sb("idx", [P, PH, 2, TOPK], U32)
        idxf = sb("idxf", [P, PH, 2, TOPK])
        cand, cand2 = (x[:].rearrange("p u k -> p (u k)").rearrange("p (h k) -> p h k", k=K2) for x in (w1, w2))
        fin = sb("fin", [P, PH, TOPK])
        pos = sb("pos", [P, PH, TOPK], U32)
        pos2 = sb("pos2", [P, 2, PH, TOPK], U32)
        posf = sb("posf", [P, 2, PH, TOPK])
        iota = sb("iota", [P, TOPK])
        oh = [x[:].rearrange("p u k -> p (u k)").rearrange("p (s m) -> p s m", m=TOPK) for x in (w1, w2)]
        res = sb("res", [P, 3, PH, TOPK])
        ex = sb("ex", [P, PH, TOPK])
        sums = sb("sums", [P, PH])
        ah = Ahead(ctx, nc, "ta", 0, u_d, act_d, h)
        pt = ctx.enter_context(nc.psum_tensor("tk_pt", [P, 4, P], F32))
        shaped = sem("shaped")
        step, passed, ex_in, ex_out = sem("step"), sem("passed"), sem("ex_in"), sem("ex_out")
        res_ready = sem("res_ready")
        oh_ready, picked = sem("oh_ready"), sem("picked")
        turned, stored = sem("turned"), sem("stored")
        block = ctx.enter_context(nc.Block())

        def pick(engine, i):
            o4 = oh[i].rearrange("p (h k) m -> p h k m", k=TOPK)
            return engine.tensor_tensor(o4, o4, idxf[:, :, i, :].unsqueeze(2).broadcast_to([P, PH, TOPK, TOPK]), ALU.mult)

        @block.gpsimd
        def _(pool):
            ahead_ident(nc, pool, ah)
            nc.gpsimd.iota(iota[:], [[1, TOPK]], base=0, channel_multiplier=0,
                           allow_small_or_imprecise_dtypes=True).then_inc(shaped, 1)
            with pool.Fori(0, NT) as t:
                pool.wait_ge(oh_ready, t + 1)
                pick(nc.gpsimd, 0).then_inc(picked, 1)

        @block.sync
        def _(sp):
            ahead_load(sp, ah, 0, 0)
            ahead_load(sp, ah, 0, 1)
            with sp.Fori(0, NT) as t:
                for j in range(4):
                    ahead_tile_io(sp, ah, t * 2 + j // 2, j % 2)
            for b in range(2):
                sp.wait_ge(ah.kept[b], 16 * (TOPK_AHEAD // 2 * 3 + 1))

        @block.scalar
        def _(act):
            act.sem_inc(stored, 1)
            act.sem_inc(ah.a_act, 3)
            for b in range(2):
                act.sem_inc(ah.kept[b], 16)
            for half in range(2):
                ahead_high(nc, act, ah, 0, 0, half)
            with act.Fori(0, NT) as t:
                for j in range(4):
                    for c in range(3):
                        ahead_gelu(nc, act, ah, t * 2 + j // 2, j % 2, c)
                        if (j, c) == (3, 0):
                            act.wait_ge(ex_in, t + 1)
                            nc.scalar.activation(ex[:], ex[:], ACT.Exp).then_inc(ex_out, 1)
                act.wait_ge(turned, t + 2)
                nc.scalar.activation(sel_t[:, :, bass.ds(t * P, P)], pt[:, 0:3, :], ACT.Copy).then_inc(stored, 1)

        @block.tensor
        def _(pe):
            pe.sem_inc(turned, 1)
            pe.sem_inc(ah.turned, 2)
            pe.sem_inc(ah.a_done, 6)
            pe.wait_ge(ah.shaped, 1)
            for half in range(2):
                ahead_turn(nc, pe, ah, 0, 0, half)
            ahead_up(nc, pe, ah, 0, 0, 0)
            with pe.Fori(0, NT) as t:
                for j, c in [(j, c) for j in range(5) for c in range(3)][1:13]:
                    ahead_up(nc, pe, ah, t * 2 + j // 2, j % 2, c)
                pe.wait_ge(res_ready, t + 1)
                pe.wait_ge(stored, t + 1)
                for i in range(3):
                    mm = nc.tensor.transpose(pt[:, i, :], res[:, i].rearrange("p h k -> p (h k)"), ah.ident[:])
                mm.then_inc(turned, 1)

        @block.vector
        def _(dve):
            dve.sem_inc(ah.ut_lo, 2)
            dve.wait_ge(shaped, 1)
            for half in range(2):
                ahead_low(nc, dve, ah, 0, 0, half)
            with dve.Fori(0, NT) as t:
                n = [0]
                TOTAL = STEPS_TOPK

                def did(ins):
                    ins.then_inc(step, 1)
                    n[0] += 1

                def settle():
                    dve.wait_ge(step, t * TOTAL + n[0])
                    dve.sem_inc(passed, 1)

                def low(j, half):
                    ahead_low(nc, dve, ah, t * 2 + (j + 1) // 2, (j + 1) % 2, half)

                v = nc.vector
                did(v.tensor_copy(w1[:], s_sb[:, bass.ds(t, 1)].rearrange("p o u k -> p (o u) k")))
                settle()
                units = [(h, i) for h in range(PH) for i in range(2)]

                def key(a, u):
                    return a[:, 2 * u[0] + u[1], :]

                for u in units:
                    did(v.max(top[:, u[0], u[1], 0:8], key(w1, u)))
                settle()
                low(0, 0)
                for u in units:
                    did(v.max_index(idx[:, u[0], u[1], 0:8], top[:, u[0], u[1], 0:8], key(w1, u)))
                    did(v.match_replace(key(w2, u), top[:, u[0], u[1], 0:8], key(w1, u), NEG))
                    if u == (5, 0):
                        low(0, 1)
                settle()
                for u in units:
                    did(v.max(top[:, u[0], u[1], 8:16], key(w2, u)))
                settle()
                low(1, 0)
                for u in units:
                    did(v.max_index(idx[:, u[0], u[1], 8:16], top[:, u[0], u[1], 8:16], key(w2, u)))
                did(v.tensor_tensor(cand.rearrange("p h (a b) -> p h a b", b=TOPK),
                                    top[:, :, 0, :].unsqueeze(3).broadcast_to([P, PH, TOPK, TOPK]),
                                    top[:, :, 1, :].unsqueeze(2).broadcast_to([P, PH, TOPK, TOPK]), ALU.add))
                settle()
                did(v.tensor_copy(idxf[:], idx[:]))
                for h in range(PH):
                    did(v.max(fin[:, h, 0:8], cand[:, h]))
                low(1, 1)
                settle()
                for h in range(PH):
                    did(v.max_index(pos[:, h, 0:8], fin[:, h, 0:8], cand[:, h]))
                    did(v.match_replace(cand2[:, h], fin[:, h, 0:8], cand[:, h], NEG))
                settle()
                for h in range(PH):
                    did(v.max(fin[:, h, 8:16], cand2[:, h]))
                low(2, 0)
                settle()
                for h in range(PH):
                    did(v.max_index(pos[:, h, 8:16], fin[:, h, 8:16], cand2[:, h]))
                did(v.tensor_tensor(ex[:], fin[:], fin[:, :, 0:1].broadcast_to([P, PH, TOPK]), ALU.subtract))
                settle()
                dve.sem_inc(ex_in, 1)
                low(2, 1)
                did(v.tensor_scalar(pos2[:, 0], pos[:], 4, None, ALU.logical_shift_right))
                did(v.tensor_scalar(pos2[:, 1], pos[:], TOPK - 1, None, ALU.bitwise_and))
                settle()
                did(v.tensor_copy(posf[:], pos2[:]))
                settle()
                def hot(i):
                    return v.tensor_tensor(oh[i], iota[:].unsqueeze(1).broadcast_to([P, PH * TOPK, TOPK]),
                                           posf[:, i].rearrange("p h k -> p (h k)").unsqueeze(2)
                                           .broadcast_to([P, PH * TOPK, TOPK]), ALU.is_equal)

                hot(0).then_inc(oh_ready, 1)
                did(hot(1))
                settle()
                did(pick(v, 1))
                low(3, 0)
                settle()
                dve.wait_ge(turned, t + 1)
                for i in (1, 0):
                    if i == 0:
                        low(3, 1)
                        dve.wait_ge(picked, t + 1)
                    did(v.tensor_reduce(res[:, i].rearrange("p h k -> p (h k)"), oh[i], AX.X, ALU.add))
                dve.wait_ge(ex_out, t + 1)
                did(v.tensor_reduce(sums[:], ex[:], AX.X, ALU.add))
                settle()
                did(v.reciprocal(sums[:], sums[:]))
                settle()
                v.tensor_tensor(res[:, 2], ex[:], sums[:].unsqueeze(2).broadcast_to([P, PH, TOPK]), ALU.mult
                                ).then_inc(res_ready, 1)
                dve.wait_ge(res_ready, t + 1)
                assert n[0] == TOTAL, n[0]


STEPS_TOPK = 1 + 16 + 32 + 16 + 16 + 1 + 1 + 8 + 16 + 8 + 8 + 1 + 2 + 1 + 1 + 1 + 2 + 1 + 1


def peer_gates(nc, sel_t, w_d, u_d, act_d, h):
    with ExitStack() as ctx:
        def sb(name, shape, dt=F32):
            return ctx.enter_context(nc.sbuf_tensor("pg_" + name, shape, dt))

        def sem(name):
            return new_sem(nc, "pg_" + name)

        BT = 4
        SB = WCH // BT // 2
        THIRD = (2, 5, 8)
        LOW = {7: 0, 10: 1}
        NHB = 4
        NO = T // (2 * WCH)
        AFTER = 2
        iota = sb("iota", [P, P])
        hot_i = sb("hot_i", [P, NHB, BT, P])
        hot_j = sb("hot_j", [P, NHB, BT, P])
        wb = sb("wb", [P, 2, NK, WCH])
        ah = Ahead(ctx, nc, "ga", TOPK_AHEAD, u_d, act_d, h)
        pw = [ctx.enter_context(nc.psum_tensor(f"pg_pw{b}", [P, BT, P], F32)) for b in range(2)]
        shaped, hot = sem("shaped"), sem("hot")
        made = sem("made")
        stored = sem("stored")
        wrote = [sem(f"wrote{b}") for b in range(2)]
        PIECES = 5
        cleared = sem("cleared")
        block = ctx.enter_context(nc.Block())

        def segments(o):
            return [(s, (o * 4 + s) * SB, o * 2 + s // 2, s % 2) for s in range(4)]

        @block.gpsimd
        def _(pool):
            ahead_ident(nc, pool, ah)
            nc.gpsimd.memset(wb[:, 1], 0.0).then_inc(cleared, 1)
            nc.gpsimd.iota(iota[:], [[1, P]], base=0, channel_multiplier=0,
                           allow_small_or_imprecise_dtypes=True).then_inc(shaped, 1)

        @block.sync
        def _(sp):
            ahead_load(sp, ah, 0, 0)
            ahead_load(sp, ah, 0, 1)

            def write(slot, b2, piece):
                i = slice(piece * NK // PIECES, (piece + 1) * NK // PIECES)
                sp.dma_start(w_d[:, bass.ds(slot, 1), i].rearrange("j c i t -> j (c i t)"),
                             wb[:, b2, i].rearrange("j i t -> j (i t)")).then_inc(wrote[b2], 16)

            sp.wait_ge(cleared, 1)
            with sp.Fori(0, NO) as o:
                for b2 in range(2):
                    sp.wait_ge(stored, (o * 4 + 2 * b2) * SB + 2)
                    for s, _, r, e in segments(o)[2 * b2:2 * b2 + 2]:
                        def between(c):
                            if e * 3 + c < PIECES:
                                write(o * 2 + b2, 1 - b2, e * 3 + c)
                        ahead_tile_io(sp, ah, r, e, between)
            sp.wait_ge(stored, NO * 4 * SB + 2)
            for r in range(2 * NO, 2 * NO + AFTER):
                for e in range(2):
                    def between(c):
                        piece = ((r - 2 * NO) * 2 + e) * 3 + c
                        if piece < PIECES:
                            write(NCH, 1, piece)
                    ahead_tile_io(sp, ah, r, e, between)
            sp.wait_ge(wrote[0], 16 * PIECES * (NO + 1))
            sp.wait_ge(wrote[1], 16 * PIECES * (NO + 1))
            for b in range(2):
                sp.wait_ge(ah.kept[b], 16 * ((AFTER + 2 * NO) * 3 + 1))

        @block.vector
        def _(dve):
            dve.sem_inc(ah.ut_lo, 2)
            for half in range(2):
                ahead_low(nc, dve, ah, 0, 0, half)
            dve.wait_ge(shaped, 1)
            with dve.Fori(0, NO) as o:
                for s, bank0, r, e in segments(o):
                    for b in range(SB):
                        hb = (s * SB + b) % NHB
                        dve.wait_ge(made, bank0 + b + 1)
                        for j in range(BT):
                            tok = bass.ds(bank0 * BT + b * BT + j, 1)
                            nc.vector.tensor_scalar(hot_i[:, hb, j, :], iota[:], sel_t[:, 0, tok], sel_t[:, 2, tok],
                                                    ALU.is_equal, ALU.mult)
                            ins = nc.vector.tensor_scalar(hot_j[:, hb, j, :], iota[:], sel_t[:, 1, tok], None,
                                                          ALU.is_equal)
                        ins.then_inc(hot, 1)
                        if b + 1 in LOW:
                            ahead_low(nc, dve, ah, r + e, 1 - e, LOW[b + 1])
            with dve.Fori(2 * NO, 2 * NO + AFTER) as r:
                for e in range(2):
                    for half in range(2):
                        ahead_low(nc, dve, ah, r + e, 1 - e, half)

        @block.tensor
        def _(pe):
            pe.sem_inc(made, NHB)
            pe.sem_inc(ah.turned, 2)
            pe.sem_inc(ah.a_done, 6)
            pe.wait_ge(ah.shaped, 1)
            for half in range(2):
                ahead_turn(nc, pe, ah, 0, 0, half)
            with pe.Fori(0, NO) as o:
                for s, bank0, r, e in segments(o):
                    for b in range(SB):
                        g = s * SB + b
                        pe.wait_ge(hot, bank0 + b + 1)
                        pe.wait_ge(stored, bank0 + b + 1)
                        for j in range(BT):
                            mm = nc.tensor.matmul(pw[g % 2][:, j, :], hot_j[:, g % NHB, j, :], hot_i[:, g % NHB, j, :],
                                                  start=True, stop=True)
                        mm.then_inc(made, 1)
                        if b + 1 in THIRD:
                            ahead_up(nc, pe, ah, r, e, THIRD.index(b + 1))
            with pe.Fori(2 * NO, 2 * NO + AFTER) as r:
                for e in range(2):
                    for c in range(3):
                        ahead_up(nc, pe, ah, r, e, c)

        @block.scalar
        def _(act):
            act.sem_inc(stored, 2)
            act.sem_inc(wrote[0], 16 * PIECES)
            act.sem_inc(ah.a_act, 3)
            for b in range(2):
                act.sem_inc(ah.kept[b], 16)
            for half in range(2):
                ahead_high(nc, act, ah, 0, 0, half)
            with act.Fori(0, NO) as o:
                for s, bank0, r, e in segments(o):
                    b2 = s // 2
                    if s % 2 == 0:
                        act.wait_ge(wrote[b2], (o + 1) * 16 * PIECES)
                    for b in range(SB):
                        g, t0 = s * SB + b, ((s % 2) * SB + b) * BT
                        act.wait_ge(made, bank0 + b + 1 + NHB)
                        nc.scalar.activation(wb[:, b2, :, t0:t0 + BT].rearrange("p i t -> p t i"), pw[g % 2][:],
                                             ACT.Copy).then_inc(stored, 1)
                        if b + 1 in THIRD:
                            ahead_gelu(nc, act, ah, r, e, THIRD.index(b + 1))
            with act.Fori(2 * NO, 2 * NO + AFTER) as r:
                for e in range(2):
                    for c in range(3):
                        ahead_gelu(nc, act, ah, r, e, c)


NCH = 12
WCH = T // NCH
TOPK_AHEAD = 4 * NT
NAHEAD = TOPK_AHEAD + 4 + 2 * NCH


def split_h(nc, h_t, h_hi, h_lo):
    with ExitStack() as ctx:
        hi_done = new_sem(nc, "sh_hi")
        block = ctx.enter_context(nc.Block())

        @block.scalar
        def _(act):
            for k in range(KD):
                nc.scalar.activation(h_hi[:, k], h_t[:, k], ACT.Copy).then_inc(hi_done, 1)

        @block.vector
        def _(dve):
            for k in range(KD):
                dve.wait_ge(hi_done, k + 1)
                nc.vector.tensor_tensor(h_lo[:, k], h_t[:, k], h_hi[:, k].bitcast(F32), ALU.subtract)


def peer_experts(nc, u_d, v_d, w_d, act_d, h, acc_t):
    with ExitStack() as ctx:
        def sb(name, shape, dt=F32):
            return ctx.enter_context(nc.sbuf_tensor("pe_" + name, shape, dt))

        def sem(name):
            return new_sem(nc, "pe_" + name)

        NR = NAHEAD // 2
        assert NK == 2 * NAHEAD
        OB = 3 * KD
        NEW, OLD = 0, 1
        KINDS = (NEW, OLD)
        u_sb = [sb(f"u{b}", [P, D]) for b in range(2)]
        v_sb = sb("v", [P, D])
        w_sb = [sb(f"w{b}", [P, T]) for b in KINDS]
        old_sb = sb("old", [P, T])
        a_sb = [sb(f"a{b}", [P, NW]) for b in range(2)]
        ut = [[sb(f"ut{b}{x}", [P, KD, P], F32R) for x in "hl"] for b in range(2)]
        vx = [[[sb(f"vx{b}{e}{x}", [P, D], F32R) for x in "hl"] for e in range(2)] for b in KINDS]
        wx = [[[sb(f"wx{b}{e}{x}", [P, T], F32R) for x in "hl"] for e in range(2)] for b in KINDS]
        ident = sb("ident", [P, P])
        pa = [ctx.enter_context(nc.psum_tensor(f"pe_pa{b}", [P, W4], F32)) for b in range(3)]
        pt = [ctx.enter_context(nc.psum_tensor(f"pe_pt{b}", [P, W4], F32)) for b in range(2)]
        po = [ctx.enter_context(nc.psum_tensor(f"pe_po{b}", [P, W4], F32)) for b in range(3)]
        zeroed, shaped, cleared = sem("zeroed"), sem("shaped"), sem("cleared")
        u_in = [sem(f"u_in{b}") for b in range(2)]
        v_in = sem("v_in")
        w_in = [[sem(f"w_in{b}{c}") for c in range(3)] for b in KINDS]
        old_in = [sem(f"old_in{c}") for c in range(3)]
        turned, TURNED0 = sem("turned"), 4
        ut_hi = sem("ut_hi")
        ut_lo, UT0 = sem("ut_lo"), 2
        v_hi = sem("v_hi")
        v_lo, V0 = sem("v_lo"), 1
        a_done, ADONE0 = sem("a_done"), 6
        a_act, AACT0 = sem("a_act"), 3
        a_mul, AMUL0 = [sem(f"a_mul{b}") for b in KINDS], 2
        w_hi = [sem(f"w_hi{b}") for b in KINDS]
        w_lo, W0 = [sem(f"w_lo{b}") for b in KINDS], 3
        o_done, ODONE0 = sem("o_done"), 2 * OB
        o_added, OADD0 = sem("o_added"), OB
        block = ctx.enter_context(nc.Block())

        def rounds(eng, first, prepare, downs):
            first()
            prepare(0)
            with eng.Fori(0, NR - 1) as i:
                downs(i, NEW)
                prepare(i + 1)
                downs(i, OLD)
            downs(NR - 1, NEW)
            downs(NR - 1, OLD)

        def v_before(r, kind, e):
            return r * 4 + 2 * kind + e

        def tile_of(r, kind, e):
            return r * 2 + e if kind == OLD else r * -2 + (NK - 1 - e)

        @block.gpsimd
        def _(pool):
            nc.gpsimd.memset(ident[:], 0.0).then_inc(zeroed, 1)
            pool.wait_ge(zeroed, 1)
            nc.gpsimd.affine_select(out=ident[:], in_=ident[:], compare_op=ALU.not_equal, fill=1.0, base=0,
                                    pattern=[[-1, P]], channel_multiplier=1).then_inc(shaped, 1)

            def load_w(r, kind):
                for e in range(2):
                    for c in range(3):
                        tok = slice(c * NW, (c + 1) * NW)
                        chunks = slice(1 + c * NCH // 3, 1 + (c + 1) * NCH // 3)
                        pool.wait_ge(w_lo[kind], (r * 2 + e - 1) * 3 + c + 1 + W0)
                        pool.dma_start(w_sb[kind][:, tok].rearrange("j (c t) -> j c t", t=WCH),
                                       w_d[:, chunks, bass.ds(tile_of(r, kind, e), 1), :]
                                       .rearrange("j c o t -> j c (o t)")).then_inc(w_in[kind][c], 16)
                        if kind == OLD:
                            pool.dma_start(old_sb[:, tok], act_d[bass.ds(r * 2 + e, 1), :, tok]
                                           .rearrange("o j t -> j (o t)")).then_inc(old_in[c], 16)

            with pool.Fori(0, NR) as i:
                load_w(i, NEW)
                load_w(i, OLD)

        @block.sync
        def _(sp):
            def load_u(r, e):
                sp.wait_ge(turned, (r * 2 + e - 1) * 2 + TURNED0)
                sp.dma_start(u_sb[e][:], u_d[bass.ds(tile_of(r, NEW, e) * NK, NK), :]).then_inc(u_in[e], 16)

            def load_v(r, kind, e):
                sp.wait_ge(v_lo, v_before(r, kind, e) + V0)
                sp.dma_start(v_sb[:], v_d[bass.ds(tile_of(r, kind, e) * NK, NK), :]).then_inc(v_in, 16)

            load_u(0, 0)
            load_u(0, 1)
            with sp.Fori(0, NR) as i:
                for e in range(2):
                    load_v(i, NEW, e)
                    if e == 0:
                        load_u(i + 1, 0)
                for e in range(2):
                    load_v(i, OLD, e)
                    if e == 0:
                        load_u(i + 1, 1)

        @block.tensor
        def _(pe):
            pe.sem_inc(turned, TURNED0)
            pe.sem_inc(a_done, ADONE0)
            pe.sem_inc(o_done, ODONE0)
            pe.wait_ge(shaped, 1)

            def turn(r, e, half):
                if half == 0:
                    pe.wait_ge(u_in[e], (r + 1) * 16)
                pe.wait_ge(ut_lo, (r * 2 + e - 1) * 2 + half + 1 + UT0)
                for k in range(4):
                    c = (4 * half + k) * P
                    mm = nc.tensor.transpose(pt[half][:, k * P:(k + 1) * P], u_sb[e][:, c:c + P], ident[:])
                mm.then_inc(turned, 1)

            def prepare(new):
                for e in range(2):
                    m = new * 2 + e
                    for c in range(3):
                        if c >= 1:
                            turn(new + e, 1 - e, c - 1)
                        if c == 0:
                            pe.wait_ge(ut_lo, m * 2 + 2 + UT0)
                        pe.wait_ge(a_act, (m - 1) * 3 + c + 1 + AACT0)
                        steps = [(x, y, k) for x, y in PARTS for k in range(KD)]
                        for s, (x, y, k) in enumerate(steps):
                            mm = nc.tensor.matmul(pa[c][:, 0:NW], ut[e][x][:, k, :], h[y][:, k, c * NW:(c + 1) * NW],
                                                  start=(s == 0), stop=(s == len(steps) - 1))
                        mm.then_inc(a_done, 1)

            def downs(i, kind):
                pe.wait_ge(v_lo, v_before(i, kind, 1) + 1 + V0)
                pe.wait_ge(w_lo[kind], (i + 1) * 6 + W0)
                for o in range(OB):
                    k, c = o // 3, o % 3
                    pe.wait_ge(o_added, (i * 2 + kind) * OB + o - 2 + OADD0)
                    steps = [(e, x, y) for e in range(2) for x, y in PARTS]
                    for s, (e, x, y) in enumerate(steps):
                        mm = nc.tensor.matmul(po[o % 3][:, 0:NW], vx[kind][e][x][:, k * P:(k + 1) * P],
                                              wx[kind][e][y][:, c * NW:(c + 1) * NW],
                                              start=(s == 0), stop=(s == len(steps) - 1))
                    mm.then_inc(o_done, 1)

            def first():
                turn(0, 0, 0)
                turn(0, 0, 1)

            rounds(pe, first, prepare, downs)

        @block.scalar
        def _(act):
            act.sem_inc(a_act, AACT0)

            def high_u(r, e, half):
                act.wait_ge(a_done, (r * 2 + e - 1) * 3 + ADONE0)
                act.wait_ge(turned, (r * 2 + e) * 2 + half + 1 + TURNED0)
                nc.scalar.activation(ut[e][0][:, 4 * half:4 * half + 4, :],
                                     pt[half][:].rearrange("p (k s) -> p k s", k=4), ACT.Copy).then_inc(ut_hi, 1)

            def high_v(r, kind, e):
                act.wait_ge(v_in, (v_before(r, kind, e) + 1) * 16)
                act.wait_ge(o_done, (r * 2 + kind - 1) * OB + ODONE0)
                nc.scalar.activation(vx[kind][e][0][:], v_sb[:], ACT.Copy).then_inc(v_hi, 1)

            def high_w(r, kind, e, c):
                if (e, c) == (0, 0):
                    act.wait_ge(o_done, (r * 2 + kind - 1) * OB + ODONE0)
                act.wait_ge(a_mul[kind], (r * 2 + e) * 3 + c + 1 + AMUL0)
                nc.scalar.activation(wx[kind][e][0][:, c * NW:(c + 1) * NW], w_sb[kind][:, c * NW:(c + 1) * NW],
                                     ACT.Copy).then_inc(w_hi[kind], 1)

            def prepare(new):
                for e in range(2):
                    for c in range(3):
                        m = (new * 2 + e) * 3 + c
                        if c >= 1:
                            high_u(new + e, 1 - e, c - 1)
                        act.wait_ge(a_done, m + 1 + ADONE0)
                        act.wait_ge(a_mul[NEW], m - 1 + AMUL0)
                        nc.scalar.activation(a_sb[(3 * e + c) % 2][:], pa[c][:, 0:NW], ACT.Gelu_apprx_tanh
                                             ).then_inc(a_act, 1)
                        if c == 1:
                            high_v(new, NEW, e)
                        high_w(new, NEW, e, c)

            def downs(i, kind):
                if kind == NEW:
                    for e in range(2):
                        for c in range(3):
                            high_w(i, OLD, e, c)
                            if c == 0:
                                high_v(i, OLD, e)

            def first():
                high_u(0, 0, 0)
                high_u(0, 0, 1)

            rounds(act, first, prepare, downs)

        @block.vector
        def _(dve):
            dve.sem_inc(ut_lo, UT0)
            dve.sem_inc(v_lo, V0)
            dve.sem_inc(o_added, OADD0)
            for kind in KINDS:
                dve.sem_inc(a_mul[kind], AMUL0)
                dve.sem_inc(w_lo[kind], W0)

            def low_u(r, e, half):
                k = slice(4 * half, 4 * half + 4)
                dve.wait_ge(ut_hi, (r * 2 + e) * 2 + half + 1)
                nc.vector.tensor_tensor(ut[e][1][:, k, :], pt[half][:].rearrange("p (k s) -> p k s", k=4),
                                        ut[e][0][:, k, :].bitcast(F32), ALU.subtract).then_inc(ut_lo, 1)

            def low_v(r, kind, e):
                dve.wait_ge(v_hi, v_before(r, kind, e) + 1)
                nc.vector.tensor_tensor(vx[kind][e][1][:], v_sb[:], vx[kind][e][0][:].bitcast(F32),
                                        ALU.subtract).then_inc(v_lo, 1)

            def mul(r, kind, e, c, a):
                w = w_sb[kind][:, c * NW:(c + 1) * NW]
                dve.wait_ge(w_in[kind][c], (r * 2 + e + 1) * 16)
                nc.vector.tensor_tensor(w, w, a, ALU.mult).then_inc(a_mul[kind], 1)

            def low_w(r, kind, e, c):
                tok = slice(c * NW, (c + 1) * NW)
                dve.wait_ge(w_hi[kind], (r * 2 + e) * 3 + c + 1)
                nc.vector.tensor_tensor(wx[kind][e][1][:, tok], w_sb[kind][:, tok], wx[kind][e][0][:, tok].bitcast(F32),
                                        ALU.subtract).then_inc(w_lo[kind], 1)

            def prepare(new):
                for e in range(2):
                    for c in range(3):
                        if c >= 1:
                            low_u(new + e, 1 - e, c - 1)
                        dve.wait_ge(a_act, (new * 2 + e) * 3 + c + 1 + AACT0)
                        mul(new, NEW, e, c, a_sb[(3 * e + c) % 2][:])
                        if c == 1:
                            low_v(new, NEW, e)
                        low_w(new, NEW, e, c)

            def downs(i, kind):
                for o in range(OB):
                    m = (i * 2 + kind) * OB + o
                    out = acc_t[:, o // 3, (o % 3) * NW:(o % 3 + 1) * NW]
                    dve.wait_ge(o_done, m + 1 + ODONE0)
                    dve.wait_ge(o_added, m - OB + 1 + OADD0)
                    nc.vector.tensor_tensor(out, po[o % 3][:, 0:NW], out, ALU.add).then_inc(o_added, 1)
                    if kind == NEW:
                        e, c = o // 4 // 3, o // 4 % 3
                        if o % 4 == 0:
                            dve.wait_ge(old_in[c], (i * 2 + e + 1) * 16)
                            mul(i, OLD, e, c, old_sb[:, c * NW:(c + 1) * NW])
                        if o % 4 == 1:
                            low_w(i, OLD, e, c)
                        if o % 4 == 2 and c == 0:
                            low_v(i, OLD, e)

            def first():
                low_u(0, 0, 0)
                low_u(0, 0, 1)
                nc.vector.memset(acc_t[:], 0.0).then_inc(cleared, 1)
                dve.wait_ge(cleared, 1)

            rounds(dve, first, prepare, downs)


def finish(nc, final_norm, x2_tiles, acc_t, y_tiles):
    with ExitStack() as ctx:
        def sb(name, shape, dt=F32):
            return ctx.enter_context(nc.sbuf_tensor("fn_" + name, shape, dt))

        def sem(name):
            return new_sem(nc, "fn_" + name)

        gain = sb("gain", [P, D])
        x = [sb(f"x{t}", [P, D]) for t in range(NT)]
        sq = sb("sq", [P, D])
        ident = sb("ident", [P, P])
        ss, rinv, rstd = sb("ss", [P, NT]), sb("rinv", [P, NT]), sb("rstd", [P, NT])
        pt = [ctx.enter_context(nc.psum_tensor(f"fn_pt{b}", [P, W4], F32)) for b in range(4)]
        gain_loaded = sem("gain_loaded")
        x_loaded = [sem(f"x_loaded{t}") for t in range(NT)]
        zeroed, shaped = sem("zeroed"), sem("shaped")
        turned, added, summed, meaned, inverted, rooted, scaled, ready, stored = (sem(n) for n in (
            "turned", "added", "summed", "meaned", "inverted", "rooted", "scaled", "ready", "stored"))
        block = ctx.enter_context(nc.Block())

        @block.sync
        def _(sp):
            sp.dma_start(gain[:], final_norm.rearrange("(o d) -> o d", o=1).broadcast_to([P, D])).then_inc(gain_loaded, 16)
            for t in range(NT):
                sp.dma_start(x[t][0:rows(t)], x2_tiles[t]).then_inc(x_loaded[t], 16)
            for t in range(NT):
                sp.wait_ge(ready, t + 1)
                sp.dma_start(y_tiles[t], x[t][0:rows(t)]).then_inc(stored, 16)
            sp.wait_ge(stored, 16 * NT)

        @block.gpsimd
        def _(pool):
            nc.gpsimd.memset(ident[:], 0.0).then_inc(zeroed, 1)
            pool.wait_ge(zeroed, 1)
            nc.gpsimd.affine_select(out=ident[:], in_=ident[:], compare_op=ALU.not_equal, fill=1.0, base=0,
                                    pattern=[[-1, P]], channel_multiplier=1).then_inc(shaped, 1)

        @block.tensor
        def _(pe):
            pe.wait_ge(shaped, 1)
            for t in range(NT):
                r = rows(t)
                for half in range(2):
                    if t >= 2:
                        pe.wait_ge(added, 2 * (t - 2) + half + 1)
                    for k in range(4):
                        mm = nc.tensor.transpose(pt[2 * (t % 2) + half][0:r, k * P:(k + 1) * P],
                                                 acc_t[:, 4 * half + k, t * P:t * P + r], ident[:])
                    mm.then_inc(turned, 1)

        @block.scalar
        def _(act):
            def scale(t):
                r = rows(t)
                act.wait_ge(inverted, t + 1)
                nc.scalar.activation(rstd[0:r, t:t + 1], rinv[0:r, t:t + 1], ACT.Sqrt).then_inc(rooted, 1)
                act.wait_ge(rooted, t + 1)
                nc.scalar.activation(x[t][0:r], x[t][0:r], ACT.Copy, scale=rstd[0:r, t:t + 1]).then_inc(scaled, 1)

            for t in range(NT):
                r = rows(t)
                act.wait_ge(added, 2 * t + 2)
                if t >= 1:
                    act.wait_ge(summed, t)
                nc.scalar.activation(sq[0:r], x[t][0:r], ACT.Square, accum_out=ss[0:r, t:t + 1]).then_inc(summed, 1)
                if t >= 1:
                    scale(t - 1)
            scale(NT - 1)

        @block.vector
        def _(dve):
            dve.wait_ge(gain_loaded, 16)
            for t in range(NT + 2):
                if t < NT:
                    r = rows(t)
                    dve.wait_ge(x_loaded[t], 16)
                    for half in range(2):
                        dve.wait_ge(turned, 2 * t + half + 1)
                        xs = x[t][0:r, half * W4:(half + 1) * W4]
                        nc.vector.tensor_tensor(xs, xs, pt[2 * (t % 2) + half][0:r, :], ALU.add).then_inc(added, 1)
                if 1 <= t <= NT:
                    r = rows(t - 1)
                    dve.wait_ge(summed, t)
                    nc.vector.tensor_scalar(ss[0:r, t - 1:t], ss[0:r, t - 1:t], 1.0 / D, EPS, ALU.mult, ALU.add
                                            ).then_inc(meaned, 1)
                    dve.wait_ge(meaned, t)
                    nc.vector.reciprocal(rinv[0:r, t - 1:t], ss[0:r, t - 1:t]).then_inc(inverted, 1)
                if t >= 2:
                    r = rows(t - 2)
                    xs = x[t - 2][0:r]
                    dve.wait_ge(scaled, t - 1)
                    nc.vector.tensor_tensor(xs, xs, gain[0:r], ALU.mult).then_inc(ready, 1)


class Tables:

    def __init__(self, ctx, nc):
        def sb(name, shape):
            return ctx.enter_context(nc.sbuf_tensor("tab_" + name, shape, F32))

        self.cm = sb("cm", [P, GP, 2, 2, P])
        self.tp = sb("tp", [P, G, P])
        self.bm = sb("bm", [P, GP, 2, P])
        self.w = sb("w", [P, 2, GP, NM + 1])
        self.r8 = sb("r8", [P, GP])
        self.a4 = sb("a4", [P, 2, GP])


def mixers(nc, A, O, x_tiles, x2_tiles):
    with ExitStack() as ctx:
        o_t = ctx.enter_context(nc.sbuf_tensor("o_t", [P, KD, T], F32))
        u_sb = ctx.enter_context(nc.sbuf_tensor("u_sb", [P, G, SC, GCH], F32))
        us_nat = ctx.enter_context(nc.sbuf_tensor("us_nat", [TS, W4], F32))
        with ExitStack() as c2:
            def sb(name, shape):
                return c2.enter_context(nc.sbuf_tensor(name, shape, F32))

            qk_t = sb("qk_t", [P, 4, T])
            la_t = sb("la_t", [P, 2, T])
            v_sb = sb("v_sb", [P, NT, W4])
            g_sb = sb("g_sb", [P, NT, W4])
            fac = sb("fac", [P, 3, 2, SEQ // GC])
            fac_s = sb("fac_s", [P, 2, NSEQ])
            with nc.sbuf_tensor("h_t", [P, KD, T], F32) as h_t:
                norm_transpose(nc, "n1_", x_tiles, A["norm1"][0], h_t)
                project(nc, A["w_in"][0], A["w_a2"][0], A["b_a2"][0], h_t, qk_t, la_t, v_sb, g_sb, u_sb, us_nat)
            qz = sb("qz", [P, H, T])
            gla_decays(nc, qk_t, la_t, qz, fac, fac_s)
            gla(nc, qk_t, qz, v_sb, g_sb, fac, fac_s, A["gla_norm"][0], A["state_gla"][0], O[2][0, 0], O[5][0], o_t)
        with ExitStack() as c2:
            tab = Tables(c2, nc)
            s5_tables(nc, A, tab)
            x_g = c2.enter_context(nc.sbuf_tensor("x_g", [P, G, NMS], F32))
            s_all = c2.enter_context(nc.sbuf_tensor("s_all", [P, 2, GP, NM + 1], F32))
            s0 = c2.enter_context(nc.sbuf_tensor("s0", [P, 2, NSEQ, GP], F32))
            s5_scan(nc, A, tab, u_sb, us_nat, x_g, s_all, s0, O[3][0, 0], O[4][0, 0], O[6][0], O[7][0])
            s5_outputs(nc, A, tab, u_sb, x_g, s_all, s0, o_t)
        mix_out(nc, A["w_out"][0], o_t, x_tiles, x2_tiles)


def build(nc, A, O):
    def tiles(prompt, sample):
        return [prompt[0, t * P:(t + 1) * P, :] for t in range(NTP)] + [sample.rearrange("s j d -> (s j) d")]

    LIVE_SEMS.clear()
    x2_d = nc.dram_tensor("x2_d", [NT * P, D], F32).ap()
    w_d = nc.dram_tensor("w_d", [NK, 1 + NCH, NK, WCH], F32).ap()
    act_d = nc.dram_tensor("act_d", [NAHEAD, NK, T], F32).ap()
    x2_tiles = [x2_d[t * P:t * P + rows(t), :] for t in range(NT)]
    with nc.allow_non_contiguous_dma(reason="biases and S5 parameters, a few kilobytes"):
        mixers(nc, A, O, tiles(A["x_prompt"], A["x_sample"]), x2_tiles)
        clear_sems(nc)
        with ExitStack() as ctx:
            h_hi = ctx.enter_context(nc.sbuf_tensor("h_hi", [P, KD, T], F32R))
            h_lo = ctx.enter_context(nc.sbuf_tensor("h_lo", [P, KD, T], F32R))
            u_d, h = A["peer_u"][0], (h_hi, h_lo)
            with ExitStack() as c2:
                c_raw = c2.enter_context(ExitStack())
                raw = c_raw.enter_context(nc.sbuf_tensor("pq_raw", [P, KD, 2 * P], F32, side="right"))
                raw_loaded = new_sem(nc, "pq_raw_loaded")
                with nc.sbuf_tensor("h2_t", [P, KD, T], F32) as h_t:
                    norm_transpose(nc, "n2_", x2_tiles, A["norm2"][0], h_t,
                                   (raw[:], wq_block(A["peer_wq"][0], 0), raw_loaded))
                    split_h(nc, h_t, h_hi, h_lo)
                s_sb = c2.enter_context(nc.sbuf_tensor("s_sb", [P, NT, NU, NK], F32))
                peer_scores(nc, A["peer_wq"][0], A["peer_keys"][0], h_hi, h_lo, s_sb, raw, raw_loaded)
                c_raw.close()
                c_sel = ctx.enter_context(ExitStack())
                sel_t = c_sel.enter_context(nc.sbuf_tensor("sel_t", [P, 3, TPAD], F32, side="right"))
                peer_topk(nc, s_sb, sel_t, u_d, act_d, h)
            peer_gates(nc, sel_t, w_d, u_d, act_d, h)
            c_sel.close()
            acc_t = ctx.enter_context(nc.sbuf_tensor("acc_t", [P, KD, T], F32))
            peer_experts(nc, A["peer_u"][0], A["peer_v"][0], w_d, act_d, (h_hi, h_lo), acc_t)
            finish(nc, A["final_norm"], x2_tiles, acc_t, tiles(O[0], O[1]))


_INS = ['x_prompt', 'x_sample', 'state_gla', 'state_s5_re', 'state_s5_im', 'norm1', 'w_in', 'w_a2', 'b_a2', 'gla_norm',
        's5_lam_re', 's5_lam_im', 's5_log_dt', 's5_b_re', 's5_b_im', 's5_c_re', 's5_c_im', 's5_d', 'w_glu', 'b_glu',
        'w_out', 'norm2', 'peer_wq', 'peer_keys', 'peer_u', 'peer_v', 'final_norm']
_OUTS = [(1, SEQ, D), (NSEQ, SLEN, D), (1, 1, H, DK, DV), (1, 1, G, ST), (1, 1, G, ST),
         (1, NSEQ, H, DK, DV), (1, NSEQ, G, ST), (1, NSEQ, G, ST)]


def kernel(**inputs):
    import numpy as _np
    import concourse.bacc as _bacc
    from concourse.bass_utils import run_bass_kernel_spmd as _run

    nc = _bacc.Bacc("TRN2", target_bir_lowering=False, num_devices=1)
    arrays, args = {}, {}
    for name in _INS:
        a = _np.ascontiguousarray(inputs[name])
        arrays[f"in_{name}_dram"] = a
        args[name] = nc.dram_tensor(f"in_{name}_dram", a.shape, F32, kind="ExternalInput").ap()
    outs = [nc.dram_tensor(f"out_{i}_dram", shape, F32, kind="ExternalOutput").ap() for i, shape in enumerate(_OUTS)]
    build(nc, args, outs)
    r = _run(nc, [arrays], core_ids=[0])
    return tuple(r.results[0][f"out_{i}_dram"] for i in range(len(_OUTS)))
```
